# Optimizing a Trainium2 kernel written in Bass

```python
import math, functools
import jax, jax.numpy as jnp
from jax import lax
import numpy as np

D_MODEL = 1024
BATCH = 1
SEQ = 1024
DEPTH = 1
DEC_BATCH = 8
DEC_SEQ = 8
PAST_LEN = 4096
PAGE_SIZE = 128

HEAD_DIM = 64
MIX_WIDTH = D_MODEL
RWKV_WIDTH = MIX_WIDTH // 2
ATTN_WIDTH = MIX_WIDTH - RWKV_WIDTH
RWKV_HEADS = RWKV_WIDTH // HEAD_DIM
ATTN_HEADS = ATTN_WIDTH // HEAD_DIM
DECAY_LORA = 32
AAA_LORA = 32
GATE_LORA = 96
RWKV_PROJ = 3 * RWKV_WIDTH + DECAY_LORA + AAA_LORA + GATE_LORA
IN_PROJ = RWKV_PROJ + 3 * ATTN_WIDTH
DILATED = ((128, 1), (512, 4), (2048, 16))
WIN_MAX = 2048
ROPE_THETA = 10000.0
N_GROUPS = 4
EXPERTS_PER_GROUP = 8
N_EXPERTS = N_GROUPS * EXPERTS_PER_GROUP
TOP_K_INNER = 2
EXPERT_FF = 256
PLE_DIM = 256
RMS_EPS = 1e-6
LNX_EPS = 1e-5 * HEAD_DIM
NEG_INF = -1e30

kernel_name = 'hymba_rwkv7_dilated_hmoe_step'

def _rmsnorm(x, g):
    xf = x.astype(jnp.float32)
    y = xf * lax.rsqrt(jnp.mean(xf * xf, axis=-1, keepdims=True) + RMS_EPS)
    return (y * g.astype(jnp.float32)).astype(x.dtype)

def _rope(x, pos):
    half = HEAD_DIM // 2
    inv = jnp.power(ROPE_THETA, -jnp.arange(half, dtype=jnp.float32) * 2.0 / HEAD_DIM)
    ang = pos[:, None] * inv[None, :]
    cos = jnp.cos(ang)[None, :, None, :]
    sin = jnp.sin(ang)[None, :, None, :]
    xf = x.astype(jnp.float32)
    x1, x2 = xf[..., :half], xf[..., half:]
    return jnp.concatenate([x1 * cos - x2 * sin, x2 * cos + x1 * sin], axis=-1).astype(x.dtype)

def _branch_prompt(q, k, v, window, dil):
    B, S, H, E = q.shape
    L = window // dil
    unit = L * dil
    s_pad = -(-S // unit) * unit
    n = s_pad // unit

    def blocks(t):
        t = jnp.pad(t, ((0, 0), (0, s_pad - S), (0, 0), (0, 0)))
        return t.reshape(B, n, L, dil, H, E)

    def with_prev(t):
        prev = jnp.pad(t, ((0, 0), (1, 0), (0, 0), (0, 0), (0, 0), (0, 0)))[:, :-1]
        return jnp.concatenate([prev, t], axis=2)

    qb = blocks(q).astype(jnp.float32)
    kb = with_prev(blocks(k)).astype(jnp.float32)
    vb = with_prev(blocks(v)).astype(jnp.float32)
    s = jnp.einsum('bnidhe,bnjdhe->bndhij', qb, kb) / math.sqrt(E)
    i = jnp.arange(L)[:, None]
    j = jnp.arange(2 * L)[None, :]
    dist = i + L - j
    band = (dist >= 0) & (dist <= L)
    first = (jnp.arange(n)[:, None] * L + jnp.arange(2 * L)[None, :] - L) >= 0
    mask = band[None, :, :] & first[:, None, :]
    s = jnp.where(mask[None, :, None, None, :, :], s, NEG_INF)
    m = jnp.max(s, axis=-1, keepdims=True)
    e = jnp.exp(s - m)
    l = jnp.sum(e, axis=-1)
    o = jnp.einsum('bndhij,bnjdhe->bnidhe', e, vb)
    l_t = jnp.transpose(l, (0, 1, 4, 2, 3))
    m_t = jnp.transpose(m[..., 0], (0, 1, 4, 2, 3))
    o = (o / l_t[..., None]).reshape(B, s_pad, H, E)[:, :S]
    lse = (m_t + jnp.log(l_t)).reshape(B, s_pad, H)[:, :S]
    return o, lse

def _branch_decode(q, kc, vc, window, dil, wc):
    B, T, H, E = q.shape
    nk = window // dil + 1
    idx = wc + jnp.arange(T)[:, None] - jnp.arange(nk)[None, :] * dil
    valid = idx >= 0
    idxc = jnp.maximum(idx, 0)
    kg = kc[:, idxc].astype(jnp.float32)
    vg = vc[:, idxc].astype(jnp.float32)
    s = jnp.einsum('bthe,btkhe->bthk', q.astype(jnp.float32), kg) / math.sqrt(E)
    s = jnp.where(valid[None, :, None, :], s, NEG_INF)
    m = jnp.max(s, axis=-1, keepdims=True)
    e = jnp.exp(s - m)
    l = jnp.sum(e, axis=-1)
    o = jnp.einsum('bthk,btkhe->bthe', e, vg) / l[..., None]
    return o, m[..., 0] + jnp.log(l)

def _merge(outs, lses):
    w = jax.nn.softmax(jnp.stack(lses, axis=0), axis=0)
    return jnp.sum(w[..., None] * jnp.stack(outs, axis=0), axis=0)

def _dilated_prompt(q, k, v):
    outs, lses = [], []
    for window, dil in DILATED:
        o, l = _branch_prompt(q, k, v, window, dil)
        outs.append(o)
        lses.append(l)
    return _merge(outs, lses).astype(q.dtype)

def _dilated_decode(q, k, v, k_buf, v_buf):
    kc = jnp.concatenate([k_buf.astype(k.dtype), k], axis=1)
    vc = jnp.concatenate([v_buf.astype(v.dtype), v], axis=1)
    wc = k_buf.shape[1]
    outs, lses = [], []
    for window, dil in DILATED:
        o, l = _branch_decode(q, kc, vc, window, dil, wc)
        outs.append(o)
        lses.append(l)
    return _merge(outs, lses).astype(q.dtype)

def _wkv_step(S, inp):
    r_t, w_t, k_t, v_t, a_t, b_t = inp
    sa = jnp.einsum('bhvk,bhk->bhv', S, a_t)
    S = S * w_t[:, :, None, :] + sa[..., None] * b_t[:, :, None, :] + v_t[..., None] * k_t[:, :, None, :]
    y = jnp.einsum('bhvk,bhk->bhv', S, r_t)
    return S, y

def _rwkv7(P, shift_state, wkv_state, mu, w0, w2, a0, a2, g2, k_k, k_a, r_k, lnx_w, lnx_b):
    B, T, _ = P.shape
    H, E, C = RWKV_HEADS, HEAD_DIM, RWKV_WIDTH
    Pf = P.astype(jnp.float32)
    prev = jnp.concatenate([shift_state.astype(jnp.float32)[:, None], Pf[:, :-1]], axis=1)
    Pm = Pf + (prev - Pf) * mu
    r = Pm[..., :C]
    k = Pm[..., C:2 * C]
    v = Pm[..., 2 * C:3 * C]
    o = 3 * C
    xw = Pm[..., o:o + DECAY_LORA]
    o += DECAY_LORA
    xa = Pm[..., o:o + AAA_LORA]
    o += AAA_LORA
    xg = Pm[..., o:o + GATE_LORA]
    w = -jax.nn.softplus(-(w0 + jnp.tanh(xw) @ w2)) - 0.5
    decay = jnp.exp(-jnp.exp(w))
    a = jax.nn.sigmoid(a0 + xa @ a2)
    g = jax.nn.sigmoid(xg) @ g2
    kk = (k * k_k).reshape(B, T, H, E)
    kk = kk / jnp.maximum(jnp.sqrt(jnp.sum(kk * kk, axis=-1, keepdims=True)), 1e-12)
    k = k * (1.0 + (a - 1.0) * k_a)
    r_h = r.reshape(B, T, H, E)
    k_h = k.reshape(B, T, H, E)
    v_h = v.reshape(B, T, H, E)
    d_h = decay.reshape(B, T, H, E)
    a_h = a.reshape(B, T, H, E)
    xs = tuple(jnp.moveaxis(t, 1, 0) for t in (r_h, d_h, k_h, v_h, -kk, kk * a_h))
    S_fin, ys = lax.scan(_wkv_step, wkv_state.astype(jnp.float32), xs)
    y = jnp.moveaxis(ys, 0, 1)
    mean = jnp.mean(y, axis=-1, keepdims=True)
    var = jnp.mean(jnp.square(y - mean), axis=-1, keepdims=True)
    yn = (y - mean) * lax.rsqrt(var + LNX_EPS) * lnx_w.reshape(H, E) + lnx_b.reshape(H, E)
    bonus = jnp.sum(r_h * k_h * r_k, axis=-1, keepdims=True) * v_h
    out = ((yn + bonus).reshape(B, T, C) * g).astype(P.dtype)
    return out, P[:, -1], S_fin

def _hier_moe(u, rgw, rgb, rew, reb, ewg, ewu, ewd):
    B, T, D = u.shape
    x = u.reshape(B * T, D)
    lg = (x @ rgw).astype(jnp.float32) + rgb
    pg = jax.nn.softmax(lg, axis=-1)
    gsel = jnp.argmax(lg, axis=-1)
    pg_sel = jnp.take_along_axis(pg, gsel[:, None], axis=1)[:, 0]
    le = ((x @ rew).astype(jnp.float32) + reb).reshape(-1, N_GROUPS, EXPERTS_PER_GROUP)
    le_sel = jnp.take_along_axis(le, gsel[:, None, None], axis=1)[:, 0]
    pe = jax.nn.softmax(le_sel, axis=-1)
    top_p, top_i = lax.top_k(pe, TOP_K_INNER)
    wts = pg_sel[:, None] * top_p / jnp.sum(top_p, axis=-1, keepdims=True)
    eid = gsel[:, None] * EXPERTS_PER_GROUP + top_i
    gate = jnp.sum(jax.nn.one_hot(eid, N_EXPERTS, dtype=jnp.float32) * wts[..., None], axis=1)
    gate = gate.astype(x.dtype)
    y = jnp.zeros_like(x)
    for gi in range(N_GROUPS):
        sl = slice(gi * EXPERTS_PER_GROUP, (gi + 1) * EXPERTS_PER_GROUP)
        hg = jax.nn.silu(jnp.einsum('nd,edf->nef', x, ewg[sl])) * jnp.einsum('nd,edf->nef', x, ewu[sl])
        y = y + jnp.einsum('nef,efd->nd', hg * gate[:, sl, None], ewd[sl])
    return y.reshape(B, T, D)

def _layer(h, p, attend, pos, shift_state, wkv_state,
           norm_mix, w_in, mu_shift, decay_w0, decay_w2, iclr_a0, iclr_a2, gate_g2,
           k_k, k_a, r_k, lnx_w, lnx_b, attn_out_norm, w_out, norm_ffn,
           router_group_w, router_group_b, router_expert_w, router_expert_b,
           expert_w_gate, expert_w_up, expert_w_down, norm_ple, ple_gate_w, ple_proj):
    B, T, _ = h.shape
    u = _rmsnorm(h, norm_mix)
    proj = u @ w_in
    P = proj[..., :RWKV_PROJ]
    o = RWKV_PROJ
    q = proj[..., o:o + ATTN_WIDTH].reshape(B, T, ATTN_HEADS, HEAD_DIM)
    k = proj[..., o + ATTN_WIDTH:o + 2 * ATTN_WIDTH].reshape(B, T, ATTN_HEADS, HEAD_DIM)
    v = proj[..., o + 2 * ATTN_WIDTH:o + 3 * ATTN_WIDTH].reshape(B, T, ATTN_HEADS, HEAD_DIM)
    q = _rope(q, pos)
    k = _rope(k, pos)
    rw_out, new_shift, new_wkv = _rwkv7(P, shift_state, wkv_state, mu_shift, decay_w0, decay_w2,
                                        iclr_a0, iclr_a2, gate_g2, k_k, k_a, r_k, lnx_w, lnx_b)
    att = attend(q, k, v).reshape(B, T, ATTN_WIDTH)
    att = _rmsnorm(att, attn_out_norm)
    h = h + jnp.concatenate([rw_out, att], axis=-1) @ w_out
    h = h + _hier_moe(_rmsnorm(h, norm_ffn), router_group_w, router_group_b, router_expert_w,
                      router_expert_b, expert_w_gate, expert_w_up, expert_w_down)
    h = h + jax.nn.sigmoid(_rmsnorm(h, norm_ple) @ ple_gate_w) * (p @ ple_proj)
    return h, k, v, new_shift, new_wkv

def setup_inputs(seed: int = 0) -> dict:
    key = jax.random.key(seed)
    ks = iter(jax.random.split(key, 48))
    f32 = jnp.float32

    def nrm(shape, scale):
        return jax.random.normal(next(ks), shape, f32) * scale

    def gain(shape):
        return 1.0 + nrm(shape, 0.05)

    wc = min(WIN_MAX, PAST_LEN)
    d = {}
    d['x_prompt'] = nrm((BATCH, SEQ, D_MODEL), 1.0)
    d['x_sample'] = nrm((DEC_BATCH, DEC_SEQ, D_MODEL), 1.0)
    d['cache_k_win'] = nrm((DEPTH, DEC_BATCH, wc, ATTN_HEADS, HEAD_DIM), 1.0)
    d['cache_v_win'] = nrm((DEPTH, DEC_BATCH, wc, ATTN_HEADS, HEAD_DIM), 1.0)
    d['state_wkv'] = nrm((DEPTH, DEC_BATCH, RWKV_HEADS, HEAD_DIM, HEAD_DIM), 0.3)
    d['state_shift'] = nrm((DEPTH, DEC_BATCH, RWKV_PROJ), 1.0)
    d['p_prompt'] = nrm((DEPTH, BATCH, SEQ, PLE_DIM), 1.0)
    d['p_sample'] = nrm((DEPTH, DEC_BATCH, DEC_SEQ, PLE_DIM), 1.0)
    d['norm_mix'] = gain((DEPTH, D_MODEL))
    d['w_in'] = nrm((DEPTH, D_MODEL, IN_PROJ), D_MODEL ** -0.5)
    d['mu_shift'] = jax.random.uniform(next(ks), (DEPTH, RWKV_PROJ), f32)
    d['decay_w0'] = jax.random.uniform(next(ks), (DEPTH, RWKV_WIDTH), f32, -6.0, 1.0)
    d['decay_w2'] = nrm((DEPTH, DECAY_LORA, RWKV_WIDTH), 0.1)
    d['iclr_a0'] = nrm((DEPTH, RWKV_WIDTH), 0.1)
    d['iclr_a2'] = nrm((DEPTH, AAA_LORA, RWKV_WIDTH), 0.5 * AAA_LORA ** -0.5)
    d['gate_g2'] = nrm((DEPTH, GATE_LORA, RWKV_WIDTH), GATE_LORA ** -0.5)
    d['k_k'] = 0.85 + nrm((DEPTH, RWKV_WIDTH), 0.05)
    d['k_a'] = gain((DEPTH, RWKV_WIDTH))
    d['r_k'] = nrm((DEPTH, RWKV_HEADS, HEAD_DIM), 0.1)
    d['lnx_w'] = gain((DEPTH, RWKV_WIDTH))
    d['lnx_b'] = nrm((DEPTH, RWKV_WIDTH), 0.01)
    d['attn_out_norm'] = gain((DEPTH, ATTN_WIDTH))
    d['w_out'] = nrm((DEPTH, MIX_WIDTH, D_MODEL), MIX_WIDTH ** -0.5)
    d['norm_ffn'] = gain((DEPTH, D_MODEL))
    d['router_group_w'] = nrm((DEPTH, D_MODEL, N_GROUPS), D_MODEL ** -0.5)
    d['router_group_b'] = nrm((DEPTH, N_GROUPS), 0.01)
    d['router_expert_w'] = nrm((DEPTH, D_MODEL, N_EXPERTS), D_MODEL ** -0.5)
    d['router_expert_b'] = nrm((DEPTH, N_EXPERTS), 0.01)
    d['expert_w_gate'] = nrm((DEPTH, N_EXPERTS, D_MODEL, EXPERT_FF), D_MODEL ** -0.5)
    d['expert_w_up'] = nrm((DEPTH, N_EXPERTS, D_MODEL, EXPERT_FF), D_MODEL ** -0.5)
    d['expert_w_down'] = nrm((DEPTH, N_EXPERTS, EXPERT_FF, D_MODEL), EXPERT_FF ** -0.5)
    d['norm_ple'] = gain((DEPTH, D_MODEL))
    d['ple_gate_w'] = nrm((DEPTH, D_MODEL, D_MODEL), D_MODEL ** -0.5)
    d['ple_proj'] = nrm((DEPTH, PLE_DIM, D_MODEL), PLE_DIM ** -0.5)
    d['norm_final'] = gain((D_MODEL,))
    return d

def reference(x_prompt, x_sample, cache_k_win, cache_v_win, state_wkv, state_shift,
              p_prompt, p_sample, norm_mix, w_in, mu_shift, decay_w0, decay_w2, iclr_a0,
              iclr_a2, gate_g2, k_k, k_a, r_k, lnx_w, lnx_b, attn_out_norm, w_out, norm_ffn,
              router_group_w, router_group_b, router_expert_w, router_expert_b,
              expert_w_gate, expert_w_up, expert_w_down, norm_ple, ple_gate_w, ple_proj,
              norm_final):
    B, S, _ = x_prompt.shape
    DB, T, _ = x_sample.shape
    keep = min(WIN_MAX, S)
    pos_prompt = jnp.arange(S, dtype=jnp.float32)
    pos_sample = PAST_LEN + jnp.arange(T, dtype=jnp.float32)
    hp, hs = x_prompt, x_sample
    pk, pv, pw, psh, sk, sv, sw, ssh = [], [], [], [], [], [], [], []
    for i in range(DEPTH):
        lp = (norm_mix[i], w_in[i], mu_shift[i], decay_w0[i], decay_w2[i], iclr_a0[i], iclr_a2[i],
              gate_g2[i], k_k[i], k_a[i], r_k[i], lnx_w[i], lnx_b[i], attn_out_norm[i], w_out[i],
              norm_ffn[i], router_group_w[i], router_group_b[i], router_expert_w[i],
              router_expert_b[i], expert_w_gate[i], expert_w_up[i], expert_w_down[i],
              norm_ple[i], ple_gate_w[i], ple_proj[i])
        zero_shift = jnp.zeros((B, RWKV_PROJ), hp.dtype)
        zero_wkv = jnp.zeros((B, RWKV_HEADS, HEAD_DIM, HEAD_DIM), jnp.float32)
        hp, kp_, vp_, shp_, wkp_ = _layer(hp, p_prompt[i], _dilated_prompt, pos_prompt,
                                          zero_shift, zero_wkv, *lp)
        attend_s = functools.partial(_dilated_decode, k_buf=cache_k_win[i], v_buf=cache_v_win[i])
        hs, ks_, vs_, shs_, wks_ = _layer(hs, p_sample[i], attend_s, pos_sample,
                                          state_shift[i], state_wkv[i], *lp)
        pk.append(kp_[:, S - keep:])
        pv.append(vp_[:, S - keep:])
        pw.append(wkp_.astype(x_prompt.dtype))
        psh.append(shp_)
        sk.append(ks_)
        sv.append(vs_)
        sw.append(wks_.astype(state_wkv.dtype))
        ssh.append(shs_.astype(state_shift.dtype))
    y_prompt = _rmsnorm(hp, norm_final)
    y_sample = _rmsnorm(hs, norm_final)
    prompt_k_win = jnp.stack(pk, axis=0)
    prompt_v_win = jnp.stack(pv, axis=0)
    prompt_wkv = jnp.stack(pw, axis=0)
    prompt_shift = jnp.stack(psh, axis=0)
    sample_k_rows = jnp.stack(sk, axis=0)
    sample_v_rows = jnp.stack(sv, axis=0)
    sample_wkv = jnp.stack(sw, axis=0)
    sample_shift = jnp.stack(ssh, axis=0)
    return (y_prompt, y_sample, prompt_k_win, prompt_v_win, prompt_wkv, prompt_shift,
            sample_k_rows, sample_v_rows, sample_wkv, sample_shift)


_drawn_inputs = setup_inputs


def setup_inputs(seed=0):
    import zlib

    import numpy as np

    out = dict(_drawn_inputs(seed))
    spreads = {}
    factors = {'lnx_b': 5.22, 'router_group_b': 8.762, 'router_expert_b': 5.324, 'norm_ple': 7.793}
    for name, (base, spread) in spreads.items():
        noise = np.random.default_rng([zlib.crc32(name.encode()), seed]).standard_normal(out[name].shape)
        drawn = base * np.exp(spread * noise) if base else spread * noise
        out[name] = __import__('jax').numpy.asarray(drawn.astype(out[name].dtype))
    for name, factor in factors.items():
        out[name] = (out[name] * factor).astype(out[name].dtype)
    return out
```

```python
import numpy as np
import concourse.bass as bass
from concourse import mybir
from contextlib import ExitStack

D = 1024
KD = D // 128
S = 1024
NB, NT = 8, 8
TS = NB * NT
T = S + TS
CW = 64
NC = S // CW
NCH = NC + 1
H, E = 8, 64
RW = H * E
J = H // 2
LORA = 160
RP = 3 * RW + LORA
IP = RP + 3 * RW
TT = 9
CHUNKS = [(0, 512), (512, 512), (1024, 64)]
LOGC = float(np.exp(np.float64(-0.5)))
LNX_EPS = 1e-5 * E
RMS_EPS = 1e-6

f32 = mybir.dt.float32
i32 = mybir.dt.int32
ALU = mybir.AluOpType
ACT = mybir.ActivationFunctionType
AX = mybir.AxisListType

PC = {}
_at = 0
for _n, _k in (("norm_mix", 8), ("mu_r", 4), ("mu_k", 4), ("mu_v", 4), ("mu_wa", 1), ("mu_g", 1), ("w0", 4), ("a0", 4),
               ("k_k", 4), ("k_a", 4), ("r_k", 4), ("lnx_w", 4), ("lnx_b", 4), ("attn_norm", 4), ("norm_ffn", 8),
               ("norm_ple", 8)):
    PC[_n] = _at
    _at += _k
PCN = _at


def dyn(ap, i):
    return ap[:, bass.ds(i, 1)]


def project_tokens(nc, g):
    with ExitStack() as ctx:
        sq = ctx.enter_context(nc.sbuf_tensor("sq", [128, 2, T], f32))
        rstd = ctx.enter_context(nc.sbuf_tensor("rstd", [128, T], f32))
        sem = g.semaphores(nc, ctx)
        x_loaded = [sem(f"x_loaded{k}") for k in range(KD)]
        squared, summed, mean_ready, root_ready = sem("squared"), sem("summed"), sem("mean_ready"), sem("root_ready")
        g.clear(nc)
        with nc.Block() as block:
            @block.sync
            def _(sp):
                sp.dma_start(g.prm[:, :], g.d_prm).then_inc(g.s_const, 16)
                sp.dma_start(g.ones[:, :], g.d_ones).then_inc(g.s_const, 16)
                for k in range(KD):
                    sp.dma_start(g.uT[:, k, :], g.d_xT[k * 128:(k + 1) * 128, :]).then_inc(x_loaded[k], 16)
                for dst, src in g.constants:
                    sp.dma_start(dst, src).then_inc(g.s_const, 16)
                sp.wait_ge(g.s_const, 16 * (2 + len(g.constants)))

            @block.scalar
            def _(act):
                for k in range(KD):
                    act.wait_ge(x_loaded[k], 16)
                    if k >= 2:
                        act.wait_ge(summed, k - 1)
                    act.activation(sq[:, k % 2, :], g.uT[:, k, :], ACT.Square).then_inc(squared, 1)
                act.wait_ge(mean_ready, 1)
                act.activation(rstd[:, :], rstd[:, :], ACT.Sqrt).then_inc(root_ready, 1)

            @block.tensor
            def _(pe):
                pe.wait_ge(g.s_const, 32)
                for k in range(KD):
                    pe.wait_ge(squared, k + 1)
                    for n, (a, w) in enumerate(CHUNKS):
                        mm = pe.matmul(g.bank[n][:, 0:w], g.ones[:, :], sq[:, k % 2, a:a + w],
                                       start=(k == 0), stop=(k == KD - 1))
                    mm.then_inc(summed, 1)

            @block.vector
            def _(dve):
                dve.wait_ge(summed, KD)
                for n, (a, w) in enumerate(CHUNKS):
                    last = dve.tensor_scalar(rstd[:, a:a + w], g.bank[n][:, 0:w], 1.0 / D, RMS_EPS, ALU.mult, ALU.add)
                last.then_inc(mean_ready, 1)
                dve.wait_ge(root_ready, 1)
                dve.reciprocal(rstd[:, :], rstd[:, :])
                dve.drain()
                for k in range(KD):
                    c = PC["norm_mix"] + k
                    dve.scalar_tensor_tensor(out=g.uT[:, k, :], in0=g.uT[:, k, :], scalar=g.prm[:, c:c + 1],
                                             in1=rstd[:, :], op0=ALU.mult, op1=ALU.mult)


def token_shift(dve, raw, edge, ends, ends_ready, diff, out, mu, rows=128):
    rp, rs = raw[0:rows, 0:S + 1], raw[0:rows, S + 1:].rearrange("p (b t) -> p b t", b=NB)
    ds = diff[0:rows, S:T].rearrange("p (b t) -> p b t", b=NB)
    os_ = out[0:rows, S:T].rearrange("p (b t) -> p b t", b=NB)
    dve.tensor_copy(rs[:, :, 0:1], edge.unsqueeze(2))
    dve.tensor_copy(ends.unsqueeze(2), rs[:, :, NT:NT + 1]).then_inc(ends_ready, 1)
    dve.tensor_tensor(diff[0:rows, 0:S], rp[:, 0:S], rp[:, 1:S + 1], ALU.subtract)
    dve.drain()
    dve.tensor_tensor(ds, rs[:, :, 0:NT], rs[:, :, 1:NT + 1], ALU.subtract)
    dve.drain()
    dve.scalar_tensor_tensor(out=out[0:rows, 0:S], in0=diff[0:rows, 0:S], scalar=mu, in1=rp[:, 1:S + 1],
                             op0=ALU.mult, op1=ALU.add)
    return dve.scalar_tensor_tensor(out=os_, in0=ds, scalar=mu, in1=rs[:, :, 1:NT + 1], op0=ALU.mult, op1=ALU.add)


def raw_parts(raw, rows=128):
    rs = raw[0:rows, S + 1:].rearrange("p (b t) -> p b t", b=NB)
    return [raw[0:rows, 1:513], raw[0:rows, 513:1025], rs[:, :, 1:NT + 1]]


def psum_part(bank, n, rows=128):
    a, w = CHUNKS[n]
    ap = bank[0:rows, 0:w]
    return ap.rearrange("p (b t) -> p b t", b=NB) if n == 2 else ap


def lora_inputs(nc, g):
    with ExitStack() as ctx:
        sb = lambda n, s: ctx.enter_context(nc.sbuf_tensor(n, s, f32))
        sem = g.semaphores(nc, ctx)
        wl = sb("wl", [128, KD, LORA])
        raw = [sb("raw_wa", [64, T + 1 + NB]), sb("raw_g", [96, T + 1 + NB])]
        diff, mix = sb("ldiff", [96, T]), sb("lmix", [96, T])
        edge, ends = sb("ledge", [96, 2, NB]), sb("lends", [96, 2, NB])
        ready = sem("l_ready")
        loaded, edges, done, evac, mixed, used, outs = (sem(n) for n in (
            "l_loaded", "l_edges", "l_done", "l_evac", "l_mixed", "l_used", "l_outs"))
        rows = [64, 96]
        g.clear(nc)
        with nc.Block() as block:
            @block.sync
            def _(sp):
                sp.dma_start(wl[:, :, :], g.d_win.rearrange("(k p) n -> p k n", p=128)[:, :, 3 * RW:RP]).then_inc(loaded, 16)
                for i in range(2):
                    r0 = 3 * RW + 64 * i
                    sp.dma_start(edge[0:rows[i], i, :], g.d_shT[r0:r0 + rows[i], :]).then_inc(edges, 16)
                sp.wait_ge(evac, 6)
                sp.wait_ge(ready, 2)
                for i in range(2):
                    r0 = 3 * RW + 64 * i
                    sp.dma_start(g.o_pshift[r0:r0 + rows[i], :], raw[i][:, S:S + 1]).then_inc(outs, 16)
                    sp.dma_start(g.o_sshift[r0:r0 + rows[i], :], ends[0:rows[i], i, :]).then_inc(outs, 16)
                sp.wait_ge(outs, 64)

            @block.tensor
            def _(pe):
                pe.wait_ge(loaded, 16)
                for i in range(2):
                    for n, (a, w) in enumerate(CHUNKS):
                        for k in range(KD):
                            mm = pe.matmul(g.bank[3 * i + n][0:rows[i], 0:w], wl[:, k, 64 * i:64 * i + rows[i]],
                                           g.uT[:, k, a:a + w], start=(k == 0), stop=(k == KD - 1))
                        mm.then_inc(done, 1)

            @block.scalar
            def _(act):
                for i in range(2):
                    for n in range(3):
                        act.wait_ge(done, 3 * i + n + 1)
                        act.activation(raw_parts(raw[i], rows[i])[n], psum_part(g.bank[3 * i + n], n, rows[i]),
                                       ACT.Copy).then_inc(evac, 1)
                act.wait_ge(mixed, 1)
                act.activation(g.tw[0:32, :], mix[0:32, :], ACT.Tanh)
                act.activation(g.tw[32:64, :], mix[32:64, :], ACT.Copy).then_inc(used, 1)
                act.wait_ge(mixed, 2)
                act.activation(g.sg[:, :], mix[:, :], ACT.Sigmoid)

            @block.vector
            def _(dve):
                for i in range(2):
                    dve.memset(raw[i][:, 0:1], 0.0)
                dve.drain()
                dve.wait_ge(edges, 32)
                for i, name in enumerate(("mu_wa", "mu_g")):
                    dve.wait_ge(evac, 3 * i + 3)
                    if i:
                        dve.wait_ge(used, 1)
                    c = PC[name]
                    token_shift(dve, raw[i], edge[0:rows[i], i, :], ends[0:rows[i], i, :], ready, diff, mix, g.prm[0:rows[i], c:c + 1], rows[i]).then_inc(mixed, 1)
                    dve.drain()


def rwkv(nc, g):
    with ExitStack() as ctx:
        sb = lambda n, s: ctx.enter_context(nc.sbuf_tensor(n, s, f32))
        sem = g.semaphores(nc, ctx)
        w3 = sb("w3", [128, KD, 3, 128])
        wwa, wg2 = sb("wwa", [64, 128]), sb("wg2", [96, 128])
        raw = [sb(f"raw{i}", [128, T + 1 + NB]) for i in range(3)]
        edge, ends = sb("edge", [128, 3, NB]), sb("ends", [128, 3, NB])
        s0 = sb("s0", [128, NB, E])
        work = sb("work", [128, 4, T])
        kk, tmp, k, r = (work[:, i, :] for i in range(4))
        gm = work[:, :, :].rearrange("p a t -> p (a t)").rearrange("p (c h x) -> p c h x", c=NCH, h=2)
        v, dif = sb("v", [128, T]), sb("dif", [128, T])
        gate, dec, bon = sb("gate", [128, T]), sb("dec", [128, T]), sb("bon", [128, T])
        ar, bk = sb("ar", [128, NCH, 2, CW]), sb("bk", [128, NCH, 2, CW])
        rawc = [raw[i][:, 0:T].rearrange("p (c t) -> p c t", c=NCH) for i in range(2)]
        gain, gain_before, gain_inv = dec[:, :].rearrange("p (c t) -> p c t", c=NCH), rawc[0], rawc[1]
        alow, zb = rawc
        bv = dif[:, :].rearrange("p (c t) -> p c t", c=NCH)
        bkt = sb("bkt", [128, NCH, 2, E])
        uv = sb("uv", [128, NCH, 2, E])
        xa, xb = sb("xa", [128, NCH, CW]), sb("xb", [128, NCH, CW])
        st = sb("st", [128, 2, E])
        sdec, rhs = sb("sdec", [128, E]), sb("rhs", [128, E])
        w0s = sb("w0s", [128, 2, NB, NT])
        uvm = raw[2][:, 0:2 * NB * E].rearrange("p (h b e) -> p h b e", h=2, b=NB)
        sn = v[:, 0:NB * E].rearrange("p (b e) -> p b e", b=NB)
        bank = g.bank

        def flat(x):
            return x.rearrange("p c t -> p (c t)")

        names = ("w_loaded a_proj a_evac a_kk a_sq a_ss a_max a_root a_scan a_exp a_rkr a_bn a_done a_ends a_outs "
                 "b_job b_bv b_bvmm b_gm b_copy b_am b_amev b_z b_zev b_x b_xev b_t b_tev "
                 "c_rhs c_rhsev c_u c_uev c_uev1 c_s c_y c_sev c_yev c_w c_wev c_um c_outs d_in d_mean d_cen d_sq d_var d_eps d_root d_out").split()
        s = {n: sem(n) for n in names}

        g.clear(nc)
        with nc.Fori(0, J) as j:
            with nc.Block() as block:
                @block.gpsimd
                def _(pool):
                    for semaphore in s.values():
                        pool.sem_clear(semaphore)

            with nc.Block() as block:
                @block.sync
                def _(sp):
                    for i in range(3):
                        sp.dma_start(w3[:, :, i, :], g.d_win.rearrange("(k p) n -> p k n", p=128)[:, :, bass.ds(j * 128 + RW * i, 128)]).then_inc(s["w_loaded"], 16)
                    sp.dma_start(wwa[:, :], g.d_w2a2[:, bass.ds(j * 128, 128)]).then_inc(s["w_loaded"], 16)
                    sp.dma_start(wg2[:, :], g.d_g2[:, bass.ds(j * 128, 128)]).then_inc(s["w_loaded"], 16)
                    for i in range(3):
                        sp.dma_start(edge[:, i, :], g.d_shT[bass.ds(j * 128 + RW * i, 128), :]).then_inc(s["w_loaded"], 16)
                    sp.dma_start(s0[:, :, :].rearrange("p b v -> p (b v)"), g.d_stT[bass.ds(j * 128, 128), :]).then_inc(s["w_loaded"], 16)
                    sp.wait_ge(s["a_evac"], 9)
                    sp.wait_ge(s["a_ends"], 3)
                    for i in range(3):
                        sp.dma_start(g.o_pshift[bass.ds(j * 128 + RW * i, 128), :], raw[i][:, S:S + 1]).then_inc(s["a_outs"], 16)
                        sp.dma_start(g.o_sshift[bass.ds(j * 128 + RW * i, 128), :], ends[:, i, :]).then_inc(s["a_outs"], 16)
                    sp.wait_ge(s["a_outs"], 96)

                @block.tensor
                def _(pe):
                    pe.wait_ge(s["w_loaded"], 144)
                    job = 0
                    for q in range(6):
                        for n, (a, w) in enumerate(CHUNKS):
                            if job >= 6:
                                pe.wait_ge(s["a_evac"], job - 5)
                            out = bank[job % 6][:, 0:w]
                            if q < 3:
                                for kk in range(KD):
                                    mm = pe.matmul(out, w3[:, kk, q, :], g.uT[:, kk, a:a + w], start=(kk == 0), stop=(kk == KD - 1))
                            elif q == 3:
                                mm = pe.matmul(out, wwa[0:32, :], g.tw[0:32, a:a + w], start=True, stop=True)
                            elif q == 4:
                                mm = pe.matmul(out, wwa[32:64, :], g.tw[32:64, a:a + w], start=True, stop=True)
                            else:
                                mm = pe.matmul(out, wg2[:, :], g.sg[:, a:a + w], start=True, stop=True)
                            mm.then_inc(s["a_proj"], 1)
                            job += 1
                    pe.wait_ge(s["a_evac"], 18)
                    pe.wait_ge(s["a_sq"], 1)
                    for n, (a, w) in enumerate(CHUNKS):
                        pe.matmul(bank[n][:, 0:w], g.headones[:, :], dif[:, a:a + w], start=True, stop=True).then_inc(s["a_ss"], 1)
                    pe.wait_ge(s["a_rkr"], 1)
                    for n, (a, w) in enumerate(CHUNKS):
                        pe.matmul(bank[3 + n][:, 0:w], g.headones[:, :], tmp[:, a:a + w], start=True, stop=True).then_inc(s["a_bn"], 1)

                @block.scalar
                def _(act):
                    job = 0
                    dsts = [lambda n, i=i: raw_parts(raw[i])[n] for i in range(3)]
                    for q in range(6):
                        for n, (a, w) in enumerate(CHUNKS):
                            act.wait_ge(s["a_proj"], job + 1)
                            b = bank[job % 6][:, 0:w]
                            if q < 3:
                                act.activation(dsts[q](n), psum_part(bank[job % 6], n), ACT.Copy).then_inc(s["a_evac"], 1)
                            elif q == 3:
                                act.activation(dec[:, a:a + w], b, ACT.Sigmoid, bias=dyn(g.prm, j + PC["w0"])).then_inc(s["a_evac"], 1)
                            elif q == 4:
                                act.activation(bon[:, a:a + w], b, ACT.Sigmoid, bias=dyn(g.prm, j + PC["a0"])).then_inc(s["a_evac"], 1)
                            else:
                                act.activation(gate[:, a:a + w], b, ACT.Copy).then_inc(s["a_evac"], 1)
                            job += 1
                    act.wait_ge(s["a_kk"], 1)
                    act.activation(dif[:, :], kk, ACT.Square).then_inc(s["a_sq"], 1)
                    act.wait_ge(s["a_max"], 1)
                    act.activation(dif[:, :], dif[:, :], ACT.Sqrt).then_inc(s["a_root"], 1)
                    act.wait_ge(s["a_scan"], 1)
                    act.wait_ge(s["a_outs"], 96)
                    act.activation(gain, xa[:, :, :], ACT.Exp, scale=-LOGC)
                    act.activation(gain_before, xb[:, :, :], ACT.Exp, scale=-LOGC)
                    act.activation(gain_inv, xa[:, :, :], ACT.Exp, scale=LOGC).then_inc(s["a_exp"], 1)

                @block.vector
                def _(dve):
                    for i in range(3):
                        dve.memset(raw[i][:, 0:1], 0.0)
                    dve.drain()
                    dve.wait_ge(s["w_loaded"], 144)
                    for i, (name, out) in enumerate((("mu_k", k), ("mu_r", r), ("mu_v", v))):
                        q = {"mu_r": 0, "mu_k": 1, "mu_v": 2}[name]
                        dve.wait_ge(s["a_evac"], 3 * q + 3)
                        token_shift(dve, raw[q], edge[:, q, :], ends[:, q, :], s["a_ends"], dif, out, dyn(g.prm, j + PC[name]))
                        dve.drain()
                    dve.tensor_scalar(kk, k, dyn(g.prm, j + PC["k_k"]), None, ALU.mult).then_inc(s["a_kk"], 1)
                    dve.wait_ge(s["a_evac"], 12)
                    dve.tensor_tensor_scan(flat(xa[:, :, :]), g.keep[:, :], dec[:, :], 0.0, ALU.mult, ALU.add)
                    dve.drain()
                    dve.tensor_tensor(flat(xb[:, :, :]), flat(xa[:, :, :]), dec[:, :], ALU.subtract).then_inc(s["a_scan"], 1)
                    dve.wait_ge(s["a_evac"], 15)
                    dve.tensor_scalar(tmp, bon[:, :], -1.0, dyn(g.prm, j + PC["k_a"]), ALU.add, ALU.mult)
                    dve.drain()
                    dve.scalar_tensor_tensor(out=k, in0=tmp, scalar=1.0, in1=k, op0=ALU.add, op1=ALU.mult)
                    dve.drain()
                    dve.scalar_tensor_tensor(out=tmp, in0=r, scalar=dyn(g.prm, j + PC["r_k"]), in1=k,
                                             op0=ALU.mult, op1=ALU.mult).then_inc(s["a_rkr"], 1)
                    dve.wait_ge(s["a_ss"], 3)
                    for n, (a, w) in enumerate(CHUNKS):
                        last = dve.tensor_scalar(dif[:, a:a + w], bank[n][:, 0:w], 1e-24, None, ALU.max)
                    last.then_inc(s["a_max"], 1)
                    dve.wait_ge(s["a_root"], 1)
                    dve.reciprocal(dif[:, :], dif[:, :])
                    dve.drain()
                    dve.tensor_tensor(kk, kk, dif[:, :], ALU.mult)
                    dve.drain()
                    dve.wait_ge(s["a_exp"], 1)
                    c3 = lambda x: x.rearrange("p (c t) -> p c t", c=NCH)
                    dve.scalar_tensor_tensor(out=ar[:, :, 0, :], in0=c3(kk), scalar=-1.0, in1=gain_before, op0=ALU.mult, op1=ALU.mult)
                    dve.tensor_tensor(ar[:, :, 1, :], c3(r), gain, ALU.mult)
                    dve.tensor_tensor(dif[:, :], kk, bon[:, :], ALU.mult)
                    dve.drain()
                    dve.tensor_tensor(bk[:, :, 0, :], c3(dif[:, :]), gain_inv, ALU.mult)
                    dve.tensor_tensor(bk[:, :, 1, :], c3(k), gain_inv, ALU.mult)
                    dve.wait_ge(s["a_bn"], 3)
                    for n, (a, w) in enumerate(CHUNKS):
                        dve.tensor_tensor(bon[:, a:a + w], bank[3 + n][:, 0:w], v[:, a:a + w], ALU.mult)

            GC = [(0, 8), (8, 8), (16, 1)]

            with nc.Block() as block:
                jobs = [(kind, q, hh) for kind, n in (("gm", 5), ("bkt", 3), ("vt", 3)) for q in range(n) for hh in range(2)]
                NGM, NCP = 10, 12

                @block.tensor
                def _(pe):
                    hs = lambda hh: slice(64 * hh, 64 * hh + 64)
                    for n, (c0, m) in enumerate(GC):
                        for c in range(c0, c0 + m):
                            for hh in range(2):
                                o = (c - c0) * CW
                                pe.matmul(bank[n][hs(hh), o:o + CW], ar[hs(hh), c, 0, :], bk[hs(hh), c, 0, :], start=True, stop=True)
                                mm = pe.matmul(bank[3 + n][hs(hh), o:o + CW], bk[hs(hh), c, 0, :], ar[hs(hh), c, 0, :], start=True, stop=True)
                        mm.then_inc(s["b_am"], 1)
                    for i, (kind, q, hh) in enumerate(jobs):
                        if i >= 2:
                            if i - 2 < NGM:
                                pe.wait_ge(s["b_gm"], i - 1)
                            else:
                                pe.wait_ge(s["b_copy"], i - 1 - NGM)
                        b = bank[6 + hh]
                        per = 4 if kind == "gm" else 8
                        for c in range(per * q, min(per * q + per, NCH)):
                            p = c - per * q
                            if kind == "gm":
                                mm = pe.matmul(b[:, 128 * p:128 * p + 128], bk[hs(hh), c, :, :], ar[hs(hh), c, :, :], start=True, stop=True)
                            elif kind == "bkt":
                                mm = pe.matmul(b[:, 64 * p:64 * p + 64], bk[hs(hh), c, :, :], g.ident[hs(hh), hs(hh)], start=True, stop=True)
                            else:
                                mm = pe.matmul(b[64:128, 64 * p:64 * p + 64], v[hs(hh), c * CW:c * CW + CW], g.ident[hs(hh), hs(hh)], start=True, stop=True)
                        mm.then_inc(s["b_job"], 1)
                    for lv in range(5):
                        for n, (c0, m) in enumerate(GC):
                            pe.wait_ge(s["b_xev"], 3 * lv + n + 1)
                            if lv:
                                pe.wait_ge(s["b_tev"], 3 * (lv - 1) + n + 1)
                            for c in range(c0, c0 + m):
                                for hh in range(2):
                                    o = (c - c0) * CW
                                    mm = pe.matmul(bank[n][hs(hh), o:o + CW], alow[hs(hh), c, :], xa[hs(hh), c, :], start=True, stop=True)
                            mm.then_inc(s["b_z"], 1)
                        for n, (c0, m) in enumerate(GC):
                            pe.wait_ge(s["b_zev"], 3 * lv + n + 1)
                            for c in range(c0, c0 + m):
                                for hh in range(2):
                                    o = (c - c0) * CW
                                    mm = pe.matmul(bank[3 + n][hs(hh), o:o + CW], xb[hs(hh), c, :], zb[hs(hh), c, :], start=True, stop=True)
                            mm.then_inc(s["b_x"], 1)
                        if lv < 4:
                            for n, (c0, m) in enumerate(GC):
                                for c in range(c0, c0 + m):
                                    for hh in range(2):
                                        o = (c - c0) * CW
                                        mm = pe.matmul(bank[n][hs(hh), o:o + CW], zb[hs(hh), c, :], xb[hs(hh), c, :], start=True, stop=True)
                                mm.then_inc(s["b_t"], 1)

                    pe.wait_ge(s["b_gm"], NGM)
                    pe.wait_ge(s["b_copy"], NCP)
                    for n, (c0, m) in enumerate(GC):
                        if n == 2:
                            pe.wait_ge(s["b_bv"], 1)
                        for c in range(c0, c0 + m):
                            for hh in range(2):
                                o = (c - c0) * CW
                                mm = pe.matmul(bank[6 + n % 2][hs(hh), o:o + CW], gm[64:128, c, hh, 0:CW], uv[64:128, c, hh, :], start=True, stop=True)
                        mm.then_inc(s["b_bvmm"], 1)

                @block.scalar
                def _(act):
                    for i, (kind, q, hh) in enumerate(jobs):
                        if kind == "gm":
                            continue
                        act.wait_ge(s["b_job"], i + 1)
                        c0, c1 = 8 * q, min(8 * q + 8, NCH)
                        b = bank[6 + hh][:, 0:(c1 - c0) * 64].rearrange("p (c x) -> p c x", c=c1 - c0)
                        if kind == "bkt":
                            act.activation(bkt[:, c0:c1, hh, :], b, ACT.Copy).then_inc(s["b_copy"], 1)
                        else:
                            act.activation(uv[64:128, c0:c1, hh, :], b[64:128], ACT.Copy).then_inc(s["b_copy"], 1)
                    for n, (c0, m) in enumerate(GC):
                        act.wait_ge(s["b_bvmm"], n + 1)
                        act.activation(bv[:, c0:c0 + m, :], bank[6 + n % 2][:, 0:m * CW].rearrange("p (c x) -> p c x", c=m), ACT.Copy).then_inc(s["b_bv"], 1)

                @block.vector
                def _(dve):
                    def br(m, n):
                        return m.unsqueeze(1).broadcast_to([128, n, m.shape[-1]])

                    def b3(b, m):
                        return b[:, 0:m * CW].rearrange("p (c t) -> p c t", c=m)

                    for n, (c0, m) in enumerate(GC):
                        dve.wait_ge(s["b_am"], n + 1)
                        am = g.m_low[:, 0, :] if n < 2 else g.m_low[:, 1, :]
                        dve.tensor_tensor(alow[:, c0:c0 + m, :], b3(bank[n], m), br(am, m), ALU.mult)
                        dve.tensor_tensor(xb[:, c0:c0 + m, :], b3(bank[n], m), br(g.m_level[:, 5, :], m), ALU.mult)
                        dve.tensor_tensor(xa[:, c0:c0 + m, :], b3(bank[3 + n], m), br(g.m_level[:, 0, :], m), ALU.mult)
                        dve.drain()
                        dve.tensor_tensor(xb[:, c0:c0 + m, :], xb[:, c0:c0 + m, :], br(g.m_eye[:, :], m), ALU.add)
                        dve.tensor_tensor(xa[:, c0:c0 + m, :], xa[:, c0:c0 + m, :], br(g.m_eye[:, :], m), ALU.add).then_inc(s["b_xev"], 1)
                    for i, (kind, q, hh) in enumerate(jobs[:NGM]):
                        dve.wait_ge(s["b_job"], i + 1)
                        c0, c1 = 4 * q, min(4 * q + 4, NCH)
                        dve.tensor_tensor(gm[:, c0:c1, hh, :], bank[6 + hh][:, 0:128 * (c1 - c0)].rearrange("p (c x) -> p c x", c=c1 - c0),
                                          br(g.m_pair[:, 0 if c1 <= NC else 1, :], c1 - c0), ALU.mult).then_inc(s["b_gm"], 1)
                    for lv in range(5):
                        for n, (c0, m) in enumerate(GC):
                            dve.wait_ge(s["b_z"], 3 * lv + n + 1)
                            dve.tensor_tensor(zb[:, c0:c0 + m, :], b3(bank[n], m), br(g.m_level[:, lv + 1 if lv < 4 else 6, :], m), ALU.mult).then_inc(s["b_zev"], 1)
                        for n, (c0, m) in enumerate(GC):
                            dve.wait_ge(s["b_x"], 3 * lv + n + 1)
                            dve.tensor_tensor(xa[:, c0:c0 + m, :], xa[:, c0:c0 + m, :], b3(bank[3 + n], m), ALU.add).then_inc(s["b_xev"], 1)
                        if lv < 4:
                            for n, (c0, m) in enumerate(GC):
                                dve.wait_ge(s["b_t"], 3 * lv + n + 1)
                                dve.tensor_tensor(xb[:, c0:c0 + m, :], xb[:, c0:c0 + m, :], b3(bank[n], m), ALU.add).then_inc(s["b_tev"], 1)

            with nc.Block() as block:
                yT = xb
                hs = lambda hh: slice(64 * hh, 64 * hh + 64)

                @block.tensor
                def _(pe):
                    for b in range(NB):
                        for hh in range(2):
                            mm = pe.matmul(bank[7][hs(hh), 16 * b:16 * b + 16], s0[hs(hh), b, :],
                                           ar[hs(hh), NC, :, NT * b:NT * b + NT], start=True, stop=True)
                    mm.then_inc(s["c_w"], 1)
                    for c in range(NCH):
                        if c < NC:
                            pe.wait_ge(s["c_sev"], c + 1)
                        else:
                            pe.wait_ge(s["c_wev"], 1)
                        for hh in range(2):
                            o = bank[0][hs(hh), 0:E]
                            if c < NC:
                                mm = pe.matmul(o, ar[hs(hh), c, 0, :], st[hs(hh), c % 2, :], start=True, stop=True)
                            else:
                                mm = pe.matmul(o, w0s[hs(hh), 0, :, :], g.ident[hs(hh), hs(hh)], start=True, stop=True)
                        mm.then_inc(s["c_rhs"], 1)
                        pe.wait_ge(s["c_rhsev"], c + 1)
                        for hh in range(2):
                            mm = pe.matmul(bank[(1, 5)[hh]][0:64, 0:E], xa[hs(hh), c, :], rhs[hs(hh), :], start=True, stop=True)
                        mm.then_inc(s["c_u"], 1)
                        pe.wait_ge(s["c_uev"], c + 1)
                        pe.wait_ge(s["c_uev1"], c + 1)
                        if c < NC:
                            for hh in range(2):
                                mm = pe.matmul(bank[2][hs(hh), 0:E], bkt[:, c, hh, :], uv[:, c, hh, :], start=True, stop=True)
                            mm.then_inc(s["c_s"], 1)
                        o0 = (c % 8) * CW
                        yb = bank[3 + c // 8] if c < NC else bank[6]
                        for hh in range(2):
                            o = yb[hs(hh), o0:o0 + CW]
                            pe.matmul(o, uv[:, c, hh, :], gm[:, c, hh, CW:128], start=True, stop=False)
                            if c < NC:
                                mm = pe.matmul(o, st[hs(hh), c % 2, :], ar[hs(hh), c, 1, :], start=False, stop=True)
                            else:
                                mm = pe.matmul(o, g.ident[hs(hh), hs(hh)], w0s[hs(hh), 1, :, :], start=False, stop=True)
                        mm.then_inc(s["c_y"], 1)
                    pe.wait_ge(s["c_um"], 1)
                    for hh in range(2):
                        mm = pe.matmul(bank[7][hs(hh), :], bkt[:, NC, hh, :], uvm[:, hh, :, :], start=True, stop=True)
                    mm.then_inc(s["c_s"], 1)

                @block.scalar
                def _(act):
                    act.wait_ge(s["c_w"], 1)
                    act.activation(w0s[:, :, :, :].rearrange("p a b t -> p b a t"),
                                   bank[7][:, 0:128].rearrange("p (b a t) -> p b a t", b=NB, a=2), ACT.Copy).then_inc(s["c_wev"], 1)
                    for c in range(NCH):
                        act.wait_ge(s["c_u"], c + 1)
                        act.activation(uv[0:64, c, 0, :], bank[1][0:64, 0:E], ACT.Copy).then_inc(s["c_uev"], 1)
                        if c in (7, 15, 16):
                            act.wait_ge(s["c_y"], c + 1)
                            c0 = {7: 0, 15: 8, 16: 16}[c]
                            b = bank[{7: 3, 15: 4, 16: 6}[c]]
                            act.activation(flat(yT[:, c0:c + 1, :]), b[:, 0:(c + 1 - c0) * CW], ACT.Copy)

                @block.vector
                def _(dve):
                    gat = lambda c: gain[:, c, CW - 1:CW]
                    dve.memset(st[:, 0, :], 0.0).then_inc(s["c_sev"], 1)
                    dve.drain()
                    for c in range(NCH):
                        dve.wait_ge(s["c_rhs"], c + 1)
                        dve.tensor_tensor(rhs[:, :], bank[0][:, 0:E], bv[:, c, :], ALU.add).then_inc(s["c_rhsev"], 1)
                        if c < NC:
                            dve.tensor_scalar(sdec[:, :], st[:, c % 2, :], gat(c), None, ALU.mult)
                        dve.wait_ge(s["c_u"], c + 1)
                        dve.tensor_copy(uv[0:64, c, 1, :], bank[5][0:64, 0:E]).then_inc(s["c_uev1"], 1)
                        dve.drain()
                        if c == NC:
                            break
                        dve.wait_ge(s["c_s"], c + 1)
                        if c >= 1:
                            dve.wait_ge(s["c_y"], c)
                        dve.scalar_tensor_tensor(out=st[:, (c + 1) % 2, :], in0=bank[2][:, 0:E], scalar=gat(c), in1=sdec[:, :],
                                                 op0=ALU.mult, op1=ALU.add).then_inc(s["c_sev"], 1)
                        dve.drain()
                    dve.wait_ge(s["c_uev"], NCH)
                    for hh in range(2):
                        last = dve.tensor_tensor(uvm[:, hh, :, :], uv[:, NC, hh, :].unsqueeze(1).broadcast_to([128, NB, E]),
                                                 g.m_seq[:, :].unsqueeze(2).broadcast_to([128, NB, E]), ALU.mult)
                    last.then_inc(s["c_um"], 1)
                    dve.wait_ge(s["c_s"], NCH)
                    dve.tensor_tensor(sn[:, :, :], bank[7][:, :].rearrange("p (b e) -> p b e", b=NB), s0[:, :, :], ALU.add)
                    dve.drain()
                    gs = gain[:, NC, :].rearrange("p (b t) -> p b t", b=NB)[:, :, NT - 1:NT]
                    dve.tensor_tensor(sn[:, :, :], sn[:, :, :], gs.broadcast_to([128, NB, E]), ALU.mult).then_inc(s["d_in"], 1)

                @block.sync
                def _(sp):
                    sp.wait_ge(s["c_sev"], NCH)
                    sp.dma_start(g.o_pwkv[bass.ds(j * 128, 128), :], st[:, NC % 2, :]).then_inc(s["c_outs"], 16)
                    sp.wait_ge(s["d_in"], 1)
                    sp.dma_start(g.o_swkv[bass.ds(j * 128, 128), :], sn[:, :, :].rearrange("p b v -> p (b v)")).then_inc(s["c_outs"], 16)
                    sp.wait_ge(s["c_outs"], 32)

            with nc.Block() as block:
                y = flat(xb[:, :, :])
                cen, var = dif[:, :], work[:, 2, :]

                @block.tensor
                def _(pe):
                    for n, (a, w) in enumerate(CHUNKS):
                        pe.matmul(bank[n][:, 0:w], g.headones[:, :], y[:, a:a + w], start=True, stop=True).then_inc(s["d_mean"], 1)
                    pe.wait_ge(s["d_sq"], 1)
                    for n, (a, w) in enumerate(CHUNKS):
                        pe.matmul(bank[3 + n][:, 0:w], g.headones[:, :], tmp[:, a:a + w], start=True, stop=True).then_inc(s["d_var"], 1)

                @block.scalar
                def _(act):
                    act.wait_ge(s["d_cen"], 1)
                    act.activation(tmp, cen, ACT.Square).then_inc(s["d_sq"], 1)
                    act.wait_ge(s["d_eps"], 1)
                    act.activation(var, var, ACT.Sqrt).then_inc(s["d_root"], 1)

                @block.vector
                def _(dve):
                    for n, (a, w) in enumerate(CHUNKS):
                        dve.wait_ge(s["d_mean"], n + 1)
                        last = dve.scalar_tensor_tensor(out=cen[:, a:a + w], in0=bank[n][:, 0:w], scalar=-1.0 / E, in1=y[:, a:a + w],
                                                        op0=ALU.mult, op1=ALU.add)
                    last.then_inc(s["d_cen"], 1)
                    for n, (a, w) in enumerate(CHUNKS):
                        dve.wait_ge(s["d_var"], n + 1)
                        last = dve.tensor_scalar(var[:, a:a + w], bank[3 + n][:, 0:w], 1.0 / E, LNX_EPS, ALU.mult, ALU.add)
                    last.then_inc(s["d_eps"], 1)
                    dve.wait_ge(s["d_root"], 1)
                    dve.reciprocal(var, var)
                    dve.drain()
                    dve.tensor_tensor(cen, cen, var, ALU.mult)
                    dve.drain()
                    dve.tensor_scalar(cen, cen, dyn(g.prm, j + PC["lnx_w"]), dyn(g.prm, j + PC["lnx_b"]), ALU.mult, ALU.add)
                    dve.drain()
                    dve.tensor_tensor(cen, cen, bon[:, :], ALU.add)
                    dve.drain()
                    dve.tensor_tensor(g.rwT[:, bass.ds(j, 1), :].rearrange("p o t -> p (o t)"), cen, gate[:, :], ALU.mult)


SCALE = E ** -0.5
NSEL = 1280
KB = NSEL // 128


def attention(nc, g):
    with ExitStack() as ctx:
        sb = lambda n, s: ctx.enter_context(nc.sbuf_tensor(n, s, f32))
        sem = g.semaphores(nc, ctx)
        bank = g.bank
        cos, sin = sb("cos", [128, T]), sb("sin", [128, T])
        rot, count = sb("rot", [128, 128]), sb("count", [128, S])
        w3 = sb("wqkv", [128, KD, 3, 128])
        raw = [sb("qraw", [128, T]), sb("kraw", [128, T])]
        qz = [sb(f"qrot{hh}", [128, T]) for hh in range(2)]
        krot = sb("krot", [128, T])
        turned = sb("turned", [128, T])
        vt = sb("vt", [128, TT, 128])
        score = sb("score", [128, 2, S])
        pT = sb("pT", [128, 2, 8, 128])
        top = sb("top", [128, 4])
        ntop, total, rtotal = (sb(n, [128, 2]) for n in ("ntop", "total", "rtotal"))
        names = ("q_w q_mm q_ev q_rot q_done v_mm v_ev q_outs kept "
                 "s_qk s_neg s_exp s_tr s_tev0 s_tev1 s_pv s_norm").split()
        s = {n: sem(n) for n in names}
        tables = sem("tables")
        VJ = [(0, 4), (4, 4), (8, 1)]

        g.new += g.k_in
        g.clear(nc)
        with nc.Block() as block:
            @block.sync
            def _(sp):
                for dst, src in ((cos, g.d_cos), (sin, g.d_sin), (rot, g.d_rot), (count, g.d_count)):
                    sp.dma_start(dst[:, :], src).then_inc(tables, 16)
                for b in range(2):
                    sp.dma_start(g.kc[b][:, :, :], g.d_kcT[b].rearrange("(j p) n -> p j n", p=128)).then_inc(g.k_in[b], 16)
                sp.wait_ge(tables, 64)

            @block.vector
            def _(dve):
                for hh in range(2):
                    dve.memset(qz[hh][64 - 64 * hh:128 - 64 * hh, :], 0.0)

        with nc.Fori(0, J) as j:
            with nc.Block() as block:
                @block.gpsimd
                def _(pool):
                    for semaphore in s.values():
                        pool.sem_clear(semaphore)

            with nc.Block() as block:
                @block.sync
                def _(sp):
                    for i in range(3):
                        sp.dma_start(w3[:, :, i, :], g.d_win.rearrange("(k p) n -> p k n", p=128)
                                     [:, :, bass.ds(j * 128 + (RP + RW * i), 128)]).then_inc(s["q_w"], 16)
                    sp.wait_ge(s["q_done"], 2)
                    sp.dma_start(g.o_kT[bass.ds(j * 128, 128), :], krot[:, :]).then_inc(s["q_outs"], 16)
                    sp.wait_ge(s["v_ev"], 3)
                    sp.dma_start(g.o_v[0:S, :].rearrange("(t p) c -> p t c", p=128)[:, :, bass.ds(j * 128, 128)],
                                 vt[:, 0:8, :]).then_inc(s["q_outs"], 16)
                    sp.dma_start(g.o_v[S:T, bass.ds(j * 128, 128)], vt[0:64, 8, :]).then_inc(s["q_outs"], 16)
                    sp.wait_ge(s["q_outs"], 48)

                @block.tensor
                def _(pe):
                    pe.wait_ge(s["q_w"], 48)
                    for i in range(2):
                        for n, (a, w) in enumerate(CHUNKS):
                            for k in range(KD):
                                mm = pe.matmul(bank[3 * i + n][:, 0:w], w3[:, k, i, :], g.uT[:, k, a:a + w],
                                               start=(k == 0), stop=(k == KD - 1))
                            mm.then_inc(s["q_mm"], 1)
                    for n, (t0, m) in enumerate(VJ):
                        if n == 2:
                            pe.wait_ge(s["v_ev"], 1)
                        for t in range(t0, t0 + m):
                            rows = min(128, T - 128 * t)
                            for k in range(KD):
                                mm = pe.matmul(bank[6 + n % 2][0:rows, 128 * (t - t0):128 * (t - t0) + 128],
                                               g.uT[:, k, 128 * t:128 * t + rows], w3[:, k, 2, :], start=(k == 0), stop=(k == KD - 1))
                        mm.then_inc(s["v_mm"], 1)
                    for i in range(2):
                        for n, (a, w) in enumerate(CHUNKS):
                            pe.wait_ge(s["q_ev"], 3 * i + n + 1)
                            pe.matmul(bank[3 * i + n][:, 0:w], rot[:, :], raw[i][:, a:a + w], start=True, stop=True).then_inc(s["q_rot"], 1)

                @block.scalar
                def _(act):
                    for i in range(2):
                        for n, (a, w) in enumerate(CHUNKS):
                            act.wait_ge(s["q_mm"], 3 * i + n + 1)
                            act.activation(raw[i][:, a:a + w], bank[3 * i + n][:, 0:w], ACT.Copy).then_inc(s["q_ev"], 1)
                    for n, (t0, m) in enumerate(VJ):
                        act.wait_ge(s["v_mm"], n + 1)
                        rows = 128 if n < 2 else 64
                        act.activation(vt[0:rows, t0:t0 + m, :].rearrange("p t c -> p (t c)"), bank[6 + n % 2][0:rows, 0:128 * m],
                                       ACT.Copy).then_inc(s["v_ev"], 1)
                    act.drain()
                    act.activation(g.vs[0:TS, bass.ds(j, 1), :].rearrange("p o c -> p (o c)"), vt[0:64, 8, :], ACT.Copy)

                @block.vector
                def _(dve):
                    for i in range(2):
                        for n, (a, w) in enumerate(CHUNKS):
                            dve.wait_ge(s["q_rot"], 3 * i + n + 1)
                            dve.tensor_tensor(turned[:, a:a + w], bank[3 * i + n][:, 0:w], sin[:, a:a + w], ALU.mult)
                        dve.tensor_tensor(raw[i][:, :], raw[i][:, :], cos[:, :], ALU.mult)
                        dve.drain()
                        if i == 0:
                            for hh in range(2):
                                h = slice(64 * hh, 64 * hh + 64)
                                last = dve.tensor_tensor(qz[hh][h, :], raw[0][h, :], turned[h, :], ALU.add)
                            last.then_inc(s["q_done"], 1)
                            dve.drain()
                            for hh in range(2):
                                h = slice(64 * hh, 64 * hh + 64)
                                dve.tensor_copy(g.qs[h, bass.ds(j, 1), :].rearrange("p o c -> p (o c)"), qz[hh][h, S:T])
                        else:
                            dve.tensor_tensor(krot[:, :], raw[1][:, :], turned[:, :], ALU.add).then_inc(s["q_done"], 1)
                            dve.drain()
                            dve.tensor_copy(g.ks[:, bass.ds(j, 1), :].rearrange("p o c -> p (o c)"), krot[:, S:T])

            units = [(i, hh) for i in range(8) for hh in range(2)]
            groups = []
            for u, (i, hh) in enumerate(units):
                groups += [(u, 0, min(4, i + 1))] + ([(u, 4, i - 3)] if i >= 4 else [])
            of = [[x for x, gr in enumerate(groups) if gr[0] == u] for u in range(len(units))]
            last_by = lambda u, e: sum(1 for x in range(of[u][-1] + 1) if x % 2 == e)

            with nc.Block() as block:
                @block.tensor
                def _(pe):
                    def scores(u):
                        i, hh = units[u]
                        if u >= 2:
                            pe.wait_ge(s["s_neg"], u - 1)
                        for b in range(1 + (i >= 4)):
                            w = min(512, 128 * (i + 1) - 512 * b)
                            mm = pe.matmul(bank[2 * hh + b][:, 0:w], qz[hh][:, 128 * i:128 * i + 128], krot[:, 512 * b:512 * b + w],
                                           start=True, stop=True)
                        mm.then_inc(s["s_qk"], 1)

                    scores(0)
                    for u, (i, hh) in enumerate(units):
                        if u + 1 < len(units):
                            scores(u + 1)
                        pe.wait_ge(s["s_exp"], u + 1)
                        for x in of[u]:
                            if x >= 2:
                                pe.wait_ge(s[f"s_tev{x % 2}"], x // 2)
                            _, b0, m = groups[x]
                            for b in range(b0, b0 + m):
                                mm = pe.transpose(bank[4 + x % 2][:, 128 * (b - b0):128 * (b - b0) + 128],
                                                  score[:, u % 2, 128 * b:128 * b + 128], g.ident[:, :])
                            mm.then_inc(s["s_tr"], 1)
                        for e in range(2):
                            if last_by(u, e):
                                pe.wait_ge(s[f"s_tev{e}"], last_by(u, e))
                        if u >= 2:
                            pe.wait_ge(s["s_norm"], u - 1)
                        for b in range(i + 1):
                            mm = pe.matmul(bank[6 + u % 2][:, 0:128], pT[:, u % 2, b, :], vt[:, b, :],
                                           start=(b == 0), stop=(b == i))
                        mm.then_inc(s["s_pv"], 1)

                def evacuate(engine, x):
                    u, b0, m = groups[x]
                    engine.wait_ge(s["s_tr"], x + 1)
                    if u >= 2:
                        engine.wait_ge(s["s_pv"], u - 1)
                    out, in_ = pT[:, u % 2, b0:b0 + m, :].rearrange("p b q -> p (b q)"), bank[4 + x % 2][:, 0:128 * m]
                    if engine is nc.vector:
                        engine.tensor_copy(out, in_).then_inc(s["s_tev1"], 1)
                    else:
                        engine.activation(out, in_, ACT.Copy).then_inc(s["s_tev0"], 1)

                @block.scalar
                def _(act):
                    for u, (i, hh) in enumerate(units):
                        act.wait_ge(s["s_neg"], u + 1)
                        n = 128 * (i + 1)
                        act.activation(score[:, u % 2, 0:n], score[:, u % 2, 0:n], ACT.Exp, bias=ntop[:, u % 2:u % 2 + 1],
                                       accum_out=total[:, u % 2:u % 2 + 1]).then_inc(s["s_exp"], 1)
                        for x in of[u]:
                            if x % 2 == 0:
                                evacuate(nc.scalar, x)

                @block.vector
                def _(dve):
                    def soften(u):
                        i, hh = units[u]
                        dve.wait_ge(s["s_qk"], u + 1)
                        if u >= 2:
                            dve.wait_ge(s["s_tr"], of[u - 2][-1] + 1)
                        n = 128 * (i + 1)
                        for b in range(1 + (i >= 4)):
                            w = min(512, n - 512 * b)
                            acc = top[:, 2 * (u % 2) + b:2 * (u % 2) + b + 1]
                            dve.tensor_tensor_reduce(out=score[:, u % 2, 512 * b:512 * b + w], in0=bank[2 * hh + b][:, 0:w],
                                                     in1=count[:, S - n + 512 * b:S - n + 512 * b + w], scale=SCALE, scalar=-3e38,
                                                     op0=ALU.add, op1=ALU.max, accum_out=acc)
                        dve.drain()
                        if i >= 4:
                            dve.tensor_scalar(ntop[:, u % 2:u % 2 + 1], top[:, 2 * (u % 2):2 * (u % 2) + 1], top[:, 2 * (u % 2) + 1:2 * (u % 2) + 2], -1.0, ALU.max, ALU.mult).then_inc(s["s_neg"], 1)
                        else:
                            dve.tensor_scalar(ntop[:, u % 2:u % 2 + 1], top[:, 2 * (u % 2):2 * (u % 2) + 1], -1.0, None, ALU.mult).then_inc(s["s_neg"], 1)

                    def finish(u):
                        i, hh = units[u]
                        dve.wait_ge(s["s_exp"], u + 1)
                        dve.reciprocal(rtotal[:, u % 2:u % 2 + 1], total[:, u % 2:u % 2 + 1])
                        dve.drain()
                        dve.wait_ge(s["s_pv"], u + 1)
                        dve.tensor_scalar(g.att[:, i, bass.ds(j * 128 + 64 * hh, E)], bank[6 + u % 2][:, 64 * hh:64 * hh + 64],
                                          rtotal[:, u % 2:u % 2 + 1], None, ALU.mult).then_inc(s["s_norm"], 1)

                    soften(0)
                    for u in range(len(units)):
                        if u + 1 < len(units):
                            soften(u + 1)
                        for x in of[u]:
                            if x % 2:
                                evacuate(nc.vector, x)
                        finish(u)
                    dve.wait_ge(s["s_pv"], len(units))


def decode_attention(nc, g):
    with ExitStack() as ctx:
        sb = lambda n, s: ctx.enter_context(nc.sbuf_tensor(n, s, f32))
        sem = g.semaphores(nc, ctx)
        bank = g.bank
        HT = H * NT
        PAIRS = NB // 2
        OWN = NSEL
        CUTS = [(0, 512), (512, 512), (1024, NSEL - 1024)]
        TURNS = [(0, 4), (4, 4), (8, 3)]
        kc = g.kc + [g.h[:, :, :].rearrange("p t d -> p (t d)")[:, 0:J * NSEL].rearrange("p (j n) -> p j n", j=J)]
        NK = len(kc)
        vc = [sb(f"vc{i}", [128, KB, RW]) for i in range(2)]
        mcache, mnew = sb("mcache", [128, NSEL]), sb("mnew", [128, PAIRS, TS])
        heads, own_row = sb("own_head", [128, RW]), sb("own_row", [128, PAIRS, TS])
        qd = sb("qd", [128, J, NB, HT])
        score = [sb(f"dscore{i}", [128, NSEL + 128]) for i in range(2)]
        eT = sb("eT", [128, KB + 1, 128])
        top, ntop = sb("dtop", [128, 4]), sb("dntop", [128, 1])
        total, rtotal = sb("dtotal", [128, 2]), sb("drtotal", [128, 2])
        picked = sb("picked", [128, PAIRS, RW])
        k_in = g.k_in + [sem("k_in2")]
        v_in = [sem(f"v_in{i}") for i in range(2)]
        names = "masks_in qd_done scored raised exped turned0 turned1 turned2 tev valued picks summed"
        masks_in, qd_done, scored, raised, exped, turned0, turned1, turned2, tev, valued, picks, summed = (sem(n) for n in names.split())
        turned = [turned0, turned1, turned2]

        g.clear(nc)
        with nc.Block() as block:
            @block.sync
            def _(sp):
                sp.dma_start(mcache[:, :], g.d_mcache).then_inc(masks_in, 16)
                sp.dma_start(mnew[:, :, :], g.d_mnew).then_inc(masks_in, 16)
                sp.dma_start(heads[:, :], g.d_own_head).then_inc(masks_in, 16)
                sp.dma_start(own_row[:, :, :], g.d_own_row).then_inc(masks_in, 16)

                def keys(b):
                    if b >= NK:
                        sp.wait_ge(scored, b - NK + 1)
                    sp.dma_start(kc[b % NK][:, :, :], g.d_kcT[b].rearrange("(j p) n -> p j n", p=128)).then_inc(k_in[b % NK], 16)

                def values(b):
                    if b >= 2:
                        sp.wait_ge(valued, b - 1)
                    sp.dma_start(vc[b % 2][:, :, :], g.d_vc[b].rearrange("(k p) c -> p k c", p=128)).then_inc(v_in[b % 2], 16)

                keys(2)
                values(0)
                keys(3)
                values(1)
                for b in range(2, NB):
                    if b + 2 < NB:
                        keys(b + 2)
                    values(b)

            @block.tensor
            def _(pe):
                def scores(pair):
                    if pair >= 1:
                        pe.wait_ge(raised, pair)
                    for b in (2 * pair, 2 * pair + 1):
                        rows = slice(HT * (b % 2), HT * (b % 2) + HT)
                        pe.wait_ge(k_in[b % NK], 16 * (b // NK + 1))
                        for n, (a, w) in enumerate(CUTS):
                            for j in range(J):
                                pe.matmul(bank[n][rows, 0:w], qd[:, j, b, :], kc[b % NK][:, j, a:a + w], start=(j == 0), stop=(j == J - 1))
                        for j in range(J):
                            mm = pe.matmul(bank[2][rows, NSEL - 1024:NSEL - 1024 + TS], qd[:, j, b, :], g.ks[:, j, :],
                                           start=(j == 0), stop=(j == J - 1))
                        mm.then_inc(scored, 1)

                def turn(pair):
                    pe.wait_ge(exped, pair + 1)
                    if pair >= 1:
                        pe.wait_ge(tev, 3 * pair)
                    for n, (k0, m) in enumerate(TURNS):
                        for k in range(k0, k0 + m):
                            mm = pe.transpose(bank[3 + n][:, 128 * (k - k0):128 * (k - k0) + 128], score[pair % 2][:, 128 * k:128 * k + 128], g.ident[:, :])
                        mm.then_inc(turned[n], 1)

                def gather(pair):
                    pe.wait_ge(tev, 3 * pair + 3)
                    if pair >= 2:
                        pe.wait_ge(picks, pair - 1)
                    for b in (2 * pair, 2 * pair + 1):
                        rows = slice(HT * (b % 2), HT * (b % 2) + HT)
                        pe.wait_ge(v_in[b % 2], 16 * (b // 2 + 1))
                        for k in range(KB):
                            pe.matmul(bank[6 + pair % 2][rows, :], eT[:, k, rows], vc[b % 2][:, k, :], start=(k == 0), stop=False)
                        pe.matmul(bank[6 + pair % 2][rows, :], eT[:, KB, rows], g.vs[:, :, :].rearrange("p j c -> p (j c)"),
                                  start=False, stop=True).then_inc(valued, 1)

                pe.wait_ge(qd_done, 1)
                scores(0)
                turn(0)
                for pair in range(PAIRS):
                    if pair + 1 < PAIRS:
                        scores(pair + 1)
                    gather(pair)
                    if pair + 1 < PAIRS:
                        turn(pair + 1)
                pe.wait_ge(masks_in, 64)
                for pair in range(PAIRS):
                    pe.wait_ge(picks, pair + 1)
                    mm = pe.matmul(bank[0][0:TS, :], own_row[:, pair, :], picked[:, pair, :], start=(pair == 0), stop=(pair == PAIRS - 1))
                mm.then_inc(summed, 1)

            @block.scalar
            def _(act):
                for pair in range(PAIRS):
                    act.wait_ge(raised, pair + 1)
                    act.activation(score[pair % 2][:, 0:NSEL + TS], score[pair % 2][:, 0:NSEL + TS], ACT.Exp, bias=ntop[:, 0:1],
                                   accum_out=total[:, pair % 2:pair % 2 + 1]).then_inc(exped, 1)
                    if pair >= 1:
                        act.wait_ge(valued, 2 * pair)
                    for n, (k0, m) in enumerate(TURNS):
                        act.wait_ge(turned[n], pair + 1)
                        act.activation(eT[:, k0:k0 + m, :].rearrange("p k q -> p (k q)"), bank[3 + n][:, 0:128 * m], ACT.Copy).then_inc(tev, 1)

            @block.vector
            def _(dve):
                dve.memset(g.att[:, TT - 1, :], 0.0)
                dve.memset(g.vs[TS:128, :, :], 0.0)
                for i in range(2):
                    dve.memset(score[i][:, NSEL + TS:NSEL + 128], 0.0)
                dve.memset(qd[:, :, :, :], 0.0)
                dve.drain()
                for hh in range(2):
                    h = slice(64 * hh, 64 * hh + 64)
                    for j in range(J):
                        o = NT * (2 * j + hh)
                        last = dve.tensor_copy(qd[h, j, :, o:o + NT], g.qs[h, j, :].rearrange("p (b t) -> p b t", b=NB))
                last.then_inc(qd_done, 1)
                dve.wait_ge(masks_in, 64)

                def soften(pair):
                    dve.wait_ge(scored, 2 * pair + 2)
                    if pair >= 1:
                        dve.wait_ge(exped, pair)
                    if pair >= 2:
                        dve.wait_ge(turned2, pair - 1)
                    parts = [(a, w, bank[n][:, 0:w], mcache[:, a:a + w]) for n, (a, w) in enumerate(CUTS)]
                    parts.append((OWN, TS, bank[2][:, NSEL - 1024:NSEL - 1024 + TS], mnew[:, pair, :]))
                    for n, (a, w, in0, in1) in enumerate(parts):
                        dve.tensor_tensor_reduce(out=score[pair % 2][:, a:a + w], in0=in0, in1=in1, scale=SCALE, scalar=-3e38,
                                                 op0=ALU.add, op1=ALU.max, accum_out=top[:, n:n + 1])
                    dve.drain()
                    dve.tensor_reduce(ntop[:, :], top[:, :], AX.X, ALU.max)
                    dve.drain()
                    dve.tensor_scalar(ntop[:, :], ntop[:, :], -1.0, None, ALU.mult).then_inc(raised, 1)

                def pick(pair):
                    dve.wait_ge(exped, pair + 1)
                    dve.reciprocal(rtotal[:, pair % 2:pair % 2 + 1], total[:, pair % 2:pair % 2 + 1])
                    dve.drain()
                    dve.wait_ge(valued, 2 * pair + 2)
                    dve.scalar_tensor_tensor(out=picked[:, pair, :], in0=bank[6 + pair % 2][:, :], scalar=rtotal[:, pair % 2:pair % 2 + 1],
                                             in1=heads[:, :], op0=ALU.mult, op1=ALU.mult).then_inc(picks, 1)

                soften(0)
                for pair in range(PAIRS):
                    if pair + 1 < PAIRS:
                        soften(pair + 1)
                    pick(pair)
                dve.wait_ge(summed, 1)
                dve.tensor_copy(g.att[0:TS, TT - 1, :], bank[0][0:TS, :])


G, EPG, NE, FF = 4, 8, 32, 256
CAP = 128
PASSES = -(-T // CAP)
SLOTS = PASSES * NE * CAP
BIG = 1e30


def rows_of(t):
    return min(128, T - 128 * t)


def out_projection(nc, g):
    with ExitStack() as ctx:
        sb = lambda n, s: ctx.enter_context(nc.sbuf_tensor(n, s, f32))
        sem = g.semaphores(nc, ctx)
        bank = g.bank
        wo = sb("wo", [128, KD, D])
        attT = sb("attT", [128, J, T])
        junk = sb("ojunk", [128, RW])
        ss, rstd = sb("oss", [128, TT]), sb("orstd", [128, TT])
        x_in, w_in, squared, meaned, rooted, scaled, turned, evac, projected, added = (
            sem("o_" + n) for n in "x w squared meaned rooted scaled turned evac projected added".split())
        g.clear(nc)
        with nc.Block() as block:
            @block.sync
            def _(sp):
                for k in range(KD):
                    sp.dma_start(wo[:, k, :], g.d_wout[128 * k:128 * k + 128, :]).then_inc(w_in, 16)
                sp.dma_start(g.h[:, 0:8, :], g.d_x[0:S, :].rearrange("(t p) d -> p t d", p=128)).then_inc(x_in, 16)
                sp.dma_start(g.h[0:TS, 8, :], g.d_x[S:T, :]).then_inc(x_in, 16)

            @block.gpsimd
            def _(pool):
                pool.memset(g.h[64:128, TT - 1, :], 0.0)

            @block.scalar
            def _(act):
                for t in range(TT):
                    last = act.activation(junk[:, :], g.att[:, t, :], ACT.Square, accum_out=ss[:, t:t + 1])
                    act.drain()
                last.then_inc(squared, 1)
                act.wait_ge(meaned, 1)
                act.activation(rstd[:, :], rstd[:, :], ACT.Sqrt).then_inc(rooted, 1)

            @block.vector
            def _(dve):
                dve.wait_ge(squared, 1)
                dve.tensor_scalar(rstd[:, :], ss[:, :], 1.0 / RW, RMS_EPS, ALU.mult, ALU.add).then_inc(meaned, 1)
                dve.wait_ge(rooted, 1)
                dve.reciprocal(rstd[:, :], rstd[:, :])
                dve.drain()
                for t in range(TT):
                    dve.tensor_scalar(g.att[:, t, :], g.att[:, t, :], rstd[:, t:t + 1], None, ALU.mult).then_inc(scaled, 1)
                c = PC["attn_norm"]
                for t in range(TT):
                    r = rows_of(t)
                    dve.wait_ge(turned, t + 1)
                    dve.tensor_tensor(attT[:, :, 128 * t:128 * t + r], bank[t % 2][:, :].rearrange("p (j q) -> p j q", j=J)[:, :, 0:r],
                                      g.prm[:, c:c + J].unsqueeze(2).broadcast_to([128, J, r]), ALU.mult).then_inc(evac, 1)
                dve.wait_ge(x_in, 32)
                for t in range(TT):
                    r = rows_of(t)
                    dve.wait_ge(projected, t + 1)
                    for i in range(2):
                        last = dve.tensor_tensor(g.h[0:r, t, 512 * i:512 * i + 512], g.h[0:r, t, 512 * i:512 * i + 512],
                                                 bank[2 + 2 * (t % 3) + i][0:r, :], ALU.add)
                    last.then_inc(added, 1)

            @block.tensor
            def _(pe):
                for t in range(TT):
                    pe.wait_ge(scaled, t + 1)
                    if t >= 2:
                        pe.wait_ge(evac, t - 1)
                    for j in range(J):
                        mm = pe.transpose(bank[t % 2][:, 128 * j:128 * j + 128], g.att[:, t, 128 * j:128 * j + 128], g.ident[:, :])
                    mm.then_inc(turned, 1)
                pe.wait_ge(w_in, 16 * KD)
                pe.wait_ge(evac, TT)
                for t in range(TT):
                    r = rows_of(t)
                    if t >= 3:
                        pe.wait_ge(added, t - 2)
                    for i in range(2):
                        for k in range(KD):
                            lhs = (g.rwT if k < J else attT)[:, k % J, 128 * t:128 * t + r]
                            mm = pe.matmul(bank[2 + 2 * (t % 3) + i][0:r, :], lhs, wo[:, k, 512 * i:512 * i + 512],
                                           start=(k == 0), stop=(k == KD - 1))
                    mm.then_inc(projected, 1)


def norm_scales(nc, g, name, rstd, junk):
    with ExitStack() as ctx:
        sem = g.semaphores(nc, ctx)
        squared, meaned, rooted = (sem(name + n) for n in ("_sq", "_mn", "_rt"))
        g.clear(nc)
        with nc.Block() as block:
            @block.scalar
            def _(act):
                for t in range(TT):
                    last = act.activation(junk[:, :], g.h[:, t, :], ACT.Square, accum_out=rstd[:, t:t + 1])
                    act.drain()
                last.then_inc(squared, 1)
                act.wait_ge(meaned, 1)
                act.activation(rstd[:, :], rstd[:, :], ACT.Sqrt).then_inc(rooted, 1)

            @block.vector
            def _(dve):
                dve.wait_ge(squared, 1)
                dve.tensor_scalar(rstd[:, :], rstd[:, :], 1.0 / D, RMS_EPS, ALU.mult, ALU.add).then_inc(meaned, 1)
                dve.wait_ge(rooted, 1)
                dve.reciprocal(rstd[:, :], rstd[:, :])


def route(nc, g):
    with ExitStack() as ctx:
        sb = lambda n, s, d=f32: ctx.enter_context(nc.sbuf_tensor(n, s, d))
        sem = g.semaphores(nc, ctx)
        bank = g.bank
        rstd, junk = sb("rrstd", [128, TT]), sb("rjunk", [128, D])
        norm_scales(nc, g, "ffn", rstd, junk)
        gain = sb("ffn_gain", [128, D])
        wr, br = sb("wr", [128, KD, G + NE]), sb("br", [128, G + NE])
        xn = sb("xn", [128, 2, D])
        xnT = sb("xnT", [128, 2, KD, 128])
        lg = sb("lg", [128, TT, G + NE])
        upper = sb("upper", [128, 128])
        valid, pad_a = sb("valid", [128, TT]), sb("pad_a", [128, 2, TT])
        w4, w32, i32t = sb("w4", [128, G]), sb("w32", [128, NE]), sb("i32t", [128, NE])
        tok = sb("tok", [128, TT], i32)
        zero = sb("zeros", [128, PASSES * NE + 2], i32)
        consts, xnorm, stored, turned, evac, logits, lev, zeroed, zero_in = (
            sem("r_" + n) for n in "consts xnorm stored turned evac logits lev zeroed zero_in".split())
        stored = [stored, sem("r_stored1")]
        g.clear(nc)
        with nc.Block() as block:
            @block.sync
            def _(sp):
                loads = ((gain, g.d_ffn_gain), (wr, g.d_wr), (br, g.d_br), (upper, g.d_upper), (valid, g.d_valid),
                         (pad_a, g.d_pad_a), (w4, g.d_w4), (w32, g.d_w32), (i32t, g.d_i32t), (tok, g.d_tok))
                for dst, src in loads:
                    sp.dma_start(dst[tuple([slice(None)] * len(dst.shape))], src).then_inc(consts, 16)
                sp.wait_ge(zeroed, 1)
                sp.dma_start(g.table[0:SLOTS + 256, :].rearrange("(p n) o -> p (n o)", p=128), zero[:, :]).then_inc(zero_in, 16)
                for t in range(TT):
                    sp.wait_ge(xnorm, t + 1)
                    sp.dma_start(g.xn[128 * t:128 * t + 128, :], xn[:, t % 2, :]).then_inc(stored[t % 2], 16)
                sp.wait_ge(stored[0], 16 * (TT - TT // 2))
                sp.wait_ge(stored[1], 16 * (TT // 2))
                sp.wait_ge(zero_in, 16)
                sp.wait_ge(consts, 16 * len(loads))

            @block.gpsimd
            def _(pool):
                pool.memset(zero[:, :], 0).then_inc(zeroed, 1)

            @block.vector
            def _(dve):
                dve.wait_ge(consts, 160)
                for t in range(TT):
                    if t >= 2:
                        dve.wait_ge(stored[t % 2], 16 * (t // 2))
                        dve.wait_ge(turned, t - 1)
                    dve.scalar_tensor_tensor(out=xn[:, t % 2, :], in0=g.h[:, t, :], scalar=rstd[:, t:t + 1], in1=gain[:, :],
                                             op0=ALU.mult, op1=ALU.mult).then_inc(xnorm, 1)
                    if t >= 1:
                        dve.wait_ge(logits, t)
                        dve.tensor_tensor(lg[:, t - 1, :], bank[4 + (t - 1) % 2][:, 0:G + NE], br[:, :], ALU.add).then_inc(lev, 1)
                dve.wait_ge(logits, TT)
                dve.tensor_tensor(lg[:, TT - 1, :], bank[4 + (TT - 1) % 2][:, 0:G + NE], br[:, :], ALU.add).then_inc(lev, 1)

            @block.tensor
            def _(pe):
                pe.wait_ge(consts, 160)
                for t in range(TT):
                    pe.wait_ge(xnorm, t + 1)
                    if t >= 2:
                        pe.wait_ge(evac, t - 1)
                        pe.wait_ge(lev, t - 1)
                    for k in range(KD):
                        mm = pe.transpose(bank[2 * (t % 2) + k // 4][:, 128 * (k % 4):128 * (k % 4) + 128],
                                          xn[:, t % 2, 128 * k:128 * k + 128], g.ident[:, :])
                    mm.then_inc(turned, 1)
                    pe.wait_ge(evac, t + 1)
                    for k in range(KD):
                        mm = pe.matmul(bank[4 + t % 2][:, 0:G + NE], xnT[:, t % 2, k, :], wr[:, k, :], start=(k == 0), stop=(k == KD - 1))
                    mm.then_inc(logits, 1)

            @block.scalar
            def _(act):
                for t in range(TT):
                    act.wait_ge(turned, t + 1)
                    if t >= 2:
                        act.wait_ge(logits, t - 1)
                    for i in range(2):
                        last = act.activation(xnT[:, t % 2, 4 * i:4 * i + 4, :].rearrange("p k q -> p (k q)"), bank[2 * (t % 2) + i][:, :], ACT.Copy)
                    last.then_inc(evac, 1)

        mx, v4, sel = sb("mx", [128, TT]), sb("v4", [128, TT, G]), sb("sel", [128, TT, G])
        le, v32 = sb("le", [128, TT, NE]), sb("v32", [128, TT, NE])
        oh = [sb(f"oh{k}", [128, TT, NE]) for k in range(2)]
        m2 = sb("m2", [128, 2, TT])
        cnt, pre = sb("cnt", [128, TT, NE]), sb("pre", [128, TT + 1, NE])
        eid, pos, over, t1, t2 = (sb(n, [128, TT]) for n in ("eid", "pos", "over", "rt1", "rt2"))
        most = sb("most", [128, 1])
        ga, gb, gc, counted, ranked, placed, scat = (sem("r2_" + n) for n in "a b c counted ranked placed scat".split())
        pg, dl = sb("pg", [128, TT]), sb("dl", [128, TT])
        eg = sb("eg", [128, TT, G])
        g.clear(nc)
        with nc.Block() as block:
            @block.vector
            def _(dve):
                def op(ins):
                    dve.drain()

                def bt(x, n):
                    return x.unsqueeze(2).broadcast_to([128, TT, n])

                def bc(x, n):
                    return x.unsqueeze(1).broadcast_to([128, TT, n])
                g4, e32 = lg[:, :, 0:G], lg[:, :, G:G + NE]
                op(dve.tensor_reduce(mx[:, :], g4, AX.X, ALU.max))
                dve.tensor_tensor(eg[:, :, :], g4, bt(mx[:, :], G), ALU.subtract).then_inc(ga, 1)
                op(dve.tensor_tensor(v4[:, :, :], g4, bt(mx[:, :], G), ALU.is_equal))
                op(dve.tensor_tensor(v4[:, :, :], v4[:, :, :], bc(w4[:, :], G), ALU.mult))
                op(dve.tensor_reduce(mx[:, :], v4[:, :, :], AX.X, ALU.max))
                op(dve.tensor_tensor(sel[:, :, :], v4[:, :, :], bt(mx[:, :], G), ALU.is_equal))
                op(dve.tensor_scalar(sel[:, :, :], sel[:, :, :], -1.0, 3 * BIG, ALU.add, ALU.mult))
                op(dve.tensor_tensor(le[:, :, :].rearrange("p t (g e) -> p t g e", g=G), e32.rearrange("p t (g e) -> p t g e", g=G),
                                     sel[:, :, :].unsqueeze(3).broadcast_to([128, TT, G, EPG]), ALU.add))
                for k in range(2):
                    op(dve.tensor_reduce(m2[:, k, :], le[:, :, :], AX.X, ALU.max))
                    op(dve.tensor_tensor(v32[:, :, :], le[:, :, :], bt(m2[:, k, :], NE), ALU.is_equal))
                    op(dve.tensor_tensor(v32[:, :, :], v32[:, :, :], bc(w32[:, :], NE), ALU.mult))
                    op(dve.tensor_reduce(mx[:, :], v32[:, :, :], AX.X, ALU.max))
                    op(dve.tensor_tensor(oh[k][:, :, :], v32[:, :, :], bt(mx[:, :], NE), ALU.is_equal))
                    if k == 0:
                        op(dve.tensor_scalar(v32[:, :, :], oh[0][:, :, :], -2 * BIG, None, ALU.mult))
                        op(dve.tensor_tensor(le[:, :, :], le[:, :, :], v32[:, :, :], ALU.add))
                dve.tensor_tensor(dl[:, :], m2[:, 1, :], m2[:, 0, :], ALU.subtract).then_inc(ga, 1)
                op(dve.tensor_tensor(cnt[:, :, :], oh[0][:, :, :], oh[1][:, :, :], ALU.add))
                op(dve.tensor_tensor(cnt[:, :, :], cnt[:, :, :], bt(valid[:, :], NE), ALU.mult))
                op(dve.memset(pre[:, 0, :], 0.0))
                for t in range(TT):
                    op(dve.tensor_tensor(pre[:, t + 1, :], pre[:, t, :], cnt[:, t, :], ALU.add))
                dve.memset(most[:, :], 0.0).then_inc(counted, 1)
                dve.wait_ge(gb, 1)
                op(dve.tensor_reduce(pg[:, :], eg[:, :, :], AX.X, ALU.add))
                op(dve.reciprocal(pg[:, :], pg[:, :]))
                dve.wait_ge(gb, 2)
                op(dve.tensor_scalar(t1[:, :], dl[:, :], 1.0, None, ALU.add))
                op(dve.reciprocal(t1[:, :], t1[:, :]))
                op(dve.tensor_tensor(t1[:, :], t1[:, :], pg[:, :], ALU.mult))
                op(dve.tensor_tensor(g.gate[:, 0, :], t1[:, :], valid[:, :], ALU.mult))
                op(dve.tensor_tensor(g.gate[:, 1, :], g.gate[:, 0, :], dl[:, :], ALU.mult))
                dve.wait_ge(ranked, 1)
                for k in range(2):
                    op(dve.tensor_tensor(v32[:, :, :], oh[k][:, :, :], bank[0][:, 0:TT * NE].rearrange("p (t e) -> p t e", t=TT), ALU.mult))
                    op(dve.tensor_reduce(pos[:, :], v32[:, :, :], AX.X, ALU.add))
                    op(dve.tensor_tensor(v32[:, :, :], oh[k][:, :, :], bc(i32t[:, :], NE), ALU.mult))
                    op(dve.tensor_reduce(eid[:, :], v32[:, :, :], AX.X, ALU.add))
                    op(dve.tensor_scalar(over[:, :], pos[:, :], float(CAP), None, ALU.is_ge))
                    for m in range(2, PASSES):
                        op(dve.tensor_scalar(t1[:, :], pos[:, :], float(CAP * m), None, ALU.is_ge))
                        op(dve.tensor_tensor(over[:, :], over[:, :], t1[:, :], ALU.add))
                    n = PASSES * NE
                    op(dve.tensor_scalar(t1[:, :], pos[:, :], float(n), None, ALU.mult))
                    op(dve.tensor_tensor(t1[:, :], t1[:, :], eid[:, :], ALU.add))
                    op(dve.tensor_scalar(t2[:, :], over[:, :], float(NE - CAP * n), None, ALU.mult))
                    op(dve.tensor_tensor(t1[:, :], t1[:, :], t2[:, :], ALU.add))
                    op(dve.tensor_tensor(t1[:, :], t1[:, :], valid[:, :], ALU.mult))
                    op(dve.tensor_tensor(t1[:, :], t1[:, :], pad_a[:, k, :], ALU.add))
                    op(dve.tensor_copy(g.slot_a[:, k, :], t1[:, :]))
                    op(dve.tensor_scalar(t1[:, :], over[:, :], -1.0, None, ALU.mult))
                    op(dve.tensor_tensor(t1[:, :], t1[:, :], eid[:, :], ALU.add))
                    op(dve.tensor_scalar(t1[:, :], t1[:, :], float(CAP), None, ALU.mult))
                    op(dve.tensor_tensor(t1[:, :], t1[:, :], pos[:, :], ALU.add))
                    op(dve.tensor_tensor(g.row[:, k, :], t1[:, :], valid[:, :], ALU.mult))
                    dve.tensor_copy(g.turn[:, k, :], over[:, :]).then_inc(placed, 1)
                    dve.drain()
                op(dve.tensor_reduce(most[:, :], bank[1][:, 0:NE], AX.X, ALU.max))
                dve.tensor_copy(g.most[:, :], most[:, :])

            @block.scalar
            def _(act):
                act.wait_ge(ga, 1)
                act.activation(eg[:, :, :], eg[:, :, :], ACT.Exp).then_inc(gb, 1)
                act.wait_ge(ga, 2)
                act.activation(dl[:, :], dl[:, :], ACT.Exp).then_inc(gb, 1)

            @block.tensor
            def _(pe):
                pe.wait_ge(counted, 1)
                pe.matmul(bank[0][:, 0:TT * NE], upper[:, :], cnt[:, :, :], start=True, stop=False)
                pe.matmul(bank[0][:, 0:TT * NE], g.ones[:, :], pre[:, 0:TT, :], start=False, stop=True)
                pe.matmul(bank[1][:, 0:NE], g.ones[:, :], pre[:, TT, :], start=True, stop=True).then_inc(ranked, 1)

            @block.gpsimd
            def _(pool):
                for k in range(2):
                    pool.wait_ge(placed, k + 1)
                    for t in range(TT):
                        pool.indirect_dma_start(g.table[:, :], bass.IndirectOffsetOnAxis(g.slot_a[:, k, t:t + 1], 0), tok[:, t:t + 1], None).then_inc(scat, 16)
                pool.wait_ge(scat, 16 * 2 * TT)


def experts(nc, g):
    NW, NX = 4, 3
    with ExitStack() as ctx:
        sb = lambda n, s, d=f32: ctx.enter_context(nc.sbuf_tensor(n, s, d))
        sem = g.semaphores(nc, ctx)
        bank = g.bank
        wg = [sb(f"we_g{i}", [128, KD, FF]) for i in range(NW)]
        wu = [sb(f"we_u{i}", [128, KD, FF]) for i in range(NW)]
        wd = [sb(f"we_d{i}", [128, 2, D]) for i in range(NW)]
        idx = sb("idx", [128, NE], i32)
        xg = [sb(f"xg{i}", [128, D]) for i in range(NX)]
        xT = [sb(f"xgT{i}", [128, KD, CAP]) for i in range(2)]
        sg_, hT = [sb(f"silu{i}", [128, 2, CAP]) for i in range(2)], [sb(f"hT{i}", [128, 2, CAP]) for i in range(2)]
        yo = sb("yo", [128, 2, D])
        s = {n: sem("e_" + n) for n in ("idx turned xev up silu h down yev stored0 stored1 " + " ".join(f"w{i}" for i in range(NW))
                                        + " " + " ".join(f"x{i}" for i in range(NX))).split()}
        yk = [sb(f"yk{i}", [128, D]) for i in range(4)]
        now, here = sb("now", [128, 1]), sb("here", [128, 2, TT])
        weight, local, row = sb("weight", [128, 2, TT]), sb("local", [128, 2, TT]), sb("row_i", [128, 2, TT], i32)
        s |= {n: sem("e_" + n) for n in "rows combined y0 y1 y2 y3".split()}
        g.clear(nc)
        with nc.Block() as block:
            @block.vector
            def _(dve):
                dve.memset(now[:, :], 0.0)
        most = nc.values_load(g.most[0:1, 0:1], min_val=0, max_val=T)

        def one_pass(p):
            with nc.Block() as block:
                @block.gpsimd
                def _(pool):
                    for n, semaphore in s.items():
                        if n[0] not in "xy" or n in ("xev", "yev"):
                            pool.sem_clear(semaphore)
            with nc.Block() as block:
                @block.sync
                def _(sp):
                    sp.dma_start(idx[:, :], g.table[0:SLOTS, :].rearrange("(p n) o -> p (n o)", p=128)[:, bass.ds(p * NE, NE)]).then_inc(s["idx"], 16)
                    for e in range(NE):
                        if e >= NW:
                            sp.wait_ge(s["down"], e - NW + 1)
                        i = e % NW
                        sp.dma_start(wg[i][:, :, :], g.d_weg[e].rearrange("(p k) f -> p k f", p=128)).then_inc(s[f"w{i}"], 16)
                        sp.dma_start(wu[i][:, :, :], g.d_weu[e].rearrange("(p k) f -> p k f", p=128)).then_inc(s[f"w{i}"], 16)
                        sp.dma_start(wd[i][:, :, :], g.d_wed[e].rearrange("(f p) d -> p f d", p=128)).then_inc(s[f"w{i}"], 16)

                @block.gpsimd
                def _(pool):
                    pool.wait_ge(s["idx"], 16)
                    for e in range(NE):
                        if e >= NX:
                            pool.wait_ge(s["turned"], e - NX + 1)
                        pool.indirect_dma_start(xg[e % NX][:, :], None, g.xn[:, :], bass.IndirectOffsetOnAxis(idx[:, e:e + 1], 0)).then_inc(s[f"x{e % NX}"], 16)

                @block.tensor
                def _(pe):
                    def turn(e):
                        pe.wait_ge(s[f"x{e % NX}"], p * (16 * len(range(e % NX, NE, NX))) + 16 * (e // NX + 1))
                        if e >= 1:
                            pe.wait_ge(s["xev"], e)
                        v = xg[e % NX][:, :].rearrange("p (q k) -> p k q", k=KD)
                        for k in range(KD):
                            mm = pe.transpose(bank[k // 4][:, 128 * (k % 4):128 * (k % 4) + 128], v[:, k, :], g.ident[:, :])
                        mm.then_inc(s["turned"], 1)

                    def up(e):
                        i = e % NW
                        pe.wait_ge(s["xev"], e + 1)
                        pe.wait_ge(s[f"w{i}"], 48 * (e // NW + 1))
                        if e >= 2:
                            pe.wait_ge(s["h"], e - 1)
                        for a, w in enumerate((wg, wu)):
                            for f in range(2):
                                for k in range(KD):
                                    mm = pe.matmul(bank[2 + e % 2][:, 128 * (2 * a + f):128 * (2 * a + f) + CAP], w[i][:, k, 128 * f:128 * f + 128],
                                                   xT[e % 2][:, k, :], start=(k == 0), stop=(k == KD - 1))
                        mm.then_inc(s["up"], 1)

                    def down(e):
                        pe.wait_ge(s["h"], e + 1)
                        if e >= 2:
                            pe.wait_ge(s["yev"], e - 1)
                        for c in range(2):
                            for f in range(2):
                                mm = pe.matmul(bank[4 + 2 * (e % 2) + c][:, :], hT[e % 2][:, f, :], wd[e % NW][:, f, 512 * c:512 * c + 512],
                                               start=(f == 0), stop=(f == 1))
                        mm.then_inc(s["down"], 1)

                    turn(0)
                    for e in range(NE):
                        up(e)
                        if e + 1 < NE:
                            turn(e + 1)
                        if e >= 1:
                            down(e - 1)
                    down(NE - 1)

                def result(act, e):
                    act.wait_ge(s["down"], e + 1)
                    if e >= 2:
                        act.wait_ge(s[f"stored{e % 2}"], 16 * (e // 2))
                    for c in range(2):
                        last = act.activation(yo[:, e % 2, 512 * c:512 * c + 512], bank[4 + 2 * (e % 2) + c][:, :], ACT.Copy)
                    last.then_inc(s["yev"], 1)
                    act.wait_ge(s["yev"], e + 1)
                    act.dma_start(g.yb[e * CAP:(e + 1) * CAP, :], yo[:, e % 2, :]).then_inc(s[f"stored{e % 2}"], 16)
                    if e == NE - 1:
                        act.wait_ge(s["stored0"], 8 * NE)
                        act.wait_ge(s["stored1"], 8 * NE)

                @block.scalar
                def _(act):
                    for e in range(NE):
                        act.wait_ge(s["up"], e + 1)
                        if e >= 2:
                            act.wait_ge(s["h"], e - 1)
                        act.activation(sg_[e % 2][:, :, :].rearrange("p f q -> p (f q)"), bank[2 + e % 2][:, 0:256], ACT.Silu).then_inc(s["silu"], 1)
                        if e >= 1:
                            result(act, e - 1)
                    result(act, NE - 1)

                @block.vector
                def _(dve):
                    def evac(e):
                        dve.wait_ge(s["turned"], e + 1)
                        if e >= 2:
                            dve.wait_ge(s["up"], e - 1)
                        for c in range(2):
                            last = dve.tensor_copy(xT[e % 2][:, 4 * c:4 * c + 4, :].rearrange("p k q -> p (k q)"), bank[c][:, :])
                        last.then_inc(s["xev"], 1)
                    evac(0)
                    for e in range(NE):
                        if e + 1 < NE:
                            evac(e + 1)
                        dve.wait_ge(s["silu"], e + 1)
                        if e >= 2:
                            dve.wait_ge(s["down"], e - 1)
                        dve.tensor_tensor(hT[e % 2][:, :, :].rearrange("p f q -> p (f q)"), sg_[e % 2][:, :, :].rearrange("p f q -> p (f q)"),
                                          bank[2 + e % 2][:, 256:512], ALU.mult).then_inc(s["h"], 1)

            with nc.Block() as block:
                @block.vector
                def _(dve):
                    dve.tensor_scalar(here[:, :, :], g.turn[:, :, :], now[:, 0:1], None, ALU.is_equal)
                    dve.drain()
                    dve.tensor_tensor(weight[:, :, :], here[:, :, :], g.gate[:, :, :], ALU.mult)
                    dve.tensor_tensor(local[:, :, :], here[:, :, :], g.row[:, :, :], ALU.mult)
                    dve.drain()
                    dve.tensor_copy(row[:, :, :], local[:, :, :]).then_inc(s["rows"], 1)
                    dve.tensor_scalar(now[:, :], now[:, :], 1.0, None, ALU.add)
                    for n in range(2 * TT):
                        t, k = n // 2, n % 2
                        dve.wait_ge(s[f"y{n % 4}"], p * (16 * len(range(n % 4, 2 * TT, 4))) + 16 * (n // 4 + 1))
                        dve.scalar_tensor_tensor(out=g.h[:, t, :], in0=yk[n % 4][:, :], scalar=weight[:, k, t:t + 1], in1=g.h[:, t, :],
                                                 op0=ALU.mult, op1=ALU.add).then_inc(s["combined"], 1)
                        dve.drain()

                @block.gpsimd
                def _(pool):
                    pool.wait_ge(s["rows"], 1)
                    for n in range(2 * TT):
                        t, k = n // 2, n % 2
                        if n >= 4:
                            pool.wait_ge(s["combined"], n - 3)
                        pool.indirect_dma_start(yk[n % 4][:, :], None, g.yb[:, :], bass.IndirectOffsetOnAxis(row[:, k, t:t + 1], 0)).then_inc(s[f"y{n % 4}"], 16)

        one_pass(0)
        with nc.If(most > CAP):
            with nc.Fori(1, PASSES) as p:
                one_pass(p)


def finish(nc, g):
    with ExitStack() as ctx:
        sb = lambda n, s: ctx.enter_context(nc.sbuf_tensor(n, s, f32))
        sem = g.semaphores(nc, ctx)
        bank = g.bank
        wp, pp = sb("wp", [128, KD, D]), sb("pp", [128, 2, D])
        pT = sb("ppT", [128, 2, T])
        fgain = sb("fgain", [128, D])
        rstd, junk = sb("frstd", [128, TT]), sb("fjunk", [128, D])
        loads = sem("f_loads")
        g.clear(nc)
        with nc.Block() as block:
            @block.sync
            def _(sp):
                sp.dma_start(wp[:, :, :], g.d_pgate.rearrange("(k p) n -> p k n", p=128)).then_inc(loads, 16)
                sp.dma_start(pp[:, :, :], g.d_pproj.rearrange("(k p) n -> p k n", p=128)).then_inc(loads, 16)
                sp.dma_start(pT[:, :, :], g.d_pT.rearrange("(k p) n -> p k n", p=128)).then_inc(loads, 16)
                sp.dma_start(fgain[:, :], g.d_final_gain).then_inc(loads, 16)
                sp.wait_ge(loads, 64)

        norm_scales(nc, g, "ple", rstd, junk)
        un = sb("un", [128, 2, D])
        uT = sb("unT", [128, 2, KD, 128])
        sig = sb("sig", [128, 2, D])
        normed, turned, evac, gates, sigd, projs, updated = (sem("f_" + n) for n in "normed turned evac gates sigd projs updated".split())
        c = PC["norm_ple"]
        g.clear(nc)
        with nc.Block() as block:
            @block.vector
            def _(dve):
                def update(t):
                    r = rows_of(t)
                    dve.wait_ge(projs, t + 1)
                    dve.wait_ge(sigd, t + 1)
                    for i in range(2):
                        dve.tensor_tensor(sig[0:r, t % 2, 512 * i:512 * i + 512], sig[0:r, t % 2, 512 * i:512 * i + 512], bank[6 + i][0:r, :], ALU.mult)
                    dve.drain()
                    dve.tensor_tensor(g.h[0:r, t, :], g.h[0:r, t, :], sig[0:r, t % 2, :], ALU.add).then_inc(updated, 1)

                for t in range(TT):
                    if t >= 2:
                        dve.wait_ge(turned, t - 1)
                    dve.tensor_scalar(un[:, t % 2, :], g.h[:, t, :], rstd[:, t:t + 1], None, ALU.mult).then_inc(normed, 1)
                    dve.wait_ge(turned, t + 1)
                    if t >= 2:
                        dve.wait_ge(gates, t - 1)
                    for i in range(2):
                        last = dve.tensor_tensor(uT[:, t % 2, 4 * i:4 * i + 4, :], bank[2 * (t % 2) + i][:, :].rearrange("p (k q) -> p k q", k=4),
                                                 g.prm[:, c + 4 * i:c + 4 * i + 4].unsqueeze(2).broadcast_to([128, 4, 128]), ALU.mult)
                    last.then_inc(evac, 1)
                    if t >= 1:
                        update(t - 1)
                update(TT - 1)

            @block.tensor
            def _(pe):
                for t in range(TT):
                    r = rows_of(t)
                    pe.wait_ge(normed, t + 1)
                    if t >= 2:
                        pe.wait_ge(evac, t - 1)
                    for k in range(KD):
                        mm = pe.transpose(bank[2 * (t % 2) + k // 4][:, 128 * (k % 4):128 * (k % 4) + 128],
                                          un[:, t % 2, 128 * k:128 * k + 128], g.ident[:, :])
                    mm.then_inc(turned, 1)
                    if t >= 1:
                        pe.wait_ge(updated, t)
                    for i in range(2):
                        for k in range(2):
                            mm = pe.matmul(bank[6 + i][0:r, :], pT[:, k, 128 * t:128 * t + r], pp[:, k, 512 * i:512 * i + 512], start=(k == 0), stop=(k == 1))
                    mm.then_inc(projs, 1)
                    pe.wait_ge(evac, t + 1)
                    if t >= 1:
                        pe.wait_ge(sigd, t)
                    for i in range(2):
                        for k in range(KD):
                            mm = pe.matmul(bank[4 + i][0:r, :], uT[:, t % 2, k, 0:r], wp[:, k, 512 * i:512 * i + 512], start=(k == 0), stop=(k == KD - 1))
                    mm.then_inc(gates, 1)

            @block.scalar
            def _(act):
                for t in range(TT):
                    r = rows_of(t)
                    act.wait_ge(gates, t + 1)
                    if t >= 2:
                        act.wait_ge(updated, t - 1)
                    for i in range(2):
                        last = act.activation(sig[0:r, t % 2, 512 * i:512 * i + 512], bank[4 + i][0:r, :], ACT.Sigmoid)
                    last.then_inc(sigd, 1)
        norm_scales(nc, g, "fin", rstd, junk)
        out_ready, outs = sem("out_ready"), sem("outs")
        g.clear(nc)
        with nc.Block() as block:
            @block.vector
            def _(dve):
                for t in range(TT):
                    dve.scalar_tensor_tensor(out=g.h[:, t, :], in0=g.h[:, t, :], scalar=rstd[:, t:t + 1], in1=fgain[:, :],
                                             op0=ALU.mult, op1=ALU.mult).then_inc(out_ready, 1)

            @block.sync
            def _(sp):
                for t in range(TT):
                    r = rows_of(t)
                    sp.wait_ge(out_ready, t + 1)
                    sp.dma_start(g.o_y[128 * t:128 * t + r, :], g.h[0:r, t, :]).then_inc(outs, 16)
                sp.wait_ge(outs, 16 * TT)

CACHE_POSITIONS = [x for x in range(1536) if x % 16 < 8] + list(range(1536, 2048))


def masks():
    s, t = np.arange(CW)[:, None], np.arange(CW)[None, :]
    seq = (s // NT == t // NT)
    two = lambda m: np.concatenate([m, m], 0)
    low = np.stack([two(t < s), two((t < s) & seq)], 1)
    lev = lambda m: (s // (2 * m) == t // (2 * m)) & (s // m < t // m)
    level = np.stack([two(x) for x in (lev(1), lev(2), lev(4), lev(8), lev(16), lev(1).T, lev(32))], 1)
    pair = np.stack([two(np.concatenate([(s < t) & z, (s <= t) & z], 1)) for z in (np.ones_like(seq), seq)], 1)
    mseq = (np.arange(128)[:, None] % CW) // NT == np.arange(NB)[None, :]
    keep = np.ones(T)
    keep[np.arange(0, S, CW)] = 0
    keep[np.arange(S, T, NT)] = 0
    p, q = np.arange(128)[:, None], np.arange(128)[None, :]
    f = lambda m: np.ascontiguousarray(m.astype(np.float32))
    inv = np.power(np.float32(10000.0), -np.arange(32, dtype=np.float32) * np.float32(2.0) / np.float32(E)).astype(np.float32)
    pos = np.concatenate([np.arange(S), np.tile(4096 + np.arange(NT), NB)]).astype(np.float32)
    ang = (pos[None, :] * np.tile(inv, 4)[:, None]).astype(np.float32)
    rot = np.zeros((128, 128))
    for m in range(128):
        rot[m + 32 if m % E < 32 else m - 32, m] = -1 if m % E < 32 else 1

    def log_count(dist):
        n = sum(((dist >= 0) & (dist % dil == 0) & (dist <= win)).astype(int) for win, dil in ((128, 1), (512, 4), (2048, 16)))
        return np.where(n > 0, 8 * np.log(np.maximum(n, 1)), -8e30)
    count = log_count(np.arange(128)[:, None] + (S - 128) - np.arange(S)[None, :])
    r = np.arange(128)
    mcache = log_count(2048 + (r % NT)[:, None] - np.array(CACHE_POSITIONS)[None, :])
    token = NT * (2 * np.arange(NB // 2)[None, :] + r[:, None] // (H * NT)) + r[:, None] % NT
    own = np.arange(TS)[None, None, :]
    mnew = np.where(token[:, :, None] // NT == own // NT, log_count(token[:, :, None] % NT - own % NT), -8e30)
    p, q = np.arange(128)[:, None], np.arange(128)[None, :]
    tokens = np.arange(TT)[None, :] * 128 + np.arange(128)[:, None]
    valid = tokens < T
    row = lambda v: np.broadcast_to(np.asarray(v, np.float32), (128, len(v)))
    routing = dict(upper=f(p < q), valid=f(valid), pad_a=f(np.stack([np.where(valid, 0, SLOTS + 128 * k + np.arange(128)[:, None]) for k in range(2)], 1)), w4=f(row(np.arange(G, 0, -1))),
                   w32=f(row(np.arange(NE, 0, -1))), i32t=f(row(np.arange(NE))), tok=np.ascontiguousarray(tokens.astype(np.int32)))
    return dict(routing, mcache=f(mcache), mnew=f(mnew), own_row=f(token[:, :, None] == own),
                own_head=f((r // NT % H)[:, None] == np.arange(RW)[None, :] // E), cos=f(np.cos(ang)), sin=f(np.sin(ang)), rot=f(rot), count=f(count), m_low=f(low), m_level=f(level), m_pair=f(pair), m_seq=f(mseq), m_eye=f(two(s == t)),
                keep=f(np.broadcast_to(keep, (128, T))), ones=f(np.ones((128, 128))), headones=f(p // E == q // E), ident=f(p == q))


def lay_out(i):
    a = {k: np.asarray(v) for k, v in i.items()}
    x = np.concatenate([a["x_prompt"].reshape(S, D), a["x_sample"].reshape(TS, D)], 0)
    cols = np.zeros((128, PCN), np.float32)

    def put(name, v):
        k = -(-v.size // 128)
        for n in range(k):
            part = v[128 * n:128 * n + 128]
            cols[:part.size, PC[name] + n] = part
    mu = a["mu_shift"][0]
    for n, v in (("norm_mix", a["norm_mix"][0]), ("mu_r", mu[0:RW]), ("mu_k", mu[RW:2 * RW]), ("mu_v", mu[2 * RW:3 * RW]),
                 ("mu_wa", mu[3 * RW:3 * RW + 64]), ("mu_g", mu[3 * RW + 64:]), ("w0", a["decay_w0"][0]), ("a0", a["iclr_a0"][0]),
                 ("k_k", a["k_k"][0]), ("k_a", a["k_a"][0]), ("r_k", a["r_k"][0].reshape(-1)), ("lnx_w", a["lnx_w"][0]),
                 ("lnx_b", a["lnx_b"][0]), ("attn_norm", a["attn_out_norm"][0]), ("norm_ffn", a["norm_ffn"][0]), ("norm_ple", a["norm_ple"][0])):
        put(n, v)
    c = np.ascontiguousarray
    kcT = c(a["cache_k_win"][0].reshape(NB, 2048, RW)[:, CACHE_POSITIONS].transpose(0, 2, 1))
    vc = c(a["cache_v_win"][0].reshape(NB, 2048, RW)[:, CACHE_POSITIONS])
    over = lambda v: c(np.broadcast_to(v, (128, v.size)))
    p = np.concatenate([a["p_prompt"][0].reshape(S, -1), a["p_sample"][0].reshape(TS, -1)], 0)
    wr = np.concatenate([a["router_group_w"][0], a["router_expert_w"][0]], 1)
    return dict(masks(), kcT=kcT, x=x, wout=c(a["w_out"][0]), ffn_gain=over(a["norm_ffn"][0]), final_gain=over(a["norm_final"]),
                wr=c(wr.reshape(KD, 128, G + NE).transpose(1, 0, 2)), br=over(np.concatenate([a["router_group_b"][0], a["router_expert_b"][0]])),
                weg=c(a["expert_w_gate"][0]), weu=c(a["expert_w_up"][0]), wed=c(a["expert_w_down"][0]), pgate=c(a["ple_gate_w"][0]),
                pproj=c(a["ple_proj"][0]), pT=c(p.T), vc=vc, xT=c(x.T), prm=cols, win=c(a["w_in"][0]),
                w2a2=c(np.concatenate([a["decay_w2"][0], a["iclr_a2"][0]], 0)), g2=c(a["gate_g2"][0]),
                shT=c(a["state_shift"][0].T), stT=c(a["state_wkv"][0].transpose(1, 3, 0, 2).reshape(RW, NB * E)))


OUTS = dict(pshift=(RP, 1), sshift=(RP, NB), pwkv=(RW, E), swkv=(RW, NB * E), kT=(RW, T), v=(T, RW), y=(T, D))


class Parts:

    def __init__(self):
        self.new = []

    def semaphores(self, nc, ctx):
        def take(name):
            self.new.append(ctx.enter_context(nc.semaphore(name)))
            return self.new[-1]
        return take

    def clear(self, nc):
        new, self.new = self.new, []
        with nc.Block() as block:
            @block.gpsimd
            def _(pool):
                for semaphore in new:
                    pool.sem_clear(semaphore)


def build(nc, g):
    with ExitStack() as ctx:
        sb = lambda n, s, d=f32: ctx.enter_context(nc.sbuf_tensor(n, s, d))
        g.bank = [ctx.enter_context(nc.psum_tensor(f"bank{i}", [128, 512], f32)) for i in range(8)]
        g.s_const = ctx.enter_context(nc.semaphore("s_const"))
        g.prm = sb("prm", [128, PCN])
        g.ones, g.ident = sb("ones", [128, 128]), sb("ident", [128, 128])
        g.table = nc.dram_tensor("table", (SLOTS + 256, 1), i32, kind="Internal").ap()
        g.xn = nc.dram_tensor("xn_rows", (TT * 128, D), f32, kind="Internal").ap()
        g.yb = nc.dram_tensor("y_rows", (NE * CAP, D), f32, kind="Internal").ap()
        g.h = sb("h", [128, TT, D])
        with ExitStack() as mix:
            sm = lambda n, s, d=f32: mix.enter_context(nc.sbuf_tensor(n, s, d))
            g.att = sm("att", [128, TT, RW])
            g.rwT = sm("rwT", [128, J, T])
            g.qs, g.ks, g.vs = sm("qs", [128, J, TS]), sm("ks", [128, J, TS]), sm("vs", [128, J, 128])
            with ExitStack() as early:
                se = lambda n, s, d=f32: early.enter_context(nc.sbuf_tensor(n, s, d))
                g.uT = g.h[:, :, :].rearrange("p t d -> p (t d)")[:, 0:KD * T].rearrange("p (k t) -> p k t", k=KD)
                g.constants = [(g.ident[:, :], g.d_ident)]
                g.headones = se("headones", [128, 128])
                g.m_low, g.m_level, g.m_pair = se("m_low", [128, 2, CW]), se("m_level", [128, 7, CW]), se("m_pair", [128, 2, 128])
                g.m_seq, g.m_eye, g.keep = se("m_seq", [128, NB]), se("m_eye", [128, CW]), se("keep", [128, T])
                g.constants += [(g.headones[:, :], g.d_headones), (g.m_low[:, :, :], g.d_m_low), (g.m_level[:, :, :], g.d_m_level),
                                (g.m_pair[:, :, :], g.d_m_pair), (g.m_seq[:, :], g.d_m_seq), (g.m_eye[:, :], g.d_m_eye), (g.keep[:, :], g.d_keep)]
                project_tokens(nc, g)
                with nc.sbuf_tensor("tw", [64, T], f32) as g.tw, nc.sbuf_tensor("sg", [96, T], f32) as g.sg:
                    lora_inputs(nc, g)
                    rwkv(nc, g)
            g.kc = [sm(f"kc{i}", [128, J, NSEL]) for i in range(2)]
            g.k_in = [mix.enter_context(nc.semaphore(f"k_in{i}")) for i in range(2)]
            attention(nc, g)
            decode_attention(nc, g)
            out_projection(nc, g)
        g.gate = sb("gate_w", [128, 2, TT])
        g.slot_a, g.most = sb("slot_a", [128, 2, TT], i32), sb("most_i", [128, 1], i32)
        g.row, g.turn = sb("row", [128, 2, TT]), sb("turn", [128, 2, TT])
        route(nc, g)
        experts(nc, g)
        finish(nc, g)


def kernel(**inputs):
    import concourse.bacc as bacc
    from concourse.bass_utils import run_bass_kernel_spmd as run
    nc = bacc.Bacc("TRN2", target_bir_lowering=False, num_devices=1)
    arrays = lay_out(inputs)
    g = Parts()
    for n, a in arrays.items():
        g.__dict__["d_" + n] = nc.dram_tensor("in_" + n, a.shape, mybir.dt.from_np(a.dtype), kind="ExternalInput").ap()
    for n, shape in OUTS.items():
        g.__dict__["o_" + n] = nc.dram_tensor("out_" + n, shape, f32, kind="ExternalOutput").ap()
    build(nc, g)
    r = run(nc, [{"in_" + n: a for n, a in arrays.items()}], core_ids=[0]).results[0]
    y, kT, v = np.asarray(r["out_y"]), np.asarray(r["out_kT"]).T, np.asarray(r["out_v"])
    c = np.ascontiguousarray
    heads = lambda z, *lead: c(z).reshape(1, *lead, H, E)
    pwkv = np.asarray(r["out_pwkv"]).reshape(1, 1, H, E, E).transpose(0, 1, 2, 4, 3)
    swkv = np.asarray(r["out_swkv"]).reshape(H, E, NB, E).transpose(2, 0, 3, 1)[None]
    return (c(y[:S]).reshape(1, S, D), c(y[S:]).reshape(NB, NT, D), heads(kT[:S], 1, S), heads(v[:S], 1, S), c(pwkv),
            c(np.asarray(r["out_pshift"]).reshape(1, 1, RP)), heads(kT[S:], NB, NT), heads(v[S:], NB, NT), c(swkv),
            c(np.asarray(r["out_sshift"]).T)[None])
```

```python
import numpy as np
import concourse.bass as bass
from concourse import mybir
from contextlib import ExitStack

D = 1024
KD = D // 128
S = 1024
NB, NT = 8, 8
TS = NB * NT
T = S + TS
CW = 64
NC = S // CW
NCH = NC + 1
H, E = 8, 64
RW = H * E
J = H // 2
LORA = 160
RP = 3 * RW + LORA
IP = RP + 3 * RW
TT = 9
CHUNKS = [(0, 352), (352, 352), (704, 384)]
LOGC = float(np.exp(np.float64(-0.5)))
LNX_EPS = 1e-5 * E
RMS_EPS = 1e-6

f32 = mybir.dt.float32
i32 = mybir.dt.int32
ALU = mybir.AluOpType
ACT = mybir.ActivationFunctionType
AX = mybir.AxisListType

PC = {}
_at = 0
for _n, _k in (("norm_mix", 8), ("mu_r", 4), ("mu_k", 4), ("mu_v", 4), ("mu_wa", 1), ("mu_g", 1), ("w0", 4), ("a0", 4),
               ("k_k", 4), ("k_a", 4), ("r_k", 4), ("lnx_w", 4), ("lnx_b", 4), ("attn_norm", 4), ("norm_ffn", 8),
               ("norm_ple", 8)):
    PC[_n] = _at
    _at += _k
PCN = _at


def dyn(ap, i):
    return ap[:, bass.ds(i, 1)]


def project_tokens(nc, g):
    with ExitStack() as ctx:
        sq = ctx.enter_context(nc.sbuf_tensor("sq", [128, 2, T], f32))
        rstd = ctx.enter_context(nc.sbuf_tensor("rstd", [128, T], f32))
        sem = g.semaphores(nc, ctx)
        x_loaded = [sem(f"x_loaded{k}") for k in range(KD)]
        squared, summed, mean_ready, root_ready = sem("squared"), sem("summed"), sem("mean_ready"), sem("root_ready")
        g.clear(nc)
        with nc.Block() as block:
            @block.sync
            def _(sp):
                sp.dma_start(g.prm[:, :], g.d_prm).then_inc(g.s_const, 16)
                sp.dma_start(g.ones[:, :], g.d_ones).then_inc(g.s_const, 16)
                for k in range(KD):
                    sp.dma_start(g.uT[:, k, :], g.d_xT[k * 128:(k + 1) * 128, :]).then_inc(x_loaded[k], 16)
                for dst, src in g.constants:
                    sp.dma_start(dst, src).then_inc(g.s_const, 16)
                sp.wait_ge(g.s_const, 16 * (2 + len(g.constants)))

            @block.scalar
            def _(act):
                for k in range(KD):
                    act.wait_ge(x_loaded[k], 16)
                    if k >= 2:
                        act.wait_ge(summed, k - 1)
                    act.activation(sq[:, k % 2, :], g.uT[:, k, :], ACT.Square).then_inc(squared, 1)
                act.wait_ge(mean_ready, 1)
                act.activation(rstd[:, :], rstd[:, :], ACT.Sqrt).then_inc(root_ready, 1)

            @block.tensor
            def _(pe):
                pe.wait_ge(g.s_const, 32)
                for k in range(KD):
                    pe.wait_ge(squared, k + 1)
                    for n, (a, w) in enumerate(CHUNKS):
                        mm = pe.matmul(g.bank[n][:, 0:w], g.ones[:, :], sq[:, k % 2, a:a + w],
                                       start=(k == 0), stop=(k == KD - 1))
                    mm.then_inc(summed, 1)

            @block.vector
            def _(dve):
                dve.wait_ge(summed, KD)
                for n, (a, w) in enumerate(CHUNKS):
                    last = dve.tensor_scalar(rstd[:, a:a + w], g.bank[n][:, 0:w], 1.0 / D, RMS_EPS, ALU.mult, ALU.add)
                last.then_inc(mean_ready, 1)
                dve.wait_ge(root_ready, 1)
                dve.reciprocal(rstd[:, :], rstd[:, :])
                dve.drain()
                for k in range(KD):
                    c = PC["norm_mix"] + k
                    dve.scalar_tensor_tensor(out=g.uT[:, k, :], in0=g.uT[:, k, :], scalar=g.prm[:, c:c + 1],
                                             in1=rstd[:, :], op0=ALU.mult, op1=ALU.mult)


def token_shift(dve, raw, edge, ends, ends_ready, diff, out, mu, rows=128):
    rp, rs = raw[0:rows, 0:S + 1], raw[0:rows, S + 1:].rearrange("p (b t) -> p b t", b=NB)
    ds = diff[0:rows, S:T].rearrange("p (b t) -> p b t", b=NB)
    os_ = out[0:rows, S:T].rearrange("p (b t) -> p b t", b=NB)
    dve.tensor_copy(rs[:, :, 0:1], edge.unsqueeze(2))
    dve.tensor_copy(ends.unsqueeze(2), rs[:, :, NT:NT + 1]).then_inc(ends_ready, 1)
    dve.tensor_tensor(diff[0:rows, 0:S], rp[:, 0:S], rp[:, 1:S + 1], ALU.subtract)
    dve.drain()
    dve.tensor_tensor(ds, rs[:, :, 0:NT], rs[:, :, 1:NT + 1], ALU.subtract)
    dve.drain()
    dve.scalar_tensor_tensor(out=out[0:rows, 0:S], in0=diff[0:rows, 0:S], scalar=mu, in1=rp[:, 1:S + 1],
                             op0=ALU.mult, op1=ALU.add)
    return dve.scalar_tensor_tensor(out=os_, in0=ds, scalar=mu, in1=rs[:, :, 1:NT + 1], op0=ALU.mult, op1=ALU.add)


def raw_out(act, bank, n, raw, rows=128):
    a, w = CHUNKS[n]
    prompt = min(w, S - a)
    out = act.activation(raw[0:rows, 1 + a:1 + a + prompt], bank[0:rows, 0:prompt], ACT.Copy)
    if prompt < w:
        rs = raw[0:rows, S + 1:].rearrange("p (b t) -> p b t", b=NB)
        out = act.activation(rs[:, :, 1:NT + 1], bank[0:rows, prompt:w].rearrange("p (b t) -> p b t", b=NB), ACT.Copy)
    return out


def lora_inputs(nc, g):
    with ExitStack() as ctx:
        sb = lambda n, s: ctx.enter_context(nc.sbuf_tensor(n, s, f32))
        sem = g.semaphores(nc, ctx)
        wl = sb("wl", [128, KD, LORA])
        raw = [sb("raw_wa", [64, T + 1 + NB]), sb("raw_g", [96, T + 1 + NB])]
        diff, mix = sb("ldiff", [96, T]), sb("lmix", [96, T])
        edge, ends = sb("ledge", [96, 2, NB]), sb("lends", [96, 2, NB])
        ready = sem("l_ready")
        loaded, edges, done, evac, mixed, used, outs = (sem(n) for n in (
            "l_loaded", "l_edges", "l_done", "l_evac", "l_mixed", "l_used", "l_outs"))
        rows = [64, 96]
        g.clear(nc)
        with nc.Block() as block:
            @block.sync
            def _(sp):
                sp.dma_start(wl[:, :, :], g.d_win.rearrange("(k p) n -> p k n", p=128)[:, :, 3 * RW:RP]).then_inc(loaded, 16)
                for i in range(2):
                    r0 = 3 * RW + 64 * i
                    sp.dma_start(edge[0:rows[i], i, :], g.d_shT[r0:r0 + rows[i], :]).then_inc(edges, 16)
                sp.wait_ge(evac, 6)
                sp.wait_ge(ready, 2)
                for i in range(2):
                    r0 = 3 * RW + 64 * i
                    sp.dma_start(g.o_pshift[r0:r0 + rows[i], :], raw[i][:, S:S + 1]).then_inc(outs, 16)
                    sp.dma_start(g.o_sshift[r0:r0 + rows[i], :], ends[0:rows[i], i, :]).then_inc(outs, 16)
                sp.wait_ge(outs, 64)

            @block.tensor
            def _(pe):
                pe.wait_ge(loaded, 16)
                for i in range(2):
                    for n, (a, w) in enumerate(CHUNKS):
                        for k in range(KD):
                            mm = pe.matmul(g.bank[3 * i + n][0:rows[i], 0:w], wl[:, k, 64 * i:64 * i + rows[i]],
                                           g.uT[:, k, a:a + w], start=(k == 0), stop=(k == KD - 1))
                        mm.then_inc(done, 1)

            @block.scalar
            def _(act):
                for i in range(2):
                    for n in range(3):
                        act.wait_ge(done, 3 * i + n + 1)
                        raw_out(act, g.bank[3 * i + n], n, raw[i], rows[i]).then_inc(evac, 1)
                act.wait_ge(mixed, 1)
                act.activation(g.tw[0:32, :], mix[0:32, :], ACT.Tanh)
                act.activation(g.tw[32:64, :], mix[32:64, :], ACT.Copy).then_inc(used, 1)
                act.wait_ge(mixed, 2)
                act.activation(g.sg[:, :], mix[:, :], ACT.Sigmoid)

            @block.vector
            def _(dve):
                for i in range(2):
                    dve.memset(raw[i][:, 0:1], 0.0)
                dve.drain()
                dve.wait_ge(edges, 32)
                for i, name in enumerate(("mu_wa", "mu_g")):
                    dve.wait_ge(evac, 3 * i + 3)
                    if i:
                        dve.wait_ge(used, 1)
                    c = PC[name]
                    token_shift(dve, raw[i], edge[0:rows[i], i, :], ends[0:rows[i], i, :], ready, diff, mix, g.prm[0:rows[i], c:c + 1], rows[i]).then_inc(mixed, 1)
                    dve.drain()


def rwkv(nc, g):
    with ExitStack() as ctx:
        sb = lambda n, s: ctx.enter_context(nc.sbuf_tensor(n, s, f32))
        sem = g.semaphores(nc, ctx)
        w3 = sb("w3", [128, KD, 3, 128])
        wwa, wg2 = sb("wwa", [64, 128]), sb("wg2", [96, 128])
        raw = [sb(f"raw{i}", [128, T + 1 + NB]) for i in range(3)]
        edge, ends = sb("edge", [128, 3, NB]), sb("ends", [128, 3, NB])
        s0 = sb("s0", [128, NB, E])
        work = sb("work", [128, 4, T])
        kk, tmp, k, r = (work[:, i, :] for i in range(4))
        gm = work[:, :, :].rearrange("p a t -> p (a t)").rearrange("p (c h x) -> p c h x", c=NCH, h=2)
        v, dif = sb("v", [128, T]), sb("dif", [128, T])
        gate, dec, bon = sb("gate", [128, T]), sb("dec", [128, T]), sb("bon", [128, T])
        ar, bk = sb("ar", [128, NCH, 2, CW]), sb("bk", [128, NCH, 2, CW])
        rawc = [raw[i][:, 0:T].rearrange("p (c t) -> p c t", c=NCH) for i in range(2)]
        gain, gain_inv = dec[:, :].rearrange("p (c t) -> p c t", c=NCH), rawc[1]
        gain_before = raw[2][:, 0:T].rearrange("p (c t) -> p c t", c=NCH)
        alow, zb = rawc
        bv = dif[:, :].rearrange("p (c t) -> p c t", c=NCH)
        bkt = sb("bkt", [128, NCH, 2, E])
        norm, spare = (bkt[:, :, :, :].rearrange("p c h e -> p (c h e)")[:, T * i:T * i + T] for i in range(2))
        ORDER = (1, 3, 4, 2, 0, 5)
        uv = sb("uv", [128, NCH, 2, E])
        xa, xb = sb("xa", [128, NCH, CW]), sb("xb", [128, NCH, CW])
        st = sb("st", [128, 2, E])
        sdec, rhs = sb("sdec", [128, E]), sb("rhs", [128, E])
        w0s = sb("w0s", [128, 2, NB, NT])
        uvm = raw[2][:, 0:2 * NB * E].rearrange("p (h b e) -> p h b e", h=2, b=NB)
        sn = v[:, 0:NB * E].rearrange("p (b e) -> p b e", b=NB)
        bank = g.bank

        def flat(x):
            return x.rearrange("p c t -> p (c t)")

        names = ("w_loaded w3_loaded a_proj a_evac a_kk a_sq a_ss a_max a_free a_root a_scan a_exp a_rkr a_bn a_ends a_outs a_routs "
                 "b_am b_init b_job b_gm b_copy b_bvmm b_bv b_z b_zev b_x b_xev b_t b_tev "
                 "c_rhs c_rhsev c_u c_uev c_uev1 c_s c_y c_sev c_w c_wev c_um c_outs d_in d_mean d_cen d_sq d_var d_eps d_root d_done").split()
        s = {n: sem(n) for n in names}

        def load_w3(sp, col, loaded):
            for i in range(3):
                sp.dma_start(w3[:, :, i, :], g.d_win.rearrange("(k p) n -> p k n", p=128)[:, :, bass.ds(col + RW * i, 128)]).then_inc(loaded, 16)

        g.clear(nc)
        with nc.Block() as block:
            @block.sync
            def _(sp):
                load_w3(sp, 0, s["w3_loaded"])
                sp.wait_ge(s["w3_loaded"], 48)

        def clear_counts():
            with nc.Block() as block:
                @block.gpsimd
                def _(pool):
                    for semaphore in s.values():
                        pool.sem_clear(semaphore)

        y = flat(xb[:, :, :])
        cen, var = dif[:, :], work[:, 2, :]
        NORM_BANK = (6, 7, 5)

        def norm_means(pe):
            for n, (a, w) in enumerate(CHUNKS):
                pe.matmul(bank[NORM_BANK[n]][:, 0:w], g.headones[:, :], y[:, a:a + w], start=True, stop=True).then_inc(s["d_mean"], 1)

        def norm_variances(pe):
            for n, (a, w) in enumerate(CHUNKS):
                pe.wait_ge(s["d_sq"], n + 1)
                pe.matmul(bank[NORM_BANK[n]][:, 0:w], g.headones[:, :], tmp[:, a:a + w], start=True, stop=True).then_inc(s["d_var"], 1)

        def norm_squares(act):
            for n, (a, w) in enumerate(CHUNKS):
                act.wait_ge(s["d_cen"], n + 1)
                act.activation(tmp[:, a:a + w], cen[:, a:a + w], ACT.Square).then_inc(s["d_sq"], 1)

        def norm_roots(act):
            for n, (a, w) in enumerate(CHUNKS):
                act.wait_ge(s["d_eps"], n + 1)
                act.activation(var[:, a:a + w], var[:, a:a + w], ACT.Sqrt).then_inc(s["d_root"], 1)

        def norm_outputs(dve, j):
            for n, (a, w) in enumerate(CHUNKS):
                dve.wait_ge(s["d_mean"], n + 1)
                dve.scalar_tensor_tensor(out=cen[:, a:a + w], in0=bank[NORM_BANK[n]][:, 0:w], scalar=-1.0 / E, in1=y[:, a:a + w],
                                         op0=ALU.mult, op1=ALU.add).then_inc(s["d_cen"], 1)
            for n, (a, w) in enumerate(CHUNKS):
                dve.wait_ge(s["d_var"], n + 1)
                dve.tensor_scalar(var[:, a:a + w], bank[NORM_BANK[n]][:, 0:w], 1.0 / E, LNX_EPS, ALU.mult, ALU.add).then_inc(s["d_eps"], 1)
            for n, (a, w) in enumerate(CHUNKS):
                dve.wait_ge(s["d_root"], n + 1)
                dve.reciprocal(var[:, a:a + w], var[:, a:a + w])
            dve.drain()
            dve.scalar_tensor_tensor(out=cen, in0=cen, scalar=dyn(g.prm, j + PC["lnx_w"]), in1=var, op0=ALU.mult, op1=ALU.mult)
            dve.drain()
            dve.scalar_tensor_tensor(out=cen, in0=cen, scalar=dyn(g.prm, j + PC["lnx_b"]), in1=bon[:, :], op0=ALU.add, op1=ALU.add)
            dve.drain()
            dve.tensor_tensor(g.rwT[:, bass.ds(j, 1), :].rearrange("p o t -> p (o t)"), cen, gate[:, :], ALU.mult).then_inc(s["d_done"], 1)
            dve.drain()

        def project_pair(j, last):
            with nc.Block() as block:
                @block.sync
                def _(sp):
                    sp.dma_start(wwa[:, :], g.d_w2a2[:, bass.ds(j * 128, 128)]).then_inc(s["w_loaded"], 16)
                    sp.dma_start(wg2[:, :], g.d_g2[:, bass.ds(j * 128, 128)]).then_inc(s["w_loaded"], 16)
                    for i in range(3):
                        sp.dma_start(edge[:, i, :], g.d_shT[bass.ds(j * 128 + RW * i, 128), :]).then_inc(s["w_loaded"], 16)
                    sp.dma_start(s0[:, :, :].rearrange("p b v -> p (b v)"), g.d_stT[bass.ds(j * 128, 128), :]).then_inc(s["w_loaded"], 16)
                    for i, evac, ready in ((1, 3, 1), (2, 12, 2), (0, 15, 3)):
                        stored = s["a_routs"] if i == 0 else s["a_outs"]
                        sp.wait_ge(s["a_evac"], evac)
                        sp.wait_ge(s["a_ends"], ready)
                        sp.dma_start(g.o_pshift[bass.ds(j * 128 + RW * i, 128), :], raw[i][:, S:S + 1]).then_inc(stored, 16)
                        sp.dma_start(g.o_sshift[bass.ds(j * 128 + RW * i, 128), :], ends[:, i, :]).then_inc(stored, 16)
                    sp.wait_ge(s["a_outs"], 64)
                    sp.wait_ge(s["a_routs"], 32)
                    if last is not None:
                        sp.wait_ge(s["c_outs"], 32)

                @block.tensor
                def _(pe):
                    if last is not None:
                        norm_means(pe)
                    job = 0
                    for q in ORDER:
                        for n, (a, w) in enumerate(CHUNKS):
                            if last is not None and job == 1:
                                norm_variances(pe)
                            if last is not None and job == 5:
                                pe.wait_ge(s["d_eps"], 3)
                            if job >= 6:
                                pe.wait_ge(s["a_evac"], job - 5)
                            out = bank[job % 6][:, 0:w]
                            if q < 3:
                                for kk in range(KD):
                                    mm = pe.matmul(out, w3[:, kk, q, :], g.uT[:, kk, a:a + w], start=(kk == 0), stop=(kk == KD - 1))
                            elif q == 3:
                                if n == 0:
                                    pe.wait_ge(s["w_loaded"], 96)
                                mm = pe.matmul(out, wwa[0:32, :], g.tw[0:32, a:a + w], start=True, stop=True)
                            elif q == 4:
                                mm = pe.matmul(out, wwa[32:64, :], g.tw[32:64, a:a + w], start=True, stop=True)
                            else:
                                mm = pe.matmul(out, wg2[:, :], g.sg[:, a:a + w], start=True, stop=True)
                            mm.then_inc(s["a_proj"], 1)
                            job += 1
                            if job == 10:
                                pe.wait_ge(s["a_sq"], 1)
                                for m, (a2, w2) in enumerate(CHUNKS):
                                    if m == 2:
                                        pe.wait_ge(s["a_max"], 1)
                                    pe.matmul(bank[6 + m % 2][:, 0:w2], g.headones[:, :], norm[:, a2:a2 + w2], start=True, stop=True).then_inc(s["a_ss"], 1)
                    pe.wait_ge(s["a_rkr"], 1)
                    pe.wait_ge(s["a_max"], 3)
                    pe.wait_ge(s["a_evac"], 13)
                    for n, (a, w) in enumerate(CHUNKS):
                        pe.matmul(bank[(6, 7, 0)[n]][:, 0:w], g.headones[:, :], tmp[:, a:a + w], start=True, stop=True).then_inc(s["a_bn"], 1)

                @block.scalar
                def _(act):
                    if last is not None:
                        norm_squares(act)
                    job = 0
                    for q in ORDER:
                        for n, (a, w) in enumerate(CHUNKS):
                            if last is not None and job == 1:
                                norm_roots(act)
                            if last is not None and job == 6:
                                act.wait_ge(s["d_done"], 1)
                            act.wait_ge(s["a_proj"], job + 1)
                            b = bank[job % 6][:, 0:w]
                            if q < 3:
                                raw_out(act, bank[job % 6], n, raw[q]).then_inc(s["a_evac"], 1)
                            elif q == 3:
                                act.activation(dec[:, a:a + w], b, ACT.Sigmoid, bias=dyn(g.prm, j + PC["w0"])).then_inc(s["a_evac"], 1)
                            elif q == 4:
                                act.activation(bon[:, a:a + w], b, ACT.Sigmoid, bias=dyn(g.prm, j + PC["a0"])).then_inc(s["a_evac"], 1)
                            else:
                                act.activation(gate[:, a:a + w], b, ACT.Copy).then_inc(s["a_evac"], 1)
                            job += 1
                            if job == 9:
                                act.wait_ge(s["a_kk"], 1)
                                act.activation(norm, kk, ACT.Square).then_inc(s["a_sq"], 1)
                            if job == 12:
                                act.wait_ge(s["a_max"], 3)
                                act.activation(norm, norm, ACT.Sqrt).then_inc(s["a_root"], 1)
                            if job == 13:
                                act.wait_ge(s["a_scan"], 1)
                                act.wait_ge(s["a_free"], 1)
                                act.wait_ge(s["a_outs"], 64)
                                act.activation(gain, xa[:, :, :], ACT.Exp, scale=-LOGC)
                                act.activation(gain_before, xb[:, :, :], ACT.Exp, scale=-LOGC)
                                act.activation(gain_inv, xa[:, :, :], ACT.Exp, scale=LOGC).then_inc(s["a_exp"], 1)

                @block.vector
                def _(dve):
                    if last is not None:
                        norm_outputs(dve, last)
                    for i in range(3):
                        dve.memset(raw[i][:, 0:1], 0.0)
                    dve.drain()
                    dve.wait_ge(s["w_loaded"], 96)
                    def shifted(q, name, out, evac):
                        dve.wait_ge(s["a_evac"], evac)
                        end = token_shift(dve, raw[q], edge[:, q, :], ends[:, q, :], s["a_ends"], dif, out, dyn(g.prm, j + PC[name]))
                        if q == 2:
                            end.then_inc(s["a_free"], 1)
                        dve.drain()

                    shifted(1, "mu_k", k, 3)
                    dve.tensor_scalar(kk, k, dyn(g.prm, j + PC["k_k"]), None, ALU.mult).then_inc(s["a_kk"], 1)
                    dve.wait_ge(s["a_evac"], 6)
                    dve.tensor_tensor_scan(flat(xa[:, :, :]), g.keep[:, :], dec[:, :], 0.0, ALU.mult, ALU.add)
                    dve.drain()
                    dve.tensor_tensor(flat(xb[:, :, :]), flat(xa[:, :, :]), dec[:, :], ALU.subtract).then_inc(s["a_scan"], 1)
                    dve.wait_ge(s["a_evac"], 9)
                    dve.tensor_scalar(tmp, bon[:, :], -1.0, dyn(g.prm, j + PC["k_a"]), ALU.add, ALU.mult)
                    dve.drain()
                    dve.scalar_tensor_tensor(out=k, in0=tmp, scalar=1.0, in1=k, op0=ALU.add, op1=ALU.mult)
                    for n, (a, w) in enumerate(CHUNKS):
                        dve.wait_ge(s["a_ss"], n + 1)
                        dve.tensor_scalar(norm[:, a:a + w], bank[6 + n % 2][:, 0:w], 1e-24, None, ALU.max).then_inc(s["a_max"], 1)
                    if last is not None:
                        dve.wait_ge(s["c_outs"], 32)
                    shifted(2, "mu_v", v, 12)
                    dve.wait_ge(s["a_root"], 1)
                    dve.reciprocal(norm, norm)
                    dve.drain()
                    dve.tensor_tensor(kk, kk, norm, ALU.mult)
                    dve.drain()
                    dve.tensor_tensor(spare, kk, bon[:, :], ALU.mult)
                    dve.wait_ge(s["a_exp"], 1)
                    c3 = lambda x: x.rearrange("p (c t) -> p c t", c=NCH)
                    dve.scalar_tensor_tensor(out=ar[:, :, 0, :], in0=c3(kk), scalar=-1.0, in1=gain_before, op0=ALU.mult, op1=ALU.mult)
                    dve.tensor_tensor(bk[:, :, 1, :], c3(k), gain_inv, ALU.mult)
                    dve.drain()
                    dve.tensor_tensor(bk[:, :, 0, :], c3(spare), gain_inv, ALU.mult)
                    shifted(0, "mu_r", r, 15)
                    dve.scalar_tensor_tensor(out=tmp, in0=r, scalar=dyn(g.prm, j + PC["r_k"]), in1=k,
                                             op0=ALU.mult, op1=ALU.mult).then_inc(s["a_rkr"], 1)
                    dve.tensor_tensor(ar[:, :, 1, :], c3(r), gain, ALU.mult)
                    for n, (a, w) in enumerate(CHUNKS):
                        dve.wait_ge(s["a_bn"], n + 1)
                        dve.tensor_tensor(bon[:, a:a + w], bank[(6, 7, 0)[n]][:, 0:w], v[:, a:a + w], ALU.mult)

        def recur_pair(j):
            SUBS = [[(0, 5), (5, 5)], [(10, 4), (14, 3)]]
            FIRST = 10
            PARTS = 28
            BV = [(0, 8, 22), (8, 8, 24), (16, 1, 26)]
            YG = {7: (0, 2), 15: (8, 3), NC: (NC, 6)}
            kind_of = lambda k: ("z", "x", "t")[k % 6 // 2]
            done = lambda grp, k: 10 * grp + 2 * (k // 6) + k % 2 + 1
            done_t = lambda grp, k: 8 * grp + 2 * (k // 6) + k % 2 + 1
            hs = lambda hh: slice(64 * hh, 64 * hh + 64)
            both = lambda x: x.rearrange("p a t -> p (a t)")
            with nc.Block() as block:
                yT = xb

                @block.tensor
                def _(pe):
                    def inverse_part(grp, k):
                        lv, sub = k // 6, k % 2
                        c0, m = SUBS[grp][sub]
                        kind = kind_of(k)
                        if kind == "z":
                            if lv == 0:
                                pe.wait_ge(s["b_init"], 2 * grp + sub + 1)
                            else:
                                pe.wait_ge(s["b_xev"], done(grp, k - 6))
                                pe.wait_ge(s["b_tev"], done_t(grp, k - 6))
                        elif kind == "x":
                            pe.wait_ge(s["b_zev"], done(grp, k))
                            if lv == 0 and grp:
                                pe.wait_ge(s["b_xev"], done(0, 24 + sub))
                        for c in range(c0, c0 + m):
                            for hh in range(2):
                                o = (c - c0) * CW
                                if kind == "z":
                                    mm = pe.matmul(bank[4 + sub][hs(hh), o:o + CW], alow[hs(hh), c, :], xa[hs(hh), c, :], start=True, stop=True)
                                elif kind == "x":
                                    mm = pe.matmul(bank[6 + sub][hs(hh), o:o + CW], xb[hs(hh), c, :], zb[hs(hh), c, :], start=True, stop=True)
                                else:
                                    mm = pe.matmul(bank[4 + sub][hs(hh), o:o + CW], zb[hs(hh), c, :], xb[hs(hh), c, :], start=True, stop=True)
                        mm.then_inc(s["b_" + kind], 1)

                    def pair_products(q, i):
                        if q:
                            if i < 2:
                                pe.wait_ge(s["b_gm"], 2 * q - 1 + i)
                            else:
                                pe.wait_ge(s["b_copy"], 2 * q - 3 + i)
                        for c in range(4 * q, min(4 * q + 4, NCH)):
                            o = slice(128 * (c - 4 * q), 128 * (c - 4 * q) + 128)
                            if i < 2:
                                mm = pe.matmul(bank[i][:, o], bk[hs(i), c, :, :], ar[hs(i), c, :, :], start=True, stop=True)
                            elif i == 2:
                                mm = pe.transpose(bank[2][:, o], both(bk[:, c, :, :]), g.ident[:, :])
                            else:
                                mm = pe.matmul(bank[3][64:128, o], v[:, c * CW:c * CW + CW], g.ident[:, :], start=True, stop=True)
                        mm.then_inc(s["b_job"], 1)

                    def step_rhs(c):
                        if c < NC:
                            pe.wait_ge(s["c_sev"], c + 1)
                        else:
                            pe.wait_ge(s["c_wev"], 1)
                            pe.wait_ge(s["c_sev"], NC + 1)
                        for hh in range(2):
                            if c < NC:
                                mm = pe.matmul(bank[0][hs(hh), 0:E], ar[hs(hh), c, 0, :], st[hs(hh), c % 2, :], start=True, stop=True)
                            else:
                                mm = pe.matmul(bank[0][hs(hh), 0:E], w0s[hs(hh), 0, :, :], g.ident[hs(hh), hs(hh)], start=True, stop=True)
                        mm.then_inc(s["c_rhs"], 1)

                    def step_u(c):
                        pe.wait_ge(s["c_rhsev"], c + 1)
                        for hh in range(2):
                            mm = pe.matmul(bank[hh][0:64, 0:E], xa[hs(hh), c, :], rhs[hs(hh), :], start=True, stop=True)
                        mm.then_inc(s["c_u"], 1)

                    def step_state(c):
                        pe.wait_ge(s["c_uev"], c + 1)
                        pe.wait_ge(s["c_uev1"], c + 1)
                        if c < NC:
                            for hh in range(2):
                                mm = pe.matmul(bank[0][hs(hh), 0:E], bkt[:, c, hh, :], uv[:, c, hh, :], start=True, stop=True)
                            mm.then_inc(s["c_s"], 1)
                        o0 = (c % 8) * CW
                        yb = bank[2 + c // 8] if c < NC else bank[6]
                        for hh in range(2):
                            o = yb[hs(hh), o0:o0 + CW]
                            pe.matmul(o, uv[:, c, hh, :], gm[:, c, hh, CW:128], start=True, stop=False)
                            if c < NC:
                                mm = pe.matmul(o, st[hs(hh), c % 2, :], ar[hs(hh), c, 1, :], start=False, stop=True)
                            else:
                                mm = pe.matmul(o, g.ident[hs(hh), hs(hh)], w0s[hs(hh), 1, :, :], start=False, stop=True)
                        mm.then_inc(s["c_y"], 1)

                    for n, (c0, m) in enumerate(SUBS[0] + SUBS[1]):
                        ba, bm = bank[(4, 5, 2, 0)[n]], bank[(6, 7, 3, 1)[n]]
                        for c in range(c0, c0 + m):
                            for hh in range(2):
                                o = (c - c0) * CW
                                pe.matmul(ba[hs(hh), o:o + CW], ar[hs(hh), c, 0, :], bk[hs(hh), c, 0, :], start=True, stop=True)
                                mm = pe.matmul(bm[hs(hh), o:o + CW], bk[hs(hh), c, 0, :], ar[hs(hh), c, 0, :], start=True, stop=True)
                        mm.then_inc(s["b_am"], 1)
                    for step in range(PARTS):
                        inverse_part(0, step)
                        if step < 20:
                            if step == 0:
                                pe.wait_ge(s["b_init"], 4)
                            pair_products(step // 4, step % 4)
                        for n, (c0, m, at) in enumerate(BV):
                            if step == at:
                                pe.wait_ge(s["b_gm"], 10)
                                pe.wait_ge(s["b_copy"], 10)
                                for c in range(c0, c0 + m):
                                    for hh in range(2):
                                        o = (c - c0) * CW
                                        mm = pe.matmul(bank[n][hs(hh), o:o + CW], gm[64:128, c, hh, 0:CW], uv[64:128, c, hh, :], start=True, stop=True)
                                mm.then_inc(s["b_bvmm"], 1)
                    pe.wait_ge(s["b_bv"], 3)
                    pe.wait_ge(s["b_xev"], 10)
                    for c in range(FIRST):
                        step_rhs(c)
                        if 3 * c < PARTS:
                            inverse_part(1, 3 * c)
                        step_u(c)
                        if 3 * c + 1 < PARTS:
                            inverse_part(1, 3 * c + 1)
                        step_state(c)
                        if 3 * c + 2 < PARTS:
                            inverse_part(1, 3 * c + 2)
                    pe.wait_ge(s["b_xev"], 20)
                    for b in range(NB):
                        for hh in range(2):
                            mm = pe.matmul(bank[7][hs(hh), 16 * b:16 * b + 16], s0[hs(hh), b, :],
                                           ar[hs(hh), NC, :, NT * b:NT * b + NT], start=True, stop=True)
                    mm.then_inc(s["c_w"], 1)
                    for c in range(FIRST, NCH):
                        step_rhs(c)
                        step_u(c)
                        step_state(c)
                    pe.wait_ge(s["c_um"], 1)
                    for hh in range(2):
                        mm = pe.matmul(bank[7][hs(hh), :], bkt[:, NC, hh, :], uvm[:, hh, :, :], start=True, stop=True)
                    mm.then_inc(s["c_s"], 1)

                @block.scalar
                def _(act):
                    for q in range(5):
                        c0, c1 = 4 * q, min(4 * q + 4, NCH)
                        act.wait_ge(s["b_job"], 4 * q + 3)
                        act.activation(bkt[:, c0:c1, :, :].rearrange("p c h e -> p (c h e)"), bank[2][:, 0:128 * (c1 - c0)], ACT.Copy).then_inc(s["b_copy"], 1)
                        act.wait_ge(s["b_job"], 4 * q + 4)
                        act.activation(uv[64:128, c0:c1, :, :].rearrange("p c h e -> p (c h e)"), bank[3][64:128, 0:128 * (c1 - c0)], ACT.Copy).then_inc(s["b_copy"], 1)
                    for n, (c0, m, _at) in enumerate(BV):
                        act.wait_ge(s["b_bvmm"], n + 1)
                        act.activation(bv[:, c0:c0 + m, :], bank[n][:, 0:m * CW].rearrange("p (c x) -> p c x", c=m), ACT.Copy).then_inc(s["b_bv"], 1)
                    for c in range(NCH):
                        if c == FIRST:
                            act.wait_ge(s["c_w"], 1)
                            act.activation(w0s[:, :, :, :].rearrange("p a b t -> p b a t"),
                                           bank[7][:, 0:128].rearrange("p (b a t) -> p b a t", b=NB, a=2), ACT.Copy).then_inc(s["c_wev"], 1)
                        act.wait_ge(s["c_u"], c + 1)
                        act.activation(uv[0:64, c, 0, :], bank[0][0:64, 0:E], ACT.Copy).then_inc(s["c_uev"], 1)
                        if c in YG:
                            c0, n = YG[c]
                            act.wait_ge(s["c_y"], c + 1)
                            act.activation(flat(yT[:, c0:c + 1, :]), bank[n][:, 0:(c + 1 - c0) * CW], ACT.Copy)

                @block.vector
                def _(dve):
                    def br(m, n):
                        return m.unsqueeze(1).broadcast_to([128, n, m.shape[-1]])

                    def b3(b, m):
                        return b[:, 0:m * CW].rearrange("p (c t) -> p c t", c=m)

                    def inverse_out(grp, k):
                        lv, sub = k // 6, k % 2
                        c0, m = SUBS[grp][sub]
                        kind = kind_of(k)
                        if kind == "z":
                            dve.wait_ge(s["b_z"], done(grp, k))
                            dve.tensor_tensor(zb[:, c0:c0 + m, :], b3(bank[4 + sub], m), br(g.m_level[:, lv + 1 if lv < 4 else 6, :], m), ALU.mult).then_inc(s["b_zev"], 1)
                        elif kind == "x":
                            dve.wait_ge(s["b_x"], done(grp, k))
                            dve.tensor_tensor(xa[:, c0:c0 + m, :], xa[:, c0:c0 + m, :], b3(bank[6 + sub], m), ALU.add).then_inc(s["b_xev"], 1)
                        else:
                            dve.wait_ge(s["b_t"], done_t(grp, k))
                            dve.tensor_tensor(xb[:, c0:c0 + m, :], xb[:, c0:c0 + m, :], b3(bank[4 + sub], m), ALU.add).then_inc(s["b_tev"], 1)

                    gat = lambda c: gain[:, c, CW - 1:CW]

                    def out_rhs(c):
                        dve.wait_ge(s["c_rhs"], c + 1)
                        dve.tensor_tensor(rhs[:, :], bank[0][:, 0:E], bv[:, c, :], ALU.add).then_inc(s["c_rhsev"], 1)
                        if c < NC:
                            dve.tensor_scalar(sdec[:, :], st[:, c % 2, :], gat(c), None, ALU.mult)

                    def out_u(c):
                        dve.wait_ge(s["c_u"], c + 1)
                        dve.tensor_copy(uv[0:64, c, 1, :], bank[1][0:64, 0:E]).then_inc(s["c_uev1"], 1)

                    def out_state(c):
                        dve.drain()
                        dve.wait_ge(s["c_s"], c + 1)
                        if c >= 1:
                            dve.wait_ge(s["c_y"], c)
                        dve.scalar_tensor_tensor(out=st[:, (c + 1) % 2, :], in0=bank[0][:, 0:E], scalar=gat(c), in1=sdec[:, :],
                                                 op0=ALU.mult, op1=ALU.add).then_inc(s["c_sev"], 1)
                        dve.drain()

                    for n, (c0, m) in enumerate(SUBS[0] + SUBS[1]):
                        dve.wait_ge(s["b_am"], n + 1)
                        ba, bm = bank[(4, 5, 2, 0)[n]], bank[(6, 7, 3, 1)[n]]
                        mp = m if c0 + m <= NC else m - 1
                        dve.tensor_tensor(alow[:, c0:c0 + mp, :], b3(ba, mp), br(g.m_low[:, 0, :], mp), ALU.mult)
                        if mp < m:
                            dve.tensor_tensor(alow[:, NC, :], ba[:, mp * CW:m * CW], g.m_low[:, 1, :], ALU.mult)
                        dve.tensor_tensor(xb[:, c0:c0 + m, :], b3(ba, m), br(g.m_level[:, 5, :], m), ALU.mult)
                        dve.tensor_tensor(xa[:, c0:c0 + m, :], b3(bm, m), br(g.m_level[:, 0, :], m), ALU.mult)
                        dve.drain()
                        dve.tensor_tensor(xb[:, c0:c0 + m, :], xb[:, c0:c0 + m, :], br(g.m_eye[:, :], m), ALU.add)
                        dve.tensor_tensor(xa[:, c0:c0 + m, :], xa[:, c0:c0 + m, :], br(g.m_eye[:, :], m), ALU.add).then_inc(s["b_init"], 1)
                    dve.memset(st[:, 0, :], 0.0).then_inc(s["c_sev"], 1)
                    for step in range(PARTS):
                        inverse_out(0, step)
                        if step < 20 and step % 4 < 2:
                            q, hh = step // 4, step % 4
                            dve.wait_ge(s["b_job"], step + 1)
                            c0, c1 = 4 * q, min(4 * q + 4, NCH)
                            dve.tensor_tensor(gm[:, c0:c1, hh, :], bank[hh][:, 0:128 * (c1 - c0)].rearrange("p (c x) -> p c x", c=c1 - c0),
                                              br(g.m_pair[:, 0 if c1 <= NC else 1, :], c1 - c0), ALU.mult).then_inc(s["b_gm"], 1)
                    dve.drain()
                    dve.wait_ge(s["b_bv"], 3)
                    for c in range(FIRST):
                        out_rhs(c)
                        if 3 * c < PARTS:
                            inverse_out(1, 3 * c)
                        out_u(c)
                        if 3 * c + 1 < PARTS:
                            inverse_out(1, 3 * c + 1)
                        out_state(c)
                        if 3 * c + 2 < PARTS:
                            inverse_out(1, 3 * c + 2)
                    for c in range(FIRST, NC):
                        out_rhs(c)
                        out_u(c)
                        out_state(c)
                    out_rhs(NC)
                    out_u(NC)
                    dve.drain()
                    dve.wait_ge(s["c_uev"], NCH)
                    for hh in range(2):
                        last = dve.tensor_tensor(uvm[:, hh, :, :], uv[:, NC, hh, :].unsqueeze(1).broadcast_to([128, NB, E]),
                                                 g.m_seq[:, :].unsqueeze(2).broadcast_to([128, NB, E]), ALU.mult)
                    last.then_inc(s["c_um"], 1)
                    dve.wait_ge(s["c_s"], NCH)
                    dve.tensor_tensor(sn[:, :, :], bank[7][:, :].rearrange("p (b e) -> p b e", b=NB), s0[:, :, :], ALU.add)
                    dve.drain()
                    gs = gain[:, NC, :].rearrange("p (b t) -> p b t", b=NB)[:, :, NT - 1:NT]
                    dve.tensor_tensor(sn[:, :, :], sn[:, :, :], gs.broadcast_to([128, NB, E]), ALU.mult).then_inc(s["d_in"], 1)

                @block.sync
                def _(sp):
                    load_w3(sp, j * 128 + 128, s["w3_loaded"])
                    sp.wait_ge(s["c_sev"], NCH)
                    sp.dma_start(g.o_pwkv[bass.ds(j * 128, 128), :], st[:, NC % 2, :]).then_inc(s["c_outs"], 16)
                    sp.wait_ge(s["d_in"], 1)
                    sp.dma_start(g.o_swkv[bass.ds(j * 128, 128), :], sn[:, :, :].rearrange("p b v -> p (b v)")).then_inc(s["c_outs"], 16)
                    sp.wait_ge(s["w3_loaded"], 48)

        project_pair(0, None)
        with nc.Fori(0, J - 1) as j:
            clear_counts()
            recur_pair(j)
            project_pair(j + 1, j)
        clear_counts()
        recur_pair(J - 1)
        with nc.Block() as block:
            @block.sync
            def _(sp):
                sp.wait_ge(s["c_outs"], 32)

            @block.tensor
            def _(pe):
                norm_means(pe)
                norm_variances(pe)

            @block.scalar
            def _(act):
                norm_squares(act)
                norm_roots(act)

            @block.vector
            def _(dve):
                norm_outputs(dve, J - 1)


SCALE = E ** -0.5
NSEL = 1280
KB = NSEL // 128


def attention(nc, g):
    with ExitStack() as ctx:
        sb = lambda n, s: ctx.enter_context(nc.sbuf_tensor(n, s, f32))
        sem = g.semaphores(nc, ctx)
        bank = g.bank
        cos, sin = sb("cos", [128, T]), sb("sin", [128, T])
        rot, count = sb("rot", [128, 128]), sb("count", [128, S])
        w3 = sb("wqkv", [128, KD, 3, 128])
        raw = [sb("qraw", [128, T]), sb("kraw", [128, T])]
        qz = [sb(f"qrot{hh}", [128, T]) for hh in range(2)]
        krot = sb("krot", [128, T])
        turned = sb("turned", [128, T])
        vt = sb("vt", [128, TT, 128])
        score = sb("score", [128, 2, S])
        pT = sb("pT", [128, 2, 8, 128])
        top = sb("top", [128, 4])
        ntop, total, rtotal = sb("ntop", [128, 2]), sb("total", [128, 4]), sb("rtotal", [128, 2])
        names = ("q_w q_mm q_ev q_rot q_done v_mm v_ev q_outs kept "
                 "s_qk s_neg s_exp s_tr s_tev0 s_tev1 s_pv s_norm").split()
        s = {n: sem(n) for n in names}
        tables = sem("tables")
        VJ = [(0, 4), (4, 4), (8, 1)]

        def load_w3(sp, col, loaded):
            for i in range(3):
                sp.dma_start(w3[:, :, i, :], g.d_win.rearrange("(k p) n -> p k n", p=128)[:, :, bass.ds(col + (RP + RW * i), 128)]).then_inc(loaded, 16)

        g.new += g.k_in
        g.clear(nc)
        with nc.Block() as block:
            @block.sync
            def _(sp):
                for dst, src in ((cos, g.d_cos), (sin, g.d_sin), (rot, g.d_rot), (count, g.d_count)):
                    sp.dma_start(dst[:, :], src).then_inc(tables, 16)
                load_w3(sp, 0, s["q_w"])
                for b in range(2):
                    sp.dma_start(g.kc[b][:, :, :], g.d_kcT[b].rearrange("(j p) n -> p j n", p=128)).then_inc(g.k_in[b], 16)
                sp.wait_ge(tables, 64)
                sp.wait_ge(s["q_w"], 48)

            @block.vector
            def _(dve):
                for hh in range(2):
                    dve.memset(qz[hh][64 - 64 * hh:128 - 64 * hh, :], 0.0)

        with nc.Fori(0, J) as j:
            with nc.Block() as block:
                @block.gpsimd
                def _(pool):
                    for semaphore in s.values():
                        pool.sem_clear(semaphore)

            with nc.Block() as block:
                @block.sync
                def _(sp):
                    sp.wait_ge(s["q_done"], 2)
                    sp.dma_start(g.o_kT[bass.ds(j * 128, 128), :], krot[:, :]).then_inc(s["q_outs"], 16)
                    sp.wait_ge(s["v_ev"], 3)
                    sp.dma_start(g.o_v[0:S, :].rearrange("(t p) c -> p t c", p=128)[:, :, bass.ds(j * 128, 128)],
                                 vt[:, 0:8, :]).then_inc(s["q_outs"], 16)
                    sp.dma_start(g.o_v[S:T, bass.ds(j * 128, 128)], vt[0:64, 8, :]).then_inc(s["q_outs"], 16)
                    sp.wait_ge(s["q_outs"], 48)

                @block.tensor
                def _(pe):
                    for i in range(2):
                        for n, (a, w) in enumerate(CHUNKS):
                            for k in range(KD):
                                mm = pe.matmul(bank[3 * i + n][:, 0:w], w3[:, k, i, :], g.uT[:, k, a:a + w],
                                               start=(k == 0), stop=(k == KD - 1))
                            mm.then_inc(s["q_mm"], 1)
                    for n, (t0, m) in enumerate(VJ):
                        if n < 2:
                            for c, (a, w) in enumerate(CHUNKS):
                                pe.wait_ge(s["q_ev"], 3 * n + c + 1)
                                pe.matmul(bank[3 * n + c][:, 0:w], rot[:, :], raw[n][:, a:a + w], start=True, stop=True).then_inc(s["q_rot"], 1)
                        if n == 2:
                            pe.wait_ge(s["v_ev"], 1)
                        for t in range(t0, t0 + m):
                            rows = min(128, T - 128 * t)
                            for k in range(KD):
                                mm = pe.matmul(bank[6 + n % 2][0:rows, 128 * (t - t0):128 * (t - t0) + 128],
                                               g.uT[:, k, 128 * t:128 * t + rows], w3[:, k, 2, :], start=(k == 0), stop=(k == KD - 1))
                        mm.then_inc(s["v_mm"], 1)

                @block.scalar
                def _(act):
                    for i in range(2):
                        for n, (a, w) in enumerate(CHUNKS):
                            act.wait_ge(s["q_mm"], 3 * i + n + 1)
                            act.activation(raw[i][:, a:a + w], bank[3 * i + n][:, 0:w], ACT.Copy).then_inc(s["q_ev"], 1)
                    for n, (t0, m) in enumerate(VJ):
                        act.wait_ge(s["v_mm"], n + 1)
                        rows = 128 if n < 2 else 64
                        act.activation(vt[0:rows, t0:t0 + m, :].rearrange("p t c -> p (t c)"), bank[6 + n % 2][0:rows, 0:128 * m],
                                       ACT.Copy).then_inc(s["v_ev"], 1)
                    act.drain()
                    act.activation(g.vs[0:TS, bass.ds(j, 1), :].rearrange("p o c -> p (o c)"), vt[0:64, 8, :], ACT.Copy)

                @block.vector
                def _(dve):
                    for i in range(2):
                        for n, (a, w) in enumerate(CHUNKS):
                            dve.wait_ge(s["q_rot"], 3 * i + n + 1)
                            dve.tensor_tensor(turned[:, a:a + w], bank[3 * i + n][:, 0:w], sin[:, a:a + w], ALU.mult)
                        dve.tensor_tensor(raw[i][:, :], raw[i][:, :], cos[:, :], ALU.mult)
                        dve.drain()
                        if i == 0:
                            for hh in range(2):
                                h = slice(64 * hh, 64 * hh + 64)
                                last = dve.tensor_tensor(qz[hh][h, :], raw[0][h, :], turned[h, :], ALU.add)
                            last.then_inc(s["q_done"], 1)
                            dve.drain()
                            for hh in range(2):
                                h = slice(64 * hh, 64 * hh + 64)
                                dve.tensor_copy(g.qs[h, bass.ds(j, 1), :].rearrange("p o c -> p (o c)"), qz[hh][h, S:T])
                        else:
                            dve.tensor_tensor(krot[:, :], raw[1][:, :], turned[:, :], ALU.add).then_inc(s["q_done"], 1)
                            dve.drain()
                            dve.tensor_copy(g.ks[:, bass.ds(j, 1), :].rearrange("p o c -> p (o c)"), krot[:, S:T])

            units = [(i, hh) for i in range(8) for hh in range(2)]
            groups = []
            for u, (i, hh) in enumerate(units):
                groups += [(u, 0, min(4, i + 1))] + ([(u, 4, i - 3)] if i >= 4 else [])
            of = [[x for x, gr in enumerate(groups) if gr[0] == u] for u in range(len(units))]
            last_by = lambda u, e: sum(1 for x in range(of[u][-1] + 1) if x % 2 == e)

            with nc.Block() as block:
                @block.sync
                def _(sp):
                    load_w3(sp, j * 128 + 128, s["q_w"])
                    sp.wait_ge(s["q_w"], 48)

                @block.tensor
                def _(pe):
                    def scores(u):
                        i, hh = units[u]
                        if u >= 2:
                            pe.wait_ge(s["s_neg"], u - 1)
                        for b in range(1 + (i >= 4)):
                            w = min(512, 128 * (i + 1) - 512 * b)
                            mm = pe.matmul(bank[2 * hh + b][:, 0:w], qz[hh][:, 128 * i:128 * i + 128], krot[:, 512 * b:512 * b + w],
                                           start=True, stop=True)
                        mm.then_inc(s["s_qk"], 1)

                    def turn(u):
                        pe.wait_ge(s["s_exp"], u + 1)
                        for x in of[u]:
                            if x >= 2:
                                pe.wait_ge(s[f"s_tev{x % 2}"], x // 2)
                            _, b0, m = groups[x]
                            for b in range(b0, b0 + m):
                                mm = pe.transpose(bank[4 + x % 2][:, 128 * (b - b0):128 * (b - b0) + 128],
                                                  score[:, u % 2, 128 * b:128 * b + 128], g.ident[:, :])
                            mm.then_inc(s["s_tr"], 1)

                    def values(u):
                        i, hh = units[u]
                        for e in range(2):
                            if last_by(u, e):
                                pe.wait_ge(s[f"s_tev{e}"], last_by(u, e))
                        if u >= 2:
                            pe.wait_ge(s["s_norm"], u - 1)
                        for b in range(i + 1):
                            mm = pe.matmul(bank[6 + u % 2][:, 0:128], pT[:, u % 2, b, :], vt[:, b, :], start=(b == 0), stop=(b == i))
                        mm.then_inc(s["s_pv"], 1)

                    scores(0)
                    for u in range(len(units)):
                        if u + 1 < len(units):
                            scores(u + 1)
                        turn(u)
                        if u >= 1:
                            values(u - 1)
                    values(len(units) - 1)

                def evacuate(engine, x):
                    u, b0, m = groups[x]
                    engine.wait_ge(s["s_tr"], x + 1)
                    if u >= 2:
                        engine.wait_ge(s["s_pv"], u - 1)
                    out, in_ = pT[:, u % 2, b0:b0 + m, :].rearrange("p b q -> p (b q)"), bank[4 + x % 2][:, 0:128 * m]
                    if engine is nc.vector:
                        engine.tensor_copy(out, in_).then_inc(s["s_tev1"], 1)
                    else:
                        engine.activation(out, in_, ACT.Copy).then_inc(s["s_tev0"], 1)

                @block.scalar
                def _(act):
                    for u, (i, hh) in enumerate(units):
                        act.wait_ge(s["s_neg"], u + 1)
                        n = 128 * (i + 1)
                        act.activation(score[:, u % 2, 0:n], score[:, u % 2, 0:n], ACT.Exp, bias=ntop[:, u % 2:u % 2 + 1],
                                       accum_out=total[:, u % 4:u % 4 + 1]).then_inc(s["s_exp"], 1)
                        for x in of[u]:
                            if x % 2 == 0:
                                evacuate(nc.scalar, x)

                @block.vector
                def _(dve):
                    def soften(u):
                        i, hh = units[u]
                        dve.wait_ge(s["s_qk"], u + 1)
                        if u >= 2:
                            dve.wait_ge(s["s_tr"], of[u - 2][-1] + 1)
                        n = 128 * (i + 1)
                        for b in range(1 + (i >= 4)):
                            w = min(512, n - 512 * b)
                            acc = top[:, 2 * (u % 2) + b:2 * (u % 2) + b + 1]
                            dve.tensor_tensor_reduce(out=score[:, u % 2, 512 * b:512 * b + w], in0=bank[2 * hh + b][:, 0:w],
                                                     in1=count[:, S - n + 512 * b:S - n + 512 * b + w], scale=SCALE, scalar=-3e38,
                                                     op0=ALU.add, op1=ALU.max, accum_out=acc)
                        dve.drain()
                        if i >= 4:
                            dve.tensor_scalar(ntop[:, u % 2:u % 2 + 1], top[:, 2 * (u % 2):2 * (u % 2) + 1], top[:, 2 * (u % 2) + 1:2 * (u % 2) + 2], -1.0, ALU.max, ALU.mult).then_inc(s["s_neg"], 1)
                        else:
                            dve.tensor_scalar(ntop[:, u % 2:u % 2 + 1], top[:, 2 * (u % 2):2 * (u % 2) + 1], -1.0, None, ALU.mult).then_inc(s["s_neg"], 1)

                    def finish(u):
                        i, hh = units[u]
                        dve.wait_ge(s["s_exp"], u + 1)
                        dve.reciprocal(rtotal[:, u % 2:u % 2 + 1], total[:, u % 4:u % 4 + 1])
                        dve.drain()
                        dve.wait_ge(s["s_pv"], u + 1)
                        dve.tensor_scalar(g.att[:, i, bass.ds(j * 128 + 64 * hh, E)], bank[6 + u % 2][:, 64 * hh:64 * hh + 64],
                                          rtotal[:, u % 2:u % 2 + 1], None, ALU.mult).then_inc(s["s_norm"], 1)

                    soften(0)
                    for u in range(len(units)):
                        if u + 1 < len(units):
                            soften(u + 1)
                        for x in of[u]:
                            if x % 2:
                                evacuate(nc.vector, x)
                        if u >= 1:
                            finish(u - 1)
                    finish(len(units) - 1)


def decode_attention(nc, g):
    with ExitStack() as ctx:
        sb = lambda n, s: ctx.enter_context(nc.sbuf_tensor(n, s, f32))
        sem = g.semaphores(nc, ctx)
        bank = g.bank
        HT = H * NT
        PAIRS = NB // 2
        OWN = NSEL
        CUTS = [(0, 512), (512, 512), (1024, NSEL - 1024)]
        TURNS = [(0, 4), (4, 4), (8, 3)]
        kc = g.kc + [g.h[:, :, :].rearrange("p t d -> p (t d)")[:, 0:J * NSEL].rearrange("p (j n) -> p j n", j=J)]
        NK = len(kc)
        vc = [sb(f"vc{i}", [128, KB, RW]) for i in range(2)]
        mcache, mnew = sb("mcache", [128, NSEL]), sb("mnew", [128, PAIRS, TS])
        heads, own_row = sb("own_head", [128, RW]), sb("own_row", [128, PAIRS, TS])
        qd = sb("qd", [128, J, NB, HT])
        score = [sb(f"dscore{i}", [128, NSEL + 128]) for i in range(2)]
        eT = sb("eT", [128, KB + 1, 128])
        top, ntop = sb("dtop", [128, 4]), sb("dntop", [128, 1])
        total, rtotal = sb("dtotal", [128, 2]), sb("drtotal", [128, 2])
        picked = sb("picked", [128, PAIRS, RW])
        k_in = g.k_in + [sem("k_in2")]
        v_in = [sem(f"v_in{i}") for i in range(2)]
        names = "masks_in qd_done scored raised exped turned0 turned1 turned2 tev valued picks summed"
        masks_in, qd_done, scored, raised, exped, turned0, turned1, turned2, tev, valued, picks, summed = (sem(n) for n in names.split())
        turned = [turned0, turned1, turned2]

        g.clear(nc)
        with nc.Block() as block:
            @block.sync
            def _(sp):
                sp.dma_start(mcache[:, :], g.d_mcache).then_inc(masks_in, 16)
                sp.dma_start(mnew[:, :, :], g.d_mnew).then_inc(masks_in, 16)
                sp.dma_start(heads[:, :], g.d_own_head).then_inc(masks_in, 16)
                sp.dma_start(own_row[:, :, :], g.d_own_row).then_inc(masks_in, 16)

                def keys(b):
                    if b >= NK:
                        sp.wait_ge(scored, b - NK + 1)
                    sp.dma_start(kc[b % NK][:, :, :], g.d_kcT[b].rearrange("(j p) n -> p j n", p=128)).then_inc(k_in[b % NK], 16)

                def values(b):
                    if b >= 2:
                        sp.wait_ge(valued, b - 1)
                    sp.dma_start(vc[b % 2][:, :, :], g.d_vc[b].rearrange("(k p) c -> p k c", p=128)).then_inc(v_in[b % 2], 16)

                keys(2)
                values(0)
                keys(3)
                values(1)
                for b in range(2, NB):
                    if b + 2 < NB:
                        keys(b + 2)
                    values(b)

            @block.tensor
            def _(pe):
                def scores(pair):
                    if pair >= 1:
                        pe.wait_ge(raised, pair)
                    for b in (2 * pair, 2 * pair + 1):
                        rows = slice(HT * (b % 2), HT * (b % 2) + HT)
                        pe.wait_ge(k_in[b % NK], 16 * (b // NK + 1))
                        for n, (a, w) in enumerate(CUTS):
                            for j in range(J):
                                pe.matmul(bank[n][rows, 0:w], qd[:, j, b, :], kc[b % NK][:, j, a:a + w], start=(j == 0), stop=(j == J - 1))
                        for j in range(J):
                            mm = pe.matmul(bank[2][rows, NSEL - 1024:NSEL - 1024 + TS], qd[:, j, b, :], g.ks[:, j, :],
                                           start=(j == 0), stop=(j == J - 1))
                        mm.then_inc(scored, 1)

                def turn(pair):
                    pe.wait_ge(exped, pair + 1)
                    if pair >= 1:
                        pe.wait_ge(tev, 3 * pair)
                    for n, (k0, m) in enumerate(TURNS):
                        for k in range(k0, k0 + m):
                            mm = pe.transpose(bank[3 + n][:, 128 * (k - k0):128 * (k - k0) + 128], score[pair % 2][:, 128 * k:128 * k + 128], g.ident[:, :])
                        mm.then_inc(turned[n], 1)

                def gather(pair):
                    pe.wait_ge(tev, 3 * pair + 3)
                    if pair >= 2:
                        pe.wait_ge(picks, pair - 1)
                    for b in (2 * pair, 2 * pair + 1):
                        rows = slice(HT * (b % 2), HT * (b % 2) + HT)
                        pe.wait_ge(v_in[b % 2], 16 * (b // 2 + 1))
                        for k in range(KB):
                            pe.matmul(bank[6 + pair % 2][rows, :], eT[:, k, rows], vc[b % 2][:, k, :], start=(k == 0), stop=False)
                        pe.matmul(bank[6 + pair % 2][rows, :], eT[:, KB, rows], g.vs[:, :, :].rearrange("p j c -> p (j c)"),
                                  start=False, stop=True).then_inc(valued, 1)

                pe.wait_ge(qd_done, 1)
                scores(0)
                turn(0)
                for pair in range(PAIRS):
                    if pair + 1 < PAIRS:
                        scores(pair + 1)
                    gather(pair)
                    if pair + 1 < PAIRS:
                        turn(pair + 1)
                pe.wait_ge(masks_in, 64)
                for pair in range(PAIRS):
                    pe.wait_ge(picks, pair + 1)
                    mm = pe.matmul(bank[0][0:TS, :], own_row[:, pair, :], picked[:, pair, :], start=(pair == 0), stop=(pair == PAIRS - 1))
                mm.then_inc(summed, 1)

            @block.scalar
            def _(act):
                for pair in range(PAIRS):
                    act.wait_ge(raised, pair + 1)
                    act.activation(score[pair % 2][:, 0:NSEL + TS], score[pair % 2][:, 0:NSEL + TS], ACT.Exp, bias=ntop[:, 0:1],
                                   accum_out=total[:, pair % 2:pair % 2 + 1]).then_inc(exped, 1)
                    if pair >= 1:
                        act.wait_ge(valued, 2 * pair)
                    for n, (k0, m) in enumerate(TURNS):
                        act.wait_ge(turned[n], pair + 1)
                        act.activation(eT[:, k0:k0 + m, :].rearrange("p k q -> p (k q)"), bank[3 + n][:, 0:128 * m], ACT.Copy).then_inc(tev, 1)

            @block.vector
            def _(dve):
                dve.memset(g.att[:, TT - 1, :], 0.0)
                dve.memset(g.vs[TS:128, :, :], 0.0)
                for i in range(2):
                    dve.memset(score[i][:, NSEL + TS:NSEL + 128], 0.0)
                dve.memset(qd[:, :, :, :], 0.0)
                dve.drain()
                for hh in range(2):
                    h = slice(64 * hh, 64 * hh + 64)
                    for j in range(J):
                        o = NT * (2 * j + hh)
                        last = dve.tensor_copy(qd[h, j, :, o:o + NT], g.qs[h, j, :].rearrange("p (b t) -> p b t", b=NB))
                last.then_inc(qd_done, 1)
                dve.wait_ge(masks_in, 64)

                def soften(pair):
                    dve.wait_ge(scored, 2 * pair + 2)
                    if pair >= 1:
                        dve.wait_ge(exped, pair)
                    if pair >= 2:
                        dve.wait_ge(turned2, pair - 1)
                    parts = [(a, w, bank[n][:, 0:w], mcache[:, a:a + w]) for n, (a, w) in enumerate(CUTS)]
                    parts.append((OWN, TS, bank[2][:, NSEL - 1024:NSEL - 1024 + TS], mnew[:, pair, :]))
                    for n, (a, w, in0, in1) in enumerate(parts):
                        dve.tensor_tensor_reduce(out=score[pair % 2][:, a:a + w], in0=in0, in1=in1, scale=SCALE, scalar=-3e38,
                                                 op0=ALU.add, op1=ALU.max, accum_out=top[:, n:n + 1])
                    dve.drain()
                    dve.tensor_reduce(ntop[:, :], top[:, :], AX.X, ALU.max)
                    dve.drain()
                    dve.tensor_scalar(ntop[:, :], ntop[:, :], -1.0, None, ALU.mult).then_inc(raised, 1)

                def pick(pair):
                    dve.wait_ge(exped, pair + 1)
                    dve.reciprocal(rtotal[:, pair % 2:pair % 2 + 1], total[:, pair % 2:pair % 2 + 1])
                    dve.drain()
                    dve.wait_ge(valued, 2 * pair + 2)
                    dve.scalar_tensor_tensor(out=picked[:, pair, :], in0=bank[6 + pair % 2][:, :], scalar=rtotal[:, pair % 2:pair % 2 + 1],
                                             in1=heads[:, :], op0=ALU.mult, op1=ALU.mult).then_inc(picks, 1)

                soften(0)
                for pair in range(PAIRS):
                    if pair + 1 < PAIRS:
                        soften(pair + 1)
                    pick(pair)
                dve.wait_ge(summed, 1)
                dve.tensor_copy(g.att[0:TS, TT - 1, :], bank[0][0:TS, :])


G, EPG, NE, FF = 4, 8, 32, 256
CAP = 128
PASSES = -(-T // CAP)
SLOTS = PASSES * NE * CAP
BIG = 1e30
WR = 96


def rows_of(t):
    return min(128, T - 128 * t)


def out_projection(nc, g):
    with ExitStack() as ctx:
        sb = lambda n, s: ctx.enter_context(nc.sbuf_tensor(n, s, f32))
        sem = g.semaphores(nc, ctx)
        bank = g.bank
        wo = sb("wo", [128, KD, D])
        attT = sb("attT", [128, J, T])
        junk = sb("ojunk", [128, D])
        ss, rstd = sb("oss", [128, TT]), sb("orstd", [128, TT])
        x_in, w_in, squared, meaned, rooted, scaled, turned, evac, projected, added, zeroed = (
            sem("o_" + n) for n in "x w squared meaned rooted scaled turned evac projected added zeroed".split())
        g.clear(nc)
        with nc.Block() as block:
            @block.sync
            def _(sp):
                for k in range(KD):
                    sp.dma_start(wo[:, k, :], g.d_wout[128 * k:128 * k + 128, :]).then_inc(w_in, 16)
                sp.dma_start(g.h[:, 0:8, :], g.d_x[0:S, :].rearrange("(t p) d -> p t d", p=128)).then_inc(x_in, 16)
                sp.dma_start(g.h[0:TS, 8, :], g.d_x[S:T, :]).then_inc(x_in, 16)

            @block.gpsimd
            def _(pool):
                pool.memset(g.h[64:128, TT - 1, :], 0.0).then_inc(zeroed, 1)

            @block.scalar
            def _(act):
                for t in range(TT):
                    last = act.activation(junk[:, 0:RW], g.att[:, t, :], ACT.Square, accum_out=ss[:, t:t + 1])
                    act.drain()
                last.then_inc(squared, 1)
                act.wait_ge(meaned, 1)
                act.activation(rstd[:, :], rstd[:, :], ACT.Sqrt).then_inc(rooted, 1)
                act.wait_ge(zeroed, 1)
                for t in range(TT):
                    act.wait_ge(added, t + 1)
                    act.activation(junk[:, :], g.h[:, t, :], ACT.Square, accum_out=g.ss[:, t:t + 1])
                    act.drain()

            @block.vector
            def _(dve):
                dve.wait_ge(squared, 1)
                dve.tensor_scalar(rstd[:, :], ss[:, :], 1.0 / RW, RMS_EPS, ALU.mult, ALU.add).then_inc(meaned, 1)
                dve.wait_ge(rooted, 1)
                dve.reciprocal(rstd[:, :], rstd[:, :])
                dve.drain()
                for t in range(TT):
                    dve.tensor_scalar(g.att[:, t, :], g.att[:, t, :], rstd[:, t:t + 1], None, ALU.mult).then_inc(scaled, 1)
                c = PC["attn_norm"]
                for t in range(TT):
                    r = rows_of(t)
                    dve.wait_ge(turned, t + 1)
                    dve.tensor_tensor(attT[:, :, 128 * t:128 * t + r], bank[t % 2][:, :].rearrange("p (j q) -> p j q", j=J)[:, :, 0:r],
                                      g.prm[:, c:c + J].unsqueeze(2).broadcast_to([128, J, r]), ALU.mult).then_inc(evac, 1)
                dve.wait_ge(x_in, 32)
                for t in range(TT):
                    r = rows_of(t)
                    dve.wait_ge(projected, t + 1)
                    for i in range(2):
                        last = dve.tensor_tensor(g.h[0:r, t, 512 * i:512 * i + 512], g.h[0:r, t, 512 * i:512 * i + 512],
                                                 bank[2 + 2 * (t % 3) + i][0:r, :], ALU.add)
                    last.then_inc(added, 1)

            @block.tensor
            def _(pe):
                for t in range(TT):
                    pe.wait_ge(scaled, t + 1)
                    if t >= 2:
                        pe.wait_ge(evac, t - 1)
                    for j in range(J):
                        mm = pe.transpose(bank[t % 2][:, 128 * j:128 * j + 128], g.att[:, t, 128 * j:128 * j + 128], g.ident[:, :])
                    mm.then_inc(turned, 1)
                pe.wait_ge(w_in, 16 * KD)
                pe.wait_ge(evac, TT)
                for t in range(TT):
                    r = rows_of(t)
                    if t >= 3:
                        pe.wait_ge(added, t - 2)
                    for i in range(2):
                        for k in range(KD):
                            lhs = (g.rwT if k < J else attT)[:, k % J, 128 * t:128 * t + r]
                            mm = pe.matmul(bank[2 + 2 * (t % 3) + i][0:r, :], lhs, wo[:, k, 512 * i:512 * i + 512],
                                           start=(k == 0), stop=(k == KD - 1))
                    mm.then_inc(projected, 1)


def route(nc, g):
    with ExitStack() as ctx:
        sb = lambda n, s, d=f32: ctx.enter_context(nc.sbuf_tensor(n, s, d))
        sem = g.semaphores(nc, ctx)
        bank = g.bank
        rstd = sb("rrstd", [128, TT])
        gain = sb("ffn_gain", [128, D])
        wr, br = sb("wr", [128, KD, WR]), sb("br", [128, G + NE])
        xn = sb("xn", [128, 3, D])
        xnT = sb("xnT", [128, 2, KD, 128])
        lg = sb("lg", [128, TT, G + NE])
        upper = sb("upper", [128, 128])
        valid, pad_a = sb("valid", [128, TT]), sb("pad_a", [128, 2, TT])
        w4, w32, i32t = sb("w4", [128, G]), sb("w32", [128, NE]), sb("i32t", [128, NE])
        tok = sb("tok", [128, TT], i32)
        zero = sb("zeros", [128, PASSES * NE + 2], i32)
        pp, pT = sb("pp", [128, 2, D]), sb("ppT", [128, 2, T])
        consts, meaned, rooted, xnorm, turned, evac, logits, lev, zeroed, zero_in = (
            sem("r_" + n) for n in "consts meaned rooted xnorm turned evac logits lev zeroed zero_in".split())
        stored = [sem(f"r_stored{i}") for i in range(3)]
        g.clear(nc)
        with nc.Block() as block:
            @block.sync
            def _(sp):
                loads = ((gain, g.d_ffn_gain), (wr, g.d_wr), (br, g.d_br), (upper, g.d_upper), (valid, g.d_valid),
                         (pad_a, g.d_pad_a), (w4, g.d_w4), (w32, g.d_w32), (i32t, g.d_i32t), (tok, g.d_tok))
                for dst, src in loads:
                    sp.dma_start(dst[tuple([slice(None)] * len(dst.shape))], src).then_inc(consts, 16)
                sp.wait_ge(zeroed, 1)
                sp.dma_start(g.table[0:SLOTS + 256, :].rearrange("(p n) o -> p (n o)", p=128), zero[:, :]).then_inc(zero_in, 16)
                for t in range(TT):
                    sp.wait_ge(xnorm, t + 1)
                    sp.dma_start(g.xn[128 * t:128 * t + 128, :], xn[:, t % 3, :]).then_inc(stored[t % 3], 16)
                sp.dma_start(pp[:, :, :], g.d_pproj.rearrange("(k p) n -> p k n", p=128)).then_inc(zero_in, 16)
                sp.dma_start(pT[:, :, :], g.d_pT.rearrange("(k p) n -> p k n", p=128)).then_inc(zero_in, 16)
                for i in range(3):
                    sp.wait_ge(stored[i], 16 * len(range(i, TT, 3)))
                sp.wait_ge(zero_in, 48)
                sp.wait_ge(consts, 16 * len(loads))

            @block.gpsimd
            def _(pool):
                pool.memset(zero[:, :], 0).then_inc(zeroed, 1)

            @block.vector
            def _(dve):
                def logits_out(t):
                    dve.wait_ge(logits, t + 1)
                    dve.tensor_tensor(lg[:, t, :], bank[4 + t % 2][:, 0:G + NE], br[:, :], ALU.add).then_inc(lev, 1)

                dve.tensor_scalar(rstd[:, :], g.ss[:, :], 1.0 / D, RMS_EPS, ALU.mult, ALU.add).then_inc(meaned, 1)
                dve.wait_ge(rooted, 1)
                dve.reciprocal(rstd[:, :], rstd[:, :])
                dve.drain()
                dve.wait_ge(consts, 160)
                for t in range(TT):
                    if t >= 3:
                        dve.wait_ge(stored[t % 3], 16 * (t // 3))
                        dve.wait_ge(turned, t - 2)
                    dve.scalar_tensor_tensor(out=xn[:, t % 3, :], in0=g.h[:, t, :], scalar=rstd[:, t:t + 1], in1=gain[:, :],
                                             op0=ALU.mult, op1=ALU.mult).then_inc(xnorm, 1)
                    if t >= 2:
                        logits_out(t - 2)
                logits_out(TT - 2)
                logits_out(TT - 1)

            @block.tensor
            def _(pe):
                def turn(t):
                    pe.wait_ge(xnorm, t + 1)
                    if t >= 2:
                        pe.wait_ge(evac, t - 1)
                    for k in range(KD):
                        mm = pe.transpose(bank[2 * (t % 2) + k // 4][:, 128 * (k % 4):128 * (k % 4) + 128],
                                          xn[:, t % 3, 128 * k:128 * k + 128], g.ident[:, :])
                    mm.then_inc(turned, 1)

                turn(0)
                pe.wait_ge(consts, 160)
                for t in range(TT):
                    if t + 1 < TT:
                        turn(t + 1)
                    pe.wait_ge(evac, t + 1)
                    if t >= 2:
                        pe.wait_ge(lev, t - 1)
                    for k in range(KD):
                        mm = pe.matmul(bank[4 + t % 2][:, 0:WR], xnT[:, t % 2, k, :], wr[:, k, :], start=(k == 0), stop=(k == KD - 1))
                    mm.then_inc(logits, 1)

            @block.scalar
            def _(act):
                act.wait_ge(meaned, 1)
                act.activation(rstd[:, :], rstd[:, :], ACT.Sqrt).then_inc(rooted, 1)
                for t in range(TT):
                    act.wait_ge(turned, t + 1)
                    if t >= 2:
                        act.wait_ge(logits, t - 1)
                    for i in range(2):
                        last = act.activation(xnT[:, t % 2, 4 * i:4 * i + 4, :].rearrange("p k q -> p (k q)"), bank[2 * (t % 2) + i][:, :], ACT.Copy)
                    last.then_inc(evac, 1)

        mx, v4, sel = sb("mx", [128, TT]), sb("v4", [128, TT, G]), sb("sel", [128, TT, G])
        le, v32 = sb("le", [128, TT, NE]), sb("v32", [128, TT, NE])
        oh = [sb(f"oh{k}", [128, TT, NE]) for k in range(2)]
        m2 = sb("m2", [128, 2, TT])
        cnt, pre = sb("cnt", [128, TT, NE]), sb("pre", [128, TT + 1, NE])
        eid, pos, over, t1, t2 = (sb(n, [128, TT]) for n in ("eid", "pos", "over", "rt1", "rt2"))
        most = sb("most", [128, 1])
        shifted, exped, counted, ranked, placed, scat, p_done, p_out, w_in = (
            sem("r2_" + n) for n in "shifted exped counted ranked placed scat p_done p_out w_in".split())
        pg, dl = sb("pg", [128, TT]), sb("dl", [128, TT])
        eg = sb("eg", [128, TT, G])
        g.clear(nc)
        with nc.Block() as block:
            @block.vector
            def _(dve):
                def op(ins):
                    dve.drain()

                def bt(x, n):
                    return x.unsqueeze(2).broadcast_to([128, TT, n])

                def bc(x, n):
                    return x.unsqueeze(1).broadcast_to([128, TT, n])
                g4, e32 = lg[:, :, 0:G], lg[:, :, G:G + NE]
                op(dve.tensor_reduce(mx[:, :], g4, AX.X, ALU.max))
                dve.tensor_tensor(eg[:, :, :], g4, bt(mx[:, :], G), ALU.subtract).then_inc(shifted, 1)
                op(dve.tensor_tensor(v4[:, :, :], g4, bt(mx[:, :], G), ALU.is_equal))
                op(dve.tensor_tensor(v4[:, :, :], v4[:, :, :], bc(w4[:, :], G), ALU.mult))
                op(dve.tensor_reduce(mx[:, :], v4[:, :, :], AX.X, ALU.max))
                op(dve.tensor_tensor(sel[:, :, :], v4[:, :, :], bt(mx[:, :], G), ALU.is_equal))
                op(dve.tensor_scalar(sel[:, :, :], sel[:, :, :], -1.0, 3 * BIG, ALU.add, ALU.mult))
                op(dve.tensor_tensor(le[:, :, :].rearrange("p t (g e) -> p t g e", g=G), e32.rearrange("p t (g e) -> p t g e", g=G),
                                     sel[:, :, :].unsqueeze(3).broadcast_to([128, TT, G, EPG]), ALU.add))
                for k in range(2):
                    op(dve.tensor_reduce(m2[:, k, :], le[:, :, :], AX.X, ALU.max))
                    op(dve.tensor_tensor(v32[:, :, :], le[:, :, :], bt(m2[:, k, :], NE), ALU.is_equal))
                    op(dve.tensor_tensor(v32[:, :, :], v32[:, :, :], bc(w32[:, :], NE), ALU.mult))
                    op(dve.tensor_reduce(mx[:, :], v32[:, :, :], AX.X, ALU.max))
                    op(dve.tensor_tensor(oh[k][:, :, :], v32[:, :, :], bt(mx[:, :], NE), ALU.is_equal))
                    if k == 0:
                        op(dve.tensor_scalar(v32[:, :, :], oh[0][:, :, :], -2 * BIG, None, ALU.mult))
                        op(dve.tensor_tensor(le[:, :, :], le[:, :, :], v32[:, :, :], ALU.add))
                dve.tensor_tensor(dl[:, :], m2[:, 1, :], m2[:, 0, :], ALU.subtract).then_inc(shifted, 1)
                op(dve.tensor_tensor(cnt[:, :, :], oh[0][:, :, :], oh[1][:, :, :], ALU.add))
                op(dve.tensor_tensor(cnt[:, :, :], cnt[:, :, :], bt(valid[:, :], NE), ALU.mult))
                op(dve.memset(pre[:, 0, :], 0.0))
                for t in range(TT):
                    op(dve.tensor_tensor(pre[:, t + 1, :], pre[:, t, :], cnt[:, t, :], ALU.add))
                dve.memset(most[:, :], 0.0).then_inc(counted, 1)
                dve.wait_ge(exped, 1)
                op(dve.tensor_reduce(pg[:, :], eg[:, :, :], AX.X, ALU.add))
                op(dve.reciprocal(pg[:, :], pg[:, :]))
                dve.wait_ge(exped, 2)
                op(dve.tensor_scalar(t1[:, :], dl[:, :], 1.0, None, ALU.add))
                op(dve.reciprocal(t1[:, :], t1[:, :]))
                op(dve.tensor_tensor(t1[:, :], t1[:, :], pg[:, :], ALU.mult))
                op(dve.tensor_tensor(g.gate[:, 0, :], t1[:, :], valid[:, :], ALU.mult))
                op(dve.tensor_tensor(g.gate[:, 1, :], g.gate[:, 0, :], dl[:, :], ALU.mult))
                dve.wait_ge(ranked, 1)
                for k in range(2):
                    op(dve.tensor_tensor(v32[:, :, :], oh[k][:, :, :], bank[0][:, 0:TT * NE].rearrange("p (t e) -> p t e", t=TT), ALU.mult))
                    op(dve.tensor_reduce(pos[:, :], v32[:, :, :], AX.X, ALU.add))
                    op(dve.tensor_tensor(v32[:, :, :], oh[k][:, :, :], bc(i32t[:, :], NE), ALU.mult))
                    op(dve.tensor_reduce(eid[:, :], v32[:, :, :], AX.X, ALU.add))
                    op(dve.tensor_scalar(over[:, :], pos[:, :], float(CAP), None, ALU.is_ge))
                    for m in range(2, PASSES):
                        op(dve.tensor_scalar(t1[:, :], pos[:, :], float(CAP * m), None, ALU.is_ge))
                        op(dve.tensor_tensor(over[:, :], over[:, :], t1[:, :], ALU.add))
                    n = PASSES * NE
                    op(dve.tensor_scalar(t1[:, :], pos[:, :], float(n), None, ALU.mult))
                    op(dve.tensor_tensor(t1[:, :], t1[:, :], eid[:, :], ALU.add))
                    op(dve.tensor_scalar(t2[:, :], over[:, :], float(NE - CAP * n), None, ALU.mult))
                    op(dve.tensor_tensor(t1[:, :], t1[:, :], t2[:, :], ALU.add))
                    op(dve.tensor_tensor(t1[:, :], t1[:, :], valid[:, :], ALU.mult))
                    op(dve.tensor_tensor(t1[:, :], t1[:, :], pad_a[:, k, :], ALU.add))
                    op(dve.tensor_copy(g.slot_a[:, k, :], t1[:, :]))
                    op(dve.tensor_scalar(t1[:, :], over[:, :], -1.0, None, ALU.mult))
                    op(dve.tensor_tensor(t1[:, :], t1[:, :], eid[:, :], ALU.add))
                    op(dve.tensor_scalar(t1[:, :], t1[:, :], float(CAP), None, ALU.mult))
                    op(dve.tensor_tensor(t1[:, :], t1[:, :], pos[:, :], ALU.add))
                    op(dve.tensor_tensor(g.row[:, k, :], t1[:, :], valid[:, :], ALU.mult))
                    dve.tensor_copy(g.turn[:, k, :], over[:, :]).then_inc(placed, 1)
                    dve.drain()
                op(dve.tensor_reduce(most[:, :], bank[1][:, 0:NE], AX.X, ALU.max))
                dve.tensor_copy(g.most[:, :], most[:, :])

            @block.sync
            def _(sp):
                for e, slot in enumerate(g.weights):
                    load_expert(sp, g, slot, e, w_in)
                sp.wait_ge(w_in, 48 * len(g.weights))

            @block.scalar
            def _(act):
                act.wait_ge(shifted, 1)
                act.activation(eg[:, :, :], eg[:, :, :], ACT.Exp).then_inc(exped, 1)
                for t in range(TT):
                    if t == 3:
                        act.wait_ge(shifted, 2)
                        act.activation(dl[:, :], dl[:, :], ACT.Exp).then_inc(exped, 1)
                    r = rows_of(t)
                    act.wait_ge(p_done, t + 1)
                    for i in range(2):
                        last = act.activation(g.ple_p[0:r, t, 512 * i:512 * i + 512], bank[2 + 2 * (t % 3) + i][0:r, :], ACT.Copy)
                    last.then_inc(p_out, 1)

            @block.tensor
            def _(pe):
                for t in range(TT):
                    if t == 3:
                        pe.wait_ge(counted, 1)
                        pe.matmul(bank[0][:, 0:TT * NE], upper[:, :], cnt[:, :, :], start=True, stop=False)
                        pe.matmul(bank[0][:, 0:TT * NE], g.ones[:, :], pre[:, 0:TT, :], start=False, stop=True)
                        pe.matmul(bank[1][:, 0:NE], g.ones[:, :], pre[:, TT, :], start=True, stop=True).then_inc(ranked, 1)
                    r = rows_of(t)
                    if t >= 3:
                        pe.wait_ge(p_out, t - 2)
                    for i in range(2):
                        for k in range(2):
                            mm = pe.matmul(bank[2 + 2 * (t % 3) + i][0:r, :], pT[:, k, 128 * t:128 * t + r], pp[:, k, 512 * i:512 * i + 512], start=(k == 0), stop=(k == 1))
                    mm.then_inc(p_done, 1)

            @block.gpsimd
            def _(pool):
                for k in range(2):
                    pool.wait_ge(placed, k + 1)
                    for t in range(TT):
                        pool.indirect_dma_start(g.table[:, :], bass.IndirectOffsetOnAxis(g.slot_a[:, k, t:t + 1], 0), tok[:, t:t + 1], None).then_inc(scat, 16)
                pool.wait_ge(scat, 16 * 2 * TT)


def expert_weights(sb, i):
    return sb(f"we_g{i}", [128, KD, FF]), sb(f"we_u{i}", [128, KD, FF]), sb(f"we_d{i}", [128, 2, D])


def load_expert(sp, g, slot, e, loaded):
    wg, wu, wd = slot
    sp.dma_start(wg[:, :, :], g.d_weg[e].rearrange("(p k) f -> p k f", p=128)).then_inc(loaded, 16)
    sp.dma_start(wu[:, :, :], g.d_weu[e].rearrange("(p k) f -> p k f", p=128)).then_inc(loaded, 16)
    sp.dma_start(wd[:, :, :], g.d_wed[e].rearrange("(f p) d -> p f d", p=128)).then_inc(loaded, 16)


def experts(nc, g):
    NW, NX = 4, 3
    AHEAD = len(g.weights)
    with ExitStack() as ctx:
        sb = lambda n, s, d=f32: ctx.enter_context(nc.sbuf_tensor(n, s, d))
        sem = g.semaphores(nc, ctx)
        bank = g.bank
        weights = g.weights + [expert_weights(sb, i) for i in range(AHEAD, NW)]
        idx = sb("idx", [128, NE], i32)
        xg = [sb(f"xg{i}", [128, D]) for i in range(NX)]
        xT = [sb(f"xgT{i}", [128, KD, CAP]) for i in range(2)]
        sg_, hT = [sb(f"silu{i}", [128, 2, CAP]) for i in range(2)], [sb(f"hT{i}", [128, 2, CAP]) for i in range(2)]
        yo = sb("yo", [128, 2, D])
        s = {n: sem("e_" + n) for n in ("idx turned xev up silu h down yev stored0 stored1 " + " ".join(f"w{i}" for i in range(NW))
                                        + " " + " ".join(f"x{i}" for i in range(NX))).split()}
        yk = [x[:, :] for x in xg] + [yo[:, 0, :]]
        now, here = sb("now", [128, 1]), sb("here", [128, 2, TT])
        weight, local, row = sb("weight", [128, 2, TT]), sb("local", [128, 2, TT]), sb("row_i", [128, 2, TT], i32)
        junk = yo[:, 1, :]
        s |= {n: sem("e_" + n) for n in "rows combined y0 y1 y2 y3".split()}
        g.clear(nc)
        with nc.Block() as block:
            @block.vector
            def _(dve):
                dve.memset(now[:, :], 0.0)
        most = nc.values_load(g.most[0:1, 0:1], min_val=0, max_val=T)

        def one_pass(p, ahead):
            loads = lambda e: 48 * len(range(e % NW + (NW if e % NW < ahead else 0), e + 1, NW))
            with nc.Block() as block:
                @block.gpsimd
                def _(pool):
                    for n, semaphore in s.items():
                        if n[0] not in "xy" or n in ("xev", "yev"):
                            pool.sem_clear(semaphore)
            with nc.Block() as block:
                @block.sync
                def _(sp):
                    sp.dma_start(idx[:, :], g.table[0:SLOTS, :].rearrange("(p n) o -> p (n o)", p=128)[:, bass.ds(p * NE, NE)]).then_inc(s["idx"], 16)
                    for e in range(ahead, NE):
                        if e >= NW:
                            sp.wait_ge(s["down"], e - NW + 1)
                        load_expert(sp, g, weights[e % NW], e, s[f"w{e % NW}"])

                @block.gpsimd
                def _(pool):
                    pool.wait_ge(s["idx"], 16)
                    for e in range(NE):
                        if e >= NX:
                            pool.wait_ge(s["turned"], e - NX + 1)
                        pool.indirect_dma_start(xg[e % NX][:, :], None, g.xn[:, :], bass.IndirectOffsetOnAxis(idx[:, e:e + 1], 0)).then_inc(s[f"x{e % NX}"], 16)

                @block.tensor
                def _(pe):
                    def turn(e):
                        pe.wait_ge(s[f"x{e % NX}"], p * (16 * len(range(e % NX, NE, NX))) + 16 * (e // NX + 1))
                        if e >= 1:
                            pe.wait_ge(s["xev"], e)
                        v = xg[e % NX][:, :].rearrange("p (q k) -> p k q", k=KD)
                        for k in range(KD):
                            mm = pe.transpose(bank[k // 4][:, 128 * (k % 4):128 * (k % 4) + 128], v[:, k, :], g.ident[:, :])
                        mm.then_inc(s["turned"], 1)

                    def up(e):
                        i = e % NW
                        pe.wait_ge(s["xev"], e + 1)
                        if loads(e):
                            pe.wait_ge(s[f"w{i}"], loads(e))
                        wg, wu, _ = weights[i]
                        if e >= 2:
                            pe.wait_ge(s["h"], e - 1)
                        for a, w in enumerate((wg, wu)):
                            for f in range(2):
                                for k in range(KD):
                                    mm = pe.matmul(bank[2 + e % 2][:, 128 * (2 * a + f):128 * (2 * a + f) + CAP], w[:, k, 128 * f:128 * f + 128],
                                                   xT[e % 2][:, k, :], start=(k == 0), stop=(k == KD - 1))
                        mm.then_inc(s["up"], 1)

                    def down(e):
                        pe.wait_ge(s["h"], e + 1)
                        if e >= 2:
                            pe.wait_ge(s["yev"], e - 1)
                        for c in range(2):
                            for f in range(2):
                                mm = pe.matmul(bank[4 + 2 * (e % 2) + c][:, :], hT[e % 2][:, f, :], weights[e % NW][2][:, f, 512 * c:512 * c + 512],
                                               start=(f == 0), stop=(f == 1))
                        mm.then_inc(s["down"], 1)

                    turn(0)
                    for e in range(NE):
                        up(e)
                        if e + 1 < NE:
                            turn(e + 1)
                        if e >= 1:
                            down(e - 1)
                    down(NE - 1)

                def result(act, e):
                    act.wait_ge(s["down"], e + 1)
                    if e >= 2:
                        act.wait_ge(s[f"stored{e % 2}"], 16 * (e // 2))
                    for c in range(2):
                        last = act.activation(yo[:, e % 2, 512 * c:512 * c + 512], bank[4 + 2 * (e % 2) + c][:, :], ACT.Copy)
                    last.then_inc(s["yev"], 1)
                    act.wait_ge(s["yev"], e + 1)
                    act.dma_start(g.yb[e * CAP:(e + 1) * CAP, :], yo[:, e % 2, :]).then_inc(s[f"stored{e % 2}"], 16)
                    if e == NE - 1:
                        act.wait_ge(s["stored0"], 8 * NE)
                        act.wait_ge(s["stored1"], 8 * NE)

                @block.scalar
                def _(act):
                    for e in range(NE):
                        act.wait_ge(s["up"], e + 1)
                        if e >= 2:
                            act.wait_ge(s["h"], e - 1)
                        act.activation(sg_[e % 2][:, :, :].rearrange("p f q -> p (f q)"), bank[2 + e % 2][:, 0:256], ACT.Silu).then_inc(s["silu"], 1)
                        if e >= 1:
                            result(act, e - 1)
                    result(act, NE - 1)

                @block.vector
                def _(dve):
                    def evac(e):
                        dve.wait_ge(s["turned"], e + 1)
                        if e >= 2:
                            dve.wait_ge(s["up"], e - 1)
                        for c in range(2):
                            last = dve.tensor_copy(xT[e % 2][:, 4 * c:4 * c + 4, :].rearrange("p k q -> p (k q)"), bank[c][:, :])
                        last.then_inc(s["xev"], 1)
                    evac(0)
                    for e in range(NE):
                        if e + 1 < NE:
                            evac(e + 1)
                        dve.wait_ge(s["silu"], e + 1)
                        if e >= 2:
                            dve.wait_ge(s["down"], e - 1)
                        dve.tensor_tensor(hT[e % 2][:, :, :].rearrange("p f q -> p (f q)"), sg_[e % 2][:, :, :].rearrange("p f q -> p (f q)"),
                                          bank[2 + e % 2][:, 256:512], ALU.mult).then_inc(s["h"], 1)

            with nc.Block() as block:
                @block.vector
                def _(dve):
                    dve.tensor_scalar(here[:, :, :], g.turn[:, :, :], now[:, 0:1], None, ALU.is_equal)
                    dve.drain()
                    dve.tensor_tensor(weight[:, :, :], here[:, :, :], g.gate[:, :, :], ALU.mult)
                    dve.tensor_tensor(local[:, :, :], here[:, :, :], g.row[:, :, :], ALU.mult)
                    dve.drain()
                    dve.tensor_copy(row[:, :, :], local[:, :, :]).then_inc(s["rows"], 1)
                    dve.tensor_scalar(now[:, :], now[:, :], 1.0, None, ALU.add)
                    for n in range(2 * TT):
                        t, k = n // 2, n % 2
                        dve.wait_ge(s[f"y{n % 4}"], p * (16 * len(range(n % 4, 2 * TT, 4))) + 16 * (n // 4 + 1))
                        dve.scalar_tensor_tensor(out=g.h[:, t, :], in0=yk[n % 4], scalar=weight[:, k, t:t + 1], in1=g.h[:, t, :],
                                                 op0=ALU.mult, op1=ALU.add).then_inc(s["combined"], 1)
                        dve.drain()

                @block.scalar
                def _(act):
                    for t in range(TT):
                        act.wait_ge(s["combined"], 2 * t + 2)
                        act.activation(junk, g.h[:, t, :], ACT.Square, accum_out=g.ss[:, t:t + 1])
                        act.drain()

                @block.gpsimd
                def _(pool):
                    pool.wait_ge(s["rows"], 1)
                    for n in range(2 * TT):
                        t, k = n // 2, n % 2
                        if n >= 4:
                            pool.wait_ge(s["combined"], n - 3)
                        pool.indirect_dma_start(yk[n % 4], None, g.yb[:, :], bass.IndirectOffsetOnAxis(row[:, k, t:t + 1], 0)).then_inc(s[f"y{n % 4}"], 16)

        one_pass(0, AHEAD)
        with nc.If(most > CAP):
            with nc.Fori(1, PASSES) as p:
                one_pass(p, 0)


def finish(nc, g):
    with ExitStack() as ctx:
        sb = lambda n, s: ctx.enter_context(nc.sbuf_tensor(n, s, f32))
        sem = g.semaphores(nc, ctx)
        bank = g.bank
        wp = sb("wp", [128, KD, D])
        fgain, junk = sb("fgain", [128, D]), sb("fjunk", [128, D])
        rstd, ss, rout = (sb(n, [128, TT]) for n in ("frstd", "fss", "frout"))
        un, uT, sig = sb("un", [128, 2, D]), sb("unT", [128, 2, KD, 128]), sb("sig", [128, 2, D])
        w_in = [sem(f"f_w{k}") for k in range(KD)]
        names = "gain_in meaned rooted normed turned evac gates sigd updated squared y_meaned y_rooted y_ready outs"
        gain_in, meaned, rooted, normed, turned, evac, gates, sigd, updated, squared, y_meaned, y_rooted, y_ready, outs = (
            sem("f_" + n) for n in names.split())
        c = PC["norm_ple"]
        g.clear(nc)
        with nc.Block() as block:
            @block.sync
            def _(sp):
                for k in range(KD):
                    sp.dma_start(wp[:, k, :], g.d_pgate[128 * k:128 * k + 128, :]).then_inc(w_in[k], 16)
                sp.dma_start(fgain[:, :], g.d_final_gain).then_inc(gain_in, 16)
                for t in range(TT):
                    r = rows_of(t)
                    sp.wait_ge(y_ready, t + 1)
                    sp.dma_start(g.o_y[128 * t:128 * t + r, :], g.h[0:r, t, :]).then_inc(outs, 16)
                sp.wait_ge(outs, 16 * TT)

            @block.vector
            def _(dve):
                def normalise(t):
                    if t >= 2:
                        dve.wait_ge(turned, t - 1)
                    dve.tensor_scalar(un[:, t % 2, :], g.h[:, t, :], rstd[:, t:t + 1], None, ALU.mult).then_inc(normed, 1)
                    dve.wait_ge(turned, t + 1)
                    if t >= 2:
                        dve.wait_ge(gates, t - 1)
                    for i in range(2):
                        last = dve.tensor_tensor(uT[:, t % 2, 4 * i:4 * i + 4, :], bank[2 * (t % 2) + i][:, :].rearrange("p (k q) -> p k q", k=4),
                                                 g.prm[:, c + 4 * i:c + 4 * i + 4].unsqueeze(2).broadcast_to([128, 4, 128]), ALU.mult)
                    last.then_inc(evac, 1)

                dve.tensor_scalar(rstd[:, :], g.ss[:, :], 1.0 / D, RMS_EPS, ALU.mult, ALU.add).then_inc(meaned, 1)
                dve.wait_ge(rooted, 1)
                dve.reciprocal(rstd[:, :], rstd[:, :])
                dve.drain()
                normalise(0)
                normalise(1)
                dve.wait_ge(gain_in, 16)
                for t in range(TT):
                    r = rows_of(t)
                    if t + 2 < TT:
                        normalise(t + 2)
                    dve.wait_ge(sigd, t + 1)
                    dve.tensor_tensor(sig[0:r, t % 2, :], sig[0:r, t % 2, :], g.ple_p[0:r, t, :], ALU.mult)
                    dve.drain()
                    dve.tensor_tensor(g.h[0:r, t, :], g.h[0:r, t, :], sig[0:r, t % 2, :], ALU.add).then_inc(updated, 1)
                    dve.wait_ge(squared, t + 1)
                    dve.tensor_scalar(rout[0:r, t:t + 1], ss[0:r, t:t + 1], 1.0 / D, RMS_EPS, ALU.mult, ALU.add).then_inc(y_meaned, 1)
                    dve.wait_ge(y_rooted, t + 1)
                    dve.reciprocal(rout[0:r, t:t + 1], rout[0:r, t:t + 1])
                    dve.drain()
                    dve.scalar_tensor_tensor(out=g.h[0:r, t, :], in0=g.h[0:r, t, :], scalar=rout[0:r, t:t + 1], in1=fgain[0:r, :],
                                             op0=ALU.mult, op1=ALU.mult).then_inc(y_ready, 1)

            @block.tensor
            def _(pe):
                def turn(t):
                    pe.wait_ge(normed, t + 1)
                    if t >= 2:
                        pe.wait_ge(evac, t - 1)
                    for k in range(KD):
                        mm = pe.transpose(bank[2 * (t % 2) + k // 4][:, 128 * (k % 4):128 * (k % 4) + 128],
                                          un[:, t % 2, 128 * k:128 * k + 128], g.ident[:, :])
                    mm.then_inc(turned, 1)

                turn(0)
                turn(1)
                for t in range(TT):
                    r = rows_of(t)
                    pe.wait_ge(evac, t + 1)
                    if t >= 2:
                        pe.wait_ge(sigd, t - 1)
                    for i in range(2):
                        for k in range(KD):
                            if t == 0 and i == 0:
                                pe.wait_ge(w_in[k], 16)
                            mm = pe.matmul(bank[4 + 2 * (t % 2) + i][0:r, :], uT[:, t % 2, k, 0:r], wp[:, k, 512 * i:512 * i + 512], start=(k == 0), stop=(k == KD - 1))
                    mm.then_inc(gates, 1)
                    if t + 2 < TT:
                        turn(t + 2)

            @block.scalar
            def _(act):
                act.wait_ge(meaned, 1)
                act.activation(rstd[:, :], rstd[:, :], ACT.Sqrt).then_inc(rooted, 1)
                for t in range(TT):
                    r = rows_of(t)
                    act.wait_ge(gates, t + 1)
                    if t >= 2:
                        act.wait_ge(updated, t - 1)
                    for i in range(2):
                        last = act.activation(sig[0:r, t % 2, 512 * i:512 * i + 512], bank[4 + 2 * (t % 2) + i][0:r, :], ACT.Sigmoid)
                    last.then_inc(sigd, 1)
                    act.wait_ge(updated, t + 1)
                    act.activation(junk[0:r, :], g.h[0:r, t, :], ACT.Square, accum_out=ss[0:r, t:t + 1]).then_inc(squared, 1)
                    act.wait_ge(y_meaned, t + 1)
                    act.activation(rout[0:r, t:t + 1], rout[0:r, t:t + 1], ACT.Sqrt).then_inc(y_rooted, 1)

CACHE_POSITIONS = [x for x in range(1536) if x % 16 < 8] + list(range(1536, 2048))


def masks():
    s, t = np.arange(CW)[:, None], np.arange(CW)[None, :]
    seq = (s // NT == t // NT)
    two = lambda m: np.concatenate([m, m], 0)
    low = np.stack([two(t < s), two((t < s) & seq)], 1)
    lev = lambda m: (s // (2 * m) == t // (2 * m)) & (s // m < t // m)
    level = np.stack([two(x) for x in (lev(1), lev(2), lev(4), lev(8), lev(16), lev(1).T, lev(32))], 1)
    pair = np.stack([two(np.concatenate([(s < t) & z, (s <= t) & z], 1)) for z in (np.ones_like(seq), seq)], 1)
    mseq = (np.arange(128)[:, None] % CW) // NT == np.arange(NB)[None, :]
    keep = np.ones(T)
    keep[np.arange(0, S, CW)] = 0
    keep[np.arange(S, T, NT)] = 0
    p, q = np.arange(128)[:, None], np.arange(128)[None, :]
    f = lambda m: np.ascontiguousarray(m.astype(np.float32))
    inv = np.power(np.float32(10000.0), -np.arange(32, dtype=np.float32) * np.float32(2.0) / np.float32(E)).astype(np.float32)
    pos = np.concatenate([np.arange(S), np.tile(4096 + np.arange(NT), NB)]).astype(np.float32)
    ang = (pos[None, :] * np.tile(inv, 4)[:, None]).astype(np.float32)
    rot = np.zeros((128, 128))
    for m in range(128):
        rot[m + 32 if m % E < 32 else m - 32, m] = -1 if m % E < 32 else 1

    def log_count(dist):
        n = sum(((dist >= 0) & (dist % dil == 0) & (dist <= win)).astype(int) for win, dil in ((128, 1), (512, 4), (2048, 16)))
        return np.where(n > 0, 8 * np.log(np.maximum(n, 1)), -8e30)
    count = log_count(np.arange(128)[:, None] + (S - 128) - np.arange(S)[None, :])
    r = np.arange(128)
    mcache = log_count(2048 + (r % NT)[:, None] - np.array(CACHE_POSITIONS)[None, :])
    token = NT * (2 * np.arange(NB // 2)[None, :] + r[:, None] // (H * NT)) + r[:, None] % NT
    own = np.arange(TS)[None, None, :]
    mnew = np.where(token[:, :, None] // NT == own // NT, log_count(token[:, :, None] % NT - own % NT), -8e30)
    p, q = np.arange(128)[:, None], np.arange(128)[None, :]
    tokens = np.arange(TT)[None, :] * 128 + np.arange(128)[:, None]
    valid = tokens < T
    row = lambda v: np.broadcast_to(np.asarray(v, np.float32), (128, len(v)))
    routing = dict(upper=f(p < q), valid=f(valid), pad_a=f(np.stack([np.where(valid, 0, SLOTS + 128 * k + np.arange(128)[:, None]) for k in range(2)], 1)), w4=f(row(np.arange(G, 0, -1))),
                   w32=f(row(np.arange(NE, 0, -1))), i32t=f(row(np.arange(NE))), tok=np.ascontiguousarray(tokens.astype(np.int32)))
    return dict(routing, mcache=f(mcache), mnew=f(mnew), own_row=f(token[:, :, None] == own),
                own_head=f((r // NT % H)[:, None] == np.arange(RW)[None, :] // E), cos=f(np.cos(ang)), sin=f(np.sin(ang)), rot=f(rot), count=f(count), m_low=f(low), m_level=f(level), m_pair=f(pair), m_seq=f(mseq), m_eye=f(two(s == t)),
                keep=f(np.broadcast_to(keep, (128, T))), ones=f(np.ones((128, 128))), headones=f(p // E == q // E), ident=f(p == q))


def lay_out(i):
    a = {k: np.asarray(v) for k, v in i.items()}
    x = np.concatenate([a["x_prompt"].reshape(S, D), a["x_sample"].reshape(TS, D)], 0)
    cols = np.zeros((128, PCN), np.float32)

    def put(name, v):
        k = -(-v.size // 128)
        for n in range(k):
            part = v[128 * n:128 * n + 128]
            cols[:part.size, PC[name] + n] = part
    mu = a["mu_shift"][0]
    for n, v in (("norm_mix", a["norm_mix"][0]), ("mu_r", mu[0:RW]), ("mu_k", mu[RW:2 * RW]), ("mu_v", mu[2 * RW:3 * RW]),
                 ("mu_wa", mu[3 * RW:3 * RW + 64]), ("mu_g", mu[3 * RW + 64:]), ("w0", a["decay_w0"][0]), ("a0", a["iclr_a0"][0]),
                 ("k_k", a["k_k"][0]), ("k_a", a["k_a"][0]), ("r_k", a["r_k"][0].reshape(-1)), ("lnx_w", a["lnx_w"][0]),
                 ("lnx_b", a["lnx_b"][0]), ("attn_norm", a["attn_out_norm"][0]), ("norm_ffn", a["norm_ffn"][0]), ("norm_ple", a["norm_ple"][0])):
        put(n, v)
    c = np.ascontiguousarray
    kcT = c(a["cache_k_win"][0].reshape(NB, 2048, RW)[:, CACHE_POSITIONS].transpose(0, 2, 1))
    vc = c(a["cache_v_win"][0].reshape(NB, 2048, RW)[:, CACHE_POSITIONS])
    over = lambda v: c(np.broadcast_to(v, (128, v.size)))
    p = np.concatenate([a["p_prompt"][0].reshape(S, -1), a["p_sample"][0].reshape(TS, -1)], 0)
    wr = np.pad(np.concatenate([a["router_group_w"][0], a["router_expert_w"][0]], 1), ((0, 0), (0, WR - G - NE)))
    return dict(masks(), kcT=kcT, x=x, wout=c(a["w_out"][0]), ffn_gain=over(a["norm_ffn"][0]), final_gain=over(a["norm_final"]),
                wr=c(wr.reshape(KD, 128, WR).transpose(1, 0, 2)), br=over(np.concatenate([a["router_group_b"][0], a["router_expert_b"][0]])),
                weg=c(a["expert_w_gate"][0]), weu=c(a["expert_w_up"][0]), wed=c(a["expert_w_down"][0]), pgate=c(a["ple_gate_w"][0]),
                pproj=c(a["ple_proj"][0]), pT=c(p.T), vc=vc, xT=c(x.T), prm=cols, win=c(np.pad(a["w_in"][0], ((0, 0), (0, 128)))),
                w2a2=c(np.concatenate([a["decay_w2"][0], a["iclr_a2"][0]], 0)), g2=c(a["gate_g2"][0]),
                shT=c(a["state_shift"][0].T), stT=c(a["state_wkv"][0].transpose(1, 3, 0, 2).reshape(RW, NB * E)))


OUTS = dict(pshift=(RP, 1), sshift=(RP, NB), pwkv=(RW, E), swkv=(RW, NB * E), kT=(RW, T), v=(T, RW), y=(T, D))


class Parts:

    def __init__(self):
        self.new = []

    def semaphores(self, nc, ctx):
        def take(name):
            self.new.append(ctx.enter_context(nc.semaphore(name)))
            return self.new[-1]
        return take

    def clear(self, nc):
        new, self.new = self.new, []
        with nc.Block() as block:
            @block.gpsimd
            def _(pool):
                for semaphore in new:
                    pool.sem_clear(semaphore)


def build(nc, g):
    with ExitStack() as ctx:
        sb = lambda n, s, d=f32: ctx.enter_context(nc.sbuf_tensor(n, s, d))
        g.bank = [ctx.enter_context(nc.psum_tensor(f"bank{i}", [128, 512], f32)) for i in range(8)]
        g.s_const = ctx.enter_context(nc.semaphore("s_const"))
        g.prm = sb("prm", [128, PCN])
        g.ones, g.ident = sb("ones", [128, 128]), sb("ident", [128, 128])
        g.table = nc.dram_tensor("table", (SLOTS + 256, 1), i32, kind="Internal").ap()
        g.xn = nc.dram_tensor("xn_rows", (TT * 128, D), f32, kind="Internal").ap()
        g.yb = nc.dram_tensor("y_rows", (NE * CAP, D), f32, kind="Internal").ap()
        g.h = sb("h", [128, TT, D])
        g.ss = sb("ss", [128, TT])
        with ExitStack() as mix:
            sm = lambda n, s, d=f32: mix.enter_context(nc.sbuf_tensor(n, s, d))
            g.att = sm("att", [128, TT, RW])
            g.rwT = sm("rwT", [128, J, T])
            g.qs, g.ks, g.vs = sm("qs", [128, J, TS]), sm("ks", [128, J, TS]), sm("vs", [128, J, 128])
            with ExitStack() as early:
                se = lambda n, s, d=f32: early.enter_context(nc.sbuf_tensor(n, s, d))
                g.uT = g.h[:, :, :].rearrange("p t d -> p (t d)")[:, 0:KD * T].rearrange("p (k t) -> p k t", k=KD)
                g.constants = [(g.ident[:, :], g.d_ident)]
                g.headones = se("headones", [128, 128])
                g.m_low, g.m_level, g.m_pair = se("m_low", [128, 2, CW]), se("m_level", [128, 7, CW]), se("m_pair", [128, 2, 128])
                g.m_seq, g.m_eye, g.keep = se("m_seq", [128, NB]), se("m_eye", [128, CW]), se("keep", [128, T])
                g.constants += [(g.headones[:, :], g.d_headones), (g.m_low[:, :, :], g.d_m_low), (g.m_level[:, :, :], g.d_m_level),
                                (g.m_pair[:, :, :], g.d_m_pair), (g.m_seq[:, :], g.d_m_seq), (g.m_eye[:, :], g.d_m_eye), (g.keep[:, :], g.d_keep)]
                project_tokens(nc, g)
                with nc.sbuf_tensor("tw", [64, T], f32) as g.tw, nc.sbuf_tensor("sg", [96, T], f32) as g.sg:
                    lora_inputs(nc, g)
                    rwkv(nc, g)
            g.kc = [sm(f"kc{i}", [128, J, NSEL]) for i in range(2)]
            g.k_in = [mix.enter_context(nc.semaphore(f"k_in{i}")) for i in range(2)]
            attention(nc, g)
            decode_attention(nc, g)
            out_projection(nc, g)
        g.gate = sb("gate_w", [128, 2, TT])
        g.slot_a, g.most = sb("slot_a", [128, 2, TT], i32), sb("most_i", [128, 1], i32)
        g.row, g.turn = sb("row", [128, 2, TT]), sb("turn", [128, 2, TT])
        g.ple_p = sb("ple_p", [128, TT, D])
        with ExitStack() as moe:
            g.weights = [expert_weights(lambda n, shape: moe.enter_context(nc.sbuf_tensor(n, shape, f32)), i) for i in range(3)]
            route(nc, g)
            experts(nc, g)
        finish(nc, g)


def kernel(**inputs):
    import concourse.bacc as bacc
    from concourse.bass_utils import run_bass_kernel_spmd as run
    nc = bacc.Bacc("TRN2", target_bir_lowering=False, num_devices=1)
    arrays = lay_out(inputs)
    g = Parts()
    for n, a in arrays.items():
        g.__dict__["d_" + n] = nc.dram_tensor("in_" + n, a.shape, mybir.dt.from_np(a.dtype), kind="ExternalInput").ap()
    for n, shape in OUTS.items():
        g.__dict__["o_" + n] = nc.dram_tensor("out_" + n, shape, f32, kind="ExternalOutput").ap()
    build(nc, g)
    r = run(nc, [{"in_" + n: a for n, a in arrays.items()}], core_ids=[0]).results[0]
    y, kT, v = np.asarray(r["out_y"]), np.asarray(r["out_kT"]).T, np.asarray(r["out_v"])
    c = np.ascontiguousarray
    heads = lambda z, *lead: c(z).reshape(1, *lead, H, E)
    pwkv = np.asarray(r["out_pwkv"]).reshape(1, 1, H, E, E).transpose(0, 1, 2, 4, 3)
    swkv = np.asarray(r["out_swkv"]).reshape(H, E, NB, E).transpose(2, 0, 3, 1)[None]
    return (c(y[:S]).reshape(1, S, D), c(y[S:]).reshape(NB, NT, D), heads(kT[:S], 1, S), heads(v[:S], 1, S), c(pwkv),
            c(np.asarray(r["out_pshift"]).reshape(1, 1, RP)), heads(kT[S:], NB, NT), heads(v[S:], NB, NT), c(swkv),
            c(np.asarray(r["out_sshift"]).T)[None])
```
